# Optimizing a Trainium2 kernel written in Bass

```python
import math
import jax, jax.numpy as jnp
from jax import lax
import numpy as np

D_MODEL = 1024
BATCH = 1
SEQ = 128
DEPTH = 2
DEC_BATCH = 1
DEC_SEQ = 512
PAST_LEN = 128

GRID_W = 64
N_ATT_LAYERS = (DEPTH + 1) // 2
N_SSD_LAYERS = DEPTH // 2
EPS = 1e-6
MIX_W = D_MODEL
DA_HEADS = 4
DA_HD = 64
DA_QK_W = DA_HEADS * 2 * DA_HD
DA_V_W = DA_HEADS * 2 * DA_HD
POOL_W = MIX_W - DA_V_W
POOL_WINDOWS = (2, 4, 8, 16)
POOL_GROUPS = 4
POOL_GC = POOL_W // POOL_GROUPS
ATT_IN_W = 2 * DA_QK_W + DA_V_W + POOL_W
Q_BLOCK = 128
ROPE_THETA = 10000.0
ROPE_NF = DA_HD // 4
SSD_DI = 2 * D_MODEL
SSD_HEADDIM = 64
SSD_HEADS = SSD_DI // SSD_HEADDIM
SSD_GROUPS = 4
SSD_STATE = 128
SSD_CONV = 3
SSD_CHUNK = 128
SSD_XBC_W = SSD_DI + 2 * SSD_GROUPS * SSD_STATE
SSD_IN_W = SSD_DI + SSD_XBC_W + 2 * SSD_HEADS
D_FF = 2816
FFN_CONV = 3

kernel_name = "hybrid_diffusion_diffattn_pool_ssd_step"

def rmsnorm(x, g):
    xf = x.astype(jnp.float32)
    y = xf * lax.rsqrt(jnp.mean(xf * xf, axis=-1, keepdims=True) + EPS)
    return (y * g.astype(jnp.float32)).astype(x.dtype)

def adaln(cvec, w, b):
    m = jax.nn.silu(cvec) @ w + b
    return jnp.split(m, 6, axis=-1)

def modulate(x, g, shift, scale):
    return rmsnorm(x, g) * (1 + scale[..., None, :]) + shift[..., None, :]

def dwconv_centered(x, w, b):
    k = w.shape[0]
    y = lax.conv_general_dilated(x, w[:, None, :].astype(x.dtype), window_strides=(1,),
                                 padding=[(k // 2, k - 1 - k // 2)],
                                 dimension_numbers=('NWC', 'WIO', 'NWC'),
                                 feature_group_count=x.shape[-1])
    return y + b

def axial_rope_tables(n_lat):
    rows = n_lat // GRID_W
    r, col = jnp.meshgrid(jnp.arange(rows, dtype=jnp.float32), jnp.arange(GRID_W, dtype=jnp.float32), indexing='ij')
    inv = ROPE_THETA ** (-jnp.arange(ROPE_NF, dtype=jnp.float32) / ROPE_NF)
    ang = jnp.stack([r.reshape(-1)[:, None] * inv, col.reshape(-1)[:, None] * inv], axis=1)
    return jnp.cos(ang), jnp.sin(ang)

def apply_axial_rope(x, cos, sin):
    shp = x.shape
    xr = x.astype(jnp.float32).reshape(shp[:-1] + (2, 2, ROPE_NF))
    x1, x2 = xr[..., 0, :], xr[..., 1, :]
    c = cos[None, :, None, None]
    s = sin[None, :, None, None]
    out = jnp.stack([x1 * c - x2 * s, x1 * s + x2 * c], axis=-2)
    return out.reshape(shp).astype(x.dtype)

def diff_attention(q, k, v, lam):
    b, lq = q.shape[:2]
    nb = lq // Q_BLOCK
    qb = jnp.moveaxis(q.reshape(b, nb, Q_BLOCK, DA_HEADS, 2, DA_HD), 1, 0)
    scale = DA_HD ** -0.5

    def block(qi):
        s = jnp.einsum('bqhcd,bkhcd->bhcqk', qi, k).astype(jnp.float32) * scale
        p = jax.nn.softmax(s, axis=-1)
        a = p[:, :, 0] - lam * p[:, :, 1]
        return jnp.einsum('bhqk,bkhe->bqhe', a.astype(v.dtype), v)

    o = lax.map(block, qb)
    return jnp.moveaxis(o, 0, 1).reshape(b, lq, DA_HEADS, 2 * DA_HD)

def multiscale_pool(x, w, scale):
    b, n, _ = x.shape
    xg = x.reshape(b, n, POOL_GROUPS, POOL_GC)
    cs = jnp.pad(jnp.cumsum(xg.astype(jnp.float32), axis=1), ((0, 0), (1, 0), (0, 0), (0, 0)))
    t = jnp.arange(n)
    pooled = []
    for gi, win in enumerate(POOL_WINDOWS):
        lo = jnp.clip(t - win // 2, 0, n)
        hi = jnp.clip(t + win // 2, 0, n)
        cg = cs[:, :, gi]
        mean = (cg[:, hi] - cg[:, lo]) / (hi - lo).astype(jnp.float32)[:, None]
        pooled.append(mean - xg[:, :, gi].astype(jnp.float32))
    pg = jnp.stack(pooled, axis=2).astype(x.dtype)
    y = jnp.einsum('bngc,gcd->bngd', pg, w)
    return y.reshape(b, n, POOL_W) * scale

def even_mixer(h, w_in, lam_vecs, subln_g, pool_w, pool_scale, w_out, lam_init, rope=None, ctx_k=None, ctx_v=None):
    b, n = h.shape[:2]
    proj = h @ w_in
    q, k, v, xpool = jnp.split(proj, [DA_QK_W, 2 * DA_QK_W, 2 * DA_QK_W + DA_V_W], axis=-1)
    q = q.reshape(b, n, DA_HEADS, 2, DA_HD)
    k = k.reshape(b, n, DA_HEADS, 2, DA_HD)
    v = v.reshape(b, n, DA_HEADS, 2 * DA_HD)
    if rope is None:
        q_att, k_all, v_all = q, k, v
    else:
        q_att = apply_axial_rope(q, *rope)
        k_all = jnp.concatenate([apply_axial_rope(k, *rope), ctx_k.astype(k.dtype)], axis=1)
        v_all = jnp.concatenate([v, ctx_v.astype(v.dtype)], axis=1)
    lv = lam_vecs.astype(jnp.float32)
    lam = jnp.exp(jnp.sum(lv[0] * lv[1])) - jnp.exp(jnp.sum(lv[2] * lv[3])) + lam_init
    o = diff_attention(q_att, k_all, v_all, lam)
    o = rmsnorm(o, subln_g) * (1 - lam_init)
    pool_out = multiscale_pool(xpool, pool_w, pool_scale)
    out = jnp.concatenate([o.reshape(b, n, DA_V_W), pool_out], axis=-1) @ w_out
    return out, k, v

def ssd_chunked(x, dt, a, bm, cm, init_state):
    b, n = x.shape[:2]
    nc = n // SSD_CHUNK
    r = SSD_HEADS // SSD_GROUPS
    xc = x.astype(jnp.float32).reshape(b, nc, SSD_CHUNK, SSD_GROUPS, r, SSD_HEADDIM)
    dtc = dt.reshape(b, nc, SSD_CHUNK, SSD_GROUPS, r)
    bc = bm.astype(jnp.float32).reshape(b, nc, SSD_CHUNK, SSD_GROUPS, SSD_STATE)
    cc = cm.astype(jnp.float32).reshape(b, nc, SSD_CHUNK, SSD_GROUPS, SSD_STATE)
    acs = jnp.cumsum(dtc * a.reshape(SSD_GROUPS, r), axis=2)
    seg = acs[:, :, :, None] - acs[:, :, None, :]
    lower = jnp.tril(jnp.ones((SSD_CHUNK, SSD_CHUNK), dtype=bool))[:, :, None, None]
    lmat = jnp.exp(jnp.where(lower, seg, -jnp.inf))
    cb = jnp.einsum('bcign,bcjgn->bcijg', cc, bc)
    wmat = cb[..., None] * lmat * dtc[:, :, None]
    y_diag = jnp.einsum('bcijgr,bcjgrp->bcigrp', wmat, xc)
    xw = (jnp.exp(acs[:, :, -1:] - acs) * dtc)[..., None] * xc
    chunk_states = jnp.einsum('bcjgn,bcjgrp->bcgrpn', bc, xw)
    chunk_decay = jnp.exp(acs[:, :, -1])

    def step(state, inp):
        cs_, dec = inp
        return state * dec[..., None, None] + cs_, state

    s0 = init_state.astype(jnp.float32).reshape(b, SSD_GROUPS, r, SSD_HEADDIM, SSD_STATE)
    final, starts = lax.scan(step, s0, (jnp.moveaxis(chunk_states, 1, 0), jnp.moveaxis(chunk_decay, 1, 0)))
    starts = jnp.moveaxis(starts, 0, 1)
    y_off = jnp.einsum('bcign,bcgrpn->bcigrp', cc, starts) * jnp.exp(acs)[..., None]
    y = (y_diag + y_off).reshape(b, n, SSD_HEADS, SSD_HEADDIM)
    return y, final.reshape(b, SSD_HEADS, SSD_HEADDIM, SSD_STATE)

def ssd_mixer(h, w_in, conv_w, conv_b, dt_bias, a_log, d_skip, norm_g, w_out, init_f=None, init_b=None):
    b, n = h.shape[:2]
    proj = h @ w_in
    z, xbc, dt = jnp.split(proj, [SSD_DI, SSD_DI + SSD_XBC_W], axis=-1)
    xbc = jax.nn.silu(dwconv_centered(xbc, conv_w, conv_b))
    xs, bm, cm = jnp.split(xbc, [SSD_DI, SSD_DI + SSD_GROUPS * SSD_STATE], axis=-1)
    xs = xs.reshape(b, n, SSD_HEADS, SSD_HEADDIM)
    bm = bm.reshape(b, n, SSD_GROUPS, SSD_STATE)
    cm = cm.reshape(b, n, SSD_GROUPS, SSD_STATE)
    dt = jax.nn.softplus(dt.astype(jnp.float32).reshape(b, n, 2, SSD_HEADS) + dt_bias.astype(jnp.float32))
    a = -jnp.exp(a_log.astype(jnp.float32))
    if init_f is None:
        init_f = jnp.zeros((b, SSD_HEADS, SSD_HEADDIM, SSD_STATE), jnp.float32)
        init_b = jnp.zeros((b, SSD_HEADS, SSD_HEADDIM, SSD_STATE), jnp.float32)
    y_f, s_f = ssd_chunked(xs, dt[:, :, 0], a[0], bm, cm, init_f)
    y_b, s_b = ssd_chunked(jnp.flip(xs, 1), jnp.flip(dt[:, :, 1], 1), a[1], jnp.flip(bm, 1), jnp.flip(cm, 1), init_b)
    y = y_f + jnp.flip(y_b, 1) + xs.astype(jnp.float32) * d_skip.astype(jnp.float32)[:, None]
    y = y.reshape(b, n, SSD_DI) * jax.nn.silu(z.astype(jnp.float32))
    y = rmsnorm(y, norm_g).astype(h.dtype)
    return y @ w_out, s_f, s_b

def conv_ffn(h, w_up, conv_w, conv_b, w_down):
    u = dwconv_centered(h @ w_up, conv_w, conv_b)
    g, v = jnp.split(u, 2, axis=-1)
    return (jax.nn.silu(g) * v) @ w_down

def setup_inputs(seed: int = 0) -> dict:
    key = jax.random.key(seed)
    ks = iter(jax.random.split(key, 48))

    def nrm(shape, scale):
        return jax.random.normal(next(ks), shape, jnp.float32) * scale

    def gain(shape):
        return 1.0 + nrm(shape, 0.05)

    def dt_bias(shape):
        dt = jnp.exp(jax.random.uniform(next(ks), shape, jnp.float32, math.log(1e-3), math.log(1e-1)))
        return dt + jnp.log(-jnp.expm1(-dt))

    d = D_MODEL
    return {
        "x_prompt": nrm((BATCH, SEQ, d), 1.0),
        "x_sample": nrm((DEC_BATCH, DEC_SEQ, d), 1.0),
        "cache_k": nrm((DEC_BATCH, N_ATT_LAYERS, PAST_LEN, DA_HEADS, 2, DA_HD), 1.0),
        "cache_v": nrm((DEC_BATCH, N_ATT_LAYERS, PAST_LEN, DA_HEADS, 2 * DA_HD), 1.0),
        "state_ssm_fwd": nrm((DEC_BATCH, N_SSD_LAYERS, SSD_HEADS, SSD_HEADDIM, SSD_STATE), 0.1),
        "state_ssm_bwd": nrm((DEC_BATCH, N_SSD_LAYERS, SSD_HEADS, SSD_HEADDIM, SSD_STATE), 0.1),
        "c": nrm((DEC_BATCH, d), 1.0),
        "c_ctx": nrm((d,), 1.0),
        "ada_w": nrm((DEPTH, d, 6 * d), 0.5 * d ** -0.5),
        "ada_b": nrm((DEPTH, 6 * d), 0.02),
        "norm_mix_g": gain((DEPTH, d)),
        "norm_ffn_g": gain((DEPTH, d)),
        "att_w_in": nrm((N_ATT_LAYERS, d, ATT_IN_W), d ** -0.5),
        "att_lambda": nrm((N_ATT_LAYERS, 4, DA_HD), 0.1),
        "att_subln_g": gain((N_ATT_LAYERS, 2 * DA_HD)),
        "pool_w": nrm((N_ATT_LAYERS, POOL_GROUPS, POOL_GC, POOL_GC), POOL_GC ** -0.5),
        "pool_scale": gain((N_ATT_LAYERS, POOL_W)),
        "att_w_out": nrm((N_ATT_LAYERS, MIX_W, d), MIX_W ** -0.5),
        "ssd_w_in": nrm((N_SSD_LAYERS, d, SSD_IN_W), d ** -0.5),
        "ssd_conv_w": nrm((N_SSD_LAYERS, SSD_CONV, SSD_XBC_W), SSD_CONV ** -0.5),
        "ssd_conv_b": nrm((N_SSD_LAYERS, SSD_XBC_W), 0.02),
        "ssd_dt_bias": dt_bias((N_SSD_LAYERS, 2, SSD_HEADS)),
        "ssd_a_log": jnp.log(jax.random.uniform(next(ks), (N_SSD_LAYERS, 2, SSD_HEADS), jnp.float32, 1.0, 16.0)),
        "ssd_d": gain((N_SSD_LAYERS, SSD_HEADS)),
        "ssd_norm_g": gain((N_SSD_LAYERS, SSD_DI)),
        "ssd_w_out": nrm((N_SSD_LAYERS, SSD_DI, d), SSD_DI ** -0.5),
        "ffn_w_up": nrm((DEPTH, d, 2 * D_FF), d ** -0.5),
        "ffn_conv_w": nrm((DEPTH, FFN_CONV, 2 * D_FF), FFN_CONV ** -0.5),
        "ffn_conv_b": nrm((DEPTH, 2 * D_FF), 0.02),
        "ffn_w_down": nrm((DEPTH, D_FF, d), D_FF ** -0.5),
        "final_norm_g": gain((d,)),
    }

def reference(x_prompt, x_sample, cache_k, cache_v, state_ssm_fwd, state_ssm_bwd, c, c_ctx,
              ada_w, ada_b, norm_mix_g, norm_ffn_g,
              att_w_in, att_lambda, att_subln_g, pool_w, pool_scale, att_w_out,
              ssd_w_in, ssd_conv_w, ssd_conv_b, ssd_dt_bias, ssd_a_log, ssd_d, ssd_norm_g, ssd_w_out,
              ffn_w_up, ffn_conv_w, ffn_conv_b, ffn_w_down, final_norm_g):
    rope = axial_rope_tables(x_sample.shape[1])
    xp, xs = x_prompt, x_sample
    k_new, v_new, sf_new, sb_new = [], [], [], []
    for l in range(DEPTH):
        i = l // 2
        mod_p = adaln(c_ctx, ada_w[l], ada_b[l])
        mod_s = adaln(c, ada_w[l], ada_b[l])
        hp = modulate(xp, norm_mix_g[l], mod_p[0], mod_p[1])
        hs = modulate(xs, norm_mix_g[l], mod_s[0], mod_s[1])
        if l % 2 == 0:
            lam_init = 0.8 - 0.6 * math.exp(-0.3 * l)
            att = (att_w_in[i], att_lambda[i], att_subln_g[i], pool_w[i], pool_scale[i], att_w_out[i])
            mp, kp, vp = even_mixer(hp, *att, lam_init)
            ms = even_mixer(hs, *att, lam_init, rope=rope, ctx_k=cache_k[:, i], ctx_v=cache_v[:, i])[0]
            k_new.append(kp)
            v_new.append(vp)
        else:
            ssd = (ssd_w_in[i], ssd_conv_w[i], ssd_conv_b[i], ssd_dt_bias[i], ssd_a_log[i], ssd_d[i], ssd_norm_g[i], ssd_w_out[i])
            mp, sf, sb = ssd_mixer(hp, *ssd)
            ms = ssd_mixer(hs, *ssd, init_f=state_ssm_fwd[:, i], init_b=state_ssm_bwd[:, i])[0]
            sf_new.append(sf.astype(x_prompt.dtype))
            sb_new.append(sb.astype(x_prompt.dtype))
        xp = xp + mod_p[2][..., None, :] * mp
        xs = xs + mod_s[2][..., None, :] * ms
        ffn = (ffn_w_up[l], ffn_conv_w[l], ffn_conv_b[l], ffn_w_down[l])
        xp = xp + mod_p[5][..., None, :] * conv_ffn(modulate(xp, norm_ffn_g[l], mod_p[3], mod_p[4]), *ffn)
        xs = xs + mod_s[5][..., None, :] * conv_ffn(modulate(xs, norm_ffn_g[l], mod_s[3], mod_s[4]), *ffn)
    y_prompt = rmsnorm(xp, final_norm_g)
    y_sample = rmsnorm(xs, final_norm_g)
    new_cache_k = jnp.stack(k_new, axis=1)
    new_cache_v = jnp.stack(v_new, axis=1)
    new_state_fwd = jnp.stack(sf_new, axis=1)
    new_state_bwd = jnp.stack(sb_new, axis=1)
    return (y_prompt, y_sample, new_cache_k, new_cache_v, new_state_fwd, new_state_bwd)


_drawn_inputs = setup_inputs


def setup_inputs(seed=0):
    import zlib

    import numpy as np

    out = dict(_drawn_inputs(seed))
    spreads = {}
    factors = {'norm_ffn_g': 2.833,
     'att_lambda': 8.0,
     'att_subln_g': 3.959,
     'pool_scale': 3.889,
     'ssd_d': 8.0,
     'ssd_norm_g': 4.206,
     'ffn_conv_b': 6.999,
     'state_ssm_fwd': 4.248,
     'state_ssm_bwd': 4.895}
    for name, (base, spread) in spreads.items():
        noise = np.random.default_rng([zlib.crc32(name.encode()), seed]).standard_normal(out[name].shape)
        drawn = base * np.exp(spread * noise) if base else spread * noise
        out[name] = __import__('jax').numpy.asarray(drawn.astype(out[name].dtype))
    for name, factor in factors.items():
        out[name] = (out[name] * factor).astype(out[name].dtype)
    return out
```

```python
import math
from contextlib import ExitStack

import numpy as np
import concourse.bass as bass
from concourse import mybir

F32 = mybir.dt.float32
F32R = mybir.dt.float32r
ALU = mybir.AluOpType
ACT = mybir.ActivationFunctionType
AXX = mybir.AxisListType.X

P = 128
D = 1024
KD = D // P
NP_, NS = 128, 512
W = NP_ + 1 + NS + 1
HALF = W // 4 * 2 + 2
HALVES = (slice(0, HALF), slice(HALF, W))
S0 = NP_ + 1
CHUNKS = 1 + NS // P
HEADS = 4
HD = 64
KEYS = NS + P
FF = 2816
FT = FF // P
PARTS = ((0, 8), (8, 8), (16, 6))
DI = 2048
GROUPS = 4
GH = 8
EPS = 1e-6
LAM_INIT = 0.8 - 0.6 * math.exp(0.0)
POOL_WINDOWS = (2, 4, 8, 16)

T_A, T_B, T_F0 = 0, 16, 24
FFN_TILES = 2 * FT + 3 * KD
T_E = T_F0 + FFN_TILES
T_O = T_E + 40
T_F1 = T_O + 16
T_END = T_F1 + FFN_TILES
A_B, A_E, A_O = T_B, T_E, T_O
A_F1 = A_O + 8


def chunk_col(c):
    return 0 if c == 0 else S0 + (c - 1) * P


PARAM_ROWS = (("c_ctx", 8), ("c", 8), ("norm_mix_g", 16), ("norm_ffn_g", 16), ("pool_scale", 4), ("att_subln_g", 1),
              ("ada_b", 96), ("ssd_norm_g", 16), ("ssd_conv_w", 72), ("ssd_conv_b", 24), ("ffn_conv_w", 264),
              ("ffn_conv_b", 88))
PARAM_AT = {}
_n = 0
for _name, _rows in PARAM_ROWS:
    PARAM_AT[_name] = _n
    _n += _rows
N_PARAM = _n
PARAM_TILES = -(-N_PARAM // P)
N_PAR_DMA = sum((PARAM_AT[n_] + r_ - 1) // P - PARAM_AT[n_] // P + 1 for n_, r_ in PARAM_ROWS)


def att_schedule():
    after = {}

    def put(t, q, *ev):
        after.setdefault((t, q), []).append(ev)

    for h in range(HEADS):
        b = 3 * h + 3
        if h:
            put(b, 0, "PV", h - 1, 4)
        put(3 * h + 2, 3, "rotq", h)
        put(3 * h + 2, 3, "rotk", h)
        put(3 * h + 2, 3, "trk", h)
        put(b, 0, "trv", h)
        if h:
            put(b, 1, "ssO", h - 1)
        put(b, 1, "S", h, 0)
        put(b, 3, "S", h, 1)
        put(b, 3, "T", h, 0)
        if h:
            put(b, 3, "rbO", h - 1)
        put(b + 1, 1, "S", h, 2)
        put(b + 1, 1, "T", h, 1)
        put(b + 1, 1, "PV", h, 0)
        put(b + 1, 3, "S", h, 3)
        put(b + 1, 3, "T", h, 2)
        put(b + 1, 3, "PV", h, 1)
        put(b + 2, 1, "S", h, 4)
        put(b + 2, 1, "T", h, 3)
        put(b + 2, 1, "PV", h, 2)
        put(b + 2, 2, "T", h, 4)
        put(b + 2, 2, "PV", h, 3)
    put(15, 0, "PV", 3, 4)
    put(15, 1, "ssO", 3)
    put(15, 3, "rbO", 3)
    for g in range(3):
        put(13 + g, 2, "pool", g)
    put(15, 3, "pool", 3)
    out = []
    for t in range(16):
        for q in range(4):
            out.append(("mm", t, q))
            out += after.get((t, q), [])
    return out


ATT = att_schedule()
ATT_READER = {"rotq": "dve", "rotk": "dve", "trk": "act", "trv": "act", "S": "act", "T": "act", "PV": "act",
              "ssO": "dve", "rbO": "dve", "pool": "dve"}


def uses_of(schedule, readers, expand):
    index, ends, count = {}, [], {"act": 0, "dve": 0}
    for ev in schedule:
        if ev[0] in readers:
            for key in expand(ev):
                index[key] = len(ends)
                r = readers[ev[0]]
                count[r] += 1
                ends.append((r, count[r]))
    return index, ends


ATT_USE, ATT_END = uses_of(ATT, ATT_READER, lambda ev: [ev + (0,), ev + (1,)] if ev[0] == "S" else [ev])


def ssd_schedule():
    after = {}

    def put(e, q, *ev):
        after.setdefault((e, q), []).append(ev)

    for g in range(GROUPS):
        b = 10 * g
        put(b + 1, 1, "trB", g)
        for j in range(4):
            put(b + 3 + j, 0, "trx", g, j)
        put(b + 7, 0, "init", g, 0)
        put(b + 7, 0, "init", g, 1)
        slots = [(b + 7 + i // 2, i % 2) for i in range(0, 40)]
        for i, c in enumerate((4, 3, 2, 0)):
            put(*slots[i], "csb", g, c)
        for c in range(CHUNKS):
            at = (3, 6, 10, 13, 16)[c]
            put(*slots[at], "cb", g, c)
            if c < 4:
                put(*slots[at], "csf", g, c)
            put(*slots[at + 2], "yd", g, c)
            if c:
                put(*slots[at + 3], "yo", g, c)
            put(*slots[at + 5], "yT", g, c)
        put(*slots[10], "stT", g)
    out = []
    for e in range(40):
        for q in range(2):
            out.append(("mm", e, q))
            out += sorted(after.pop((e, q), []), key=lambda ev: ev[1])
    for k in sorted(after):
        out += after[k]
    return out


SSD = ssd_schedule()
SSD_READER = {"trB": "act", "trx": "act", "init": "act", "csb": "dve", "csf": "dve", "cb": "dve", "yd": "dve",
              "yo": "dve", "yT": "dve", "stT": "act"}
SSD_USE, SSD_END = uses_of(
    SSD, SSD_READER,
    lambda ev: [ev + (0,), ev + (1,)] if ev[0] in ("trB", "trx", "yo", "stT") else [ev])
G_AT = {ev: i + 1 for i, ev in enumerate(ev for ev in ATT if ev[0] in ("rbO", "pool"))}
SSD_TILE, _e = {}, 0
for _ev in SSD:
    _e = _ev[1] if _ev[0] == "mm" else _e
    SSD_TILE[_ev] = _e
CS_LIST = [ev for ev in SSD if ev[0] in ("csb", "csf")]
CS_AT = {ev: i for i, ev in enumerate(CS_LIST)}


class Steps:

    def __init__(self, eng, sem):
        self.eng, self.sem, self.n, self.off = eng, sem, 0, 0

    def __call__(self, instruction):
        instruction.then_inc(self.sem, 1)
        self.n += 1

    def wait(self):
        self.eng.wait_ge(self.sem, self.off + self.n)

    def turn(self, i, per):
        self.mark, self.per, self.off = self.n, per, i * per

    def leave(self, turns):
        assert self.n - self.mark == self.per, (self.n - self.mark, self.per)
        self.n, self.off = self.mark + turns * self.per, 0


def bc(ap, at, n):
    shape = list(ap.shape)
    return ap.unsqueeze(at).broadcast_to(shape[:at] + [n] + shape[at:])


def build(nc, A, O):
    with ExitStack() as ctx:
        base = -(-nc.sbuf_base // 32) * 32
        top = [base]

        def at(name, shape, dt, offset):
            t = nc.alloc_sbuf_tensor_at(name, shape, dt, offset=offset)
            return t, offset + -(-4 * int(np.prod(shape[1:])) // 32) * 32

        def fixed(name, shape, dt=F32):
            t, top[0] = at(name, shape, dt, top[0])
            return t

        def phase(start, end=229344):
            here = [start]

            def alloc(name, shape, dt=F32):
                t, here[0] = at(name, shape, dt, here[0])
                assert here[0] <= end, (name, here[0])
                return t
            return alloc

        consts = fixed("consts", [P, 4 * P])
        ident, m_le, m_ge, perm = (consts[:, i * P:(i + 1) * P] for i in range(4))
        masks = consts[:, P:3 * P].rearrange("p (a b) -> p a b", a=2)
        early_at = top[0] - 4 * P
        pmat = fixed("pmat", [P, 4, P])
        wdt_hi = fixed("wdt_hi", [P, KD, 64], F32R)
        wdt_lo = fixed("wdt_lo", [P, KD, 64], F32R)
        early_end = top[0]
        ones = fixed("ones", [P, P])
        par = fixed("par", [P, N_PARAM])
        svec = fixed("svec", [P, KD, 2])
        mod = fixed("mod", [P, 96, 2])
        gain1 = fixed("gain1", [P, 4, KD, 2])
        small = fixed("small", [P, 64])
        dtb_bc = fixed("dtb_bc", [P, 64])
        a_bc = fixed("a_bc", [P, 64])
        d_bc = fixed("d_bc", [P, 32])
        h_at = top[0]
        h_hi = fixed("h_hi", [P, KD, W], F32R)
        h_lo = fixed("h_lo", [P, KD, W], F32R)
        y_hi, _ = at("y_hi", [P, 2 * KD, W], F32R, h_at)
        g_at = top[0]
        g_hi = fixed("g_hi", [P, KD, W], F32R)
        g_lo = fixed("g_lo", [P, KD, W], F32R)
        yg, _ = at("yg", [P, 2 * KD, W], F32, g_at)
        y_lo, _ = at("y_lo", [P, 2 * KD, W], F32R, g_at)
        ada0 = [at(f"ada0_{i}", [P, KD, 2 * P], F32, g_at + i * KD * 2 * P * 4)[0] for i in range(5)]
        raw = [fixed(f"raw{i}", [P, KD, P]) for i in range(4)]
        w_hi = [fixed(f"w_hi{i}", [P, KD, P], F32R) for i in range(2)]
        w_lo = [fixed(f"w_lo{i}", [P, KD, P], F32R) for i in range(2)]
        ada_at = top[0]
        ada1 = fixed("ada1", [P, KD, 2 * P])
        x_at = top[0]
        xT = fixed("xT", [P, KD, W])
        rest_at = top[0]

        a = phase(rest_at)
        sq = [a(f"sq{i}", [P, W]) for i in range(2)]
        diag = a("diag", [P, CHUNKS, P])
        tn = [a(f"tn{i}", [P, W]) for i in range(2)]
        cg, cv, sg, hm = (a(n, [P, W]) for n in ("cg", "cv", "sg", "hm"))
        rbs = a("rbs", [P, W])
        a = phase(rest_at)
        for _i in range(2):
            a(f"_pad{_i}", [P, W])
        a("_pad_d", [P, CHUNKS, P])
        for _i in range(2):
            a(f"_padt{_i}", [P, W])
        x_in = a("x_in", [P, CHUNKS, D])
        par_in = a("par_in", [P, PARAM_TILES, P])
        wdt = a("wdt", [P, KD, 64])
        lam_in = a("lam_in", [P, 4, HD])
        a = phase(rest_at)
        a("_pad2", [P, 2 * W])
        a("_pad3", [P, CHUNKS, P])
        fg_bc = a("fg_bc", [P, D])
        y_out = [a(f"y_out{i}", [P, D]) for i in range(2)]
        a = phase(x_at)
        rope = a("rope", [P, 2, NS])
        inv_n = a("inv_n", [P, NP_ + NS])
        qz = a("qz", [P, 2, NP_ + NS])
        kT = a("kT", [P, NP_ + KEYS])
        v_tok = [a(f"v_tok{i}", [P, CHUNKS + 1, P]) for i in range(2)]
        q_raw, k_raw, v_raw = (a(n, [P, W]) for n in ("q_raw", "k_raw", "v_raw"))
        ck_in = a("ck_in", [P, HEADS, P])
        k_out = a("k_out", [P, P])
        prob = [a(f"prob{i}", [P, 2, KEYS]) for i in range(2)]
        att = [a(f"att{i}", [P, KEYS]) for i in range(2)]
        attT = [a(f"attT{i}", [P, CHUNKS, P]) for i in range(2)]
        pb = [a(f"pb{i}", [P, 672]) for i in range(3)]
        pooled = a("pooled", [P, W])
        pmul = a("pmul", [P, W])
        rtmp = pmul[:, 0:NS]
        o_sb = a("o_sb", [P, W])
        o_sq = a("o_sq", [P, W])
        o_diag = a("o_diag", [P, CHUNKS, P])
        o_nrm = a("o_nrm", [P, W])
        a = phase(ada_at)
        bT = [a(f"bT{i}", [P, W]) for i in range(2)]
        cT = [a(f"cT{i}", [P, W]) for i in range(2)]
        b_tok = [a(f"b_tok{i}", [P, CHUNKS, P]) for i in range(2)]
        x_tok = [a(f"x_tok{i}", [P, CHUNKS, 512]) for i in range(2)]
        cx = a("cx", [P, W])
        R = a("R", [P, 2, GH, P])
        xdt = a("xdt", [P, 2, 512])
        xw = [a(f"xw{i}", [P, 512]) for i in range(2)]
        st_b = a("st_b", [P, 4, 512])
        st_f = [a(f"st_f{i}", [P, 512]) for i in range(2)]
        st_in = a("st_in", [P, 2, 4, P])
        st_p = a("st_p", [P, 2, 512])
        st_out = a("st_out", [P, 4, P])
        y2 = a("y2", [P, 512])
        st_tmp = y2
        dt, acs, dec, wst = (a(n, [P, CHUNKS, 64]) for n in ("dt", "acs", "dec", "wst"))
        a = phase(early_at, early_end)
        cbm = a("cbm", [P, 2, P])
        y1 = [a(f"y1_{i}", [P, 512]) for i in range(2)]
        eacs = a("eacs", [P, CHUNKS, 64])
        dt_x, dt_e, dt_s, dt_z, dt_p, da = (R[:, :, :, :].rearrange("p a b c -> p (a b c)")[:, i * 320:(i + 1) * 320]
                                            for i in range(6))
        da3 = da.rearrange("p (c x) -> p c x", c=CHUNKS)
        acsT = xdt[0:64, :, :].rearrange("p a b -> p (a b)")[:, 0:CHUNKS * P]

        scr_x = nc.dram_tensor("scr_x", (P, KD, W), F32, kind="Internal").ap()
        scr_acs = nc.dram_tensor("scr_acs", (CHUNKS, 64, P), F32, kind="Internal").ap()

        ps = ctx.enter_context(nc.psum_tensor("ps", [P, 8 * 512], F32))

        def acc(slot):
            at0 = 1024 * slot + 512 - HALF
            return ps[:, at0:at0 + W]

        def bank(b, n=512, o=0):
            return ps[:, 512 * b + o:512 * b + o + n]

        def sem(name):
            return ctx.enter_context(nc.semaphore(name))

        raw_in = [sem(f"raw_in{i}") for i in range(4)]
        ada0_in = [sem(f"ada0_in{i}") for i in range(5)]
        ada1_in = sem("ada1_in")
        consts_in, par_dma, x_dma, bcast_in, wdt_in, ones_done = (sem(n) for n in
                                                       ("consts_in", "par_dma", "x_dma", "bcast_in", "wdt_in", "ones_done"))
        x_spilled, x_back, rope_in, ck_dma, cv_dma0, cv_dma1 = (sem(n) for n in (
            "x_spilled", "x_back", "rope_in", "ck_dma", "cv_dma0", "cv_dma1"))
        inv_in = sem("inv_in")
        k_stored, v_stored, acs_stored, st_in_dma, st_stored, fg_in = (sem(n) for n in (
            "k_stored", "v_stored", "acs_stored", "st_in_dma", "st_stored", "fg_in"))
        R_in, R_used = [sem("R_in0"), sem("R_in1")], sem("R_used")
        w_hi_done, w_split, mm_done = sem("w_hi_done"), sem("w_split"), sem("mm_done")
        acc_free_dve, acc_free_act = sem("acc_free_dve"), sem("acc_free_act")
        dve_step, act_step = sem("dve_step"), sem("act_step")
        par_ps, par_done, svec_done, memset_done, xt_ps, xt_done, wdt_hi_done, lam_e = (sem(n) for n in (
            "par_ps", "par_done", "svec_done", "memset_done", "xt_ps", "xt_done", "wdt_hi_done", "lam_e"))
        abc_done, lam_s = sem("abc_done"), sem("lam_s")
        ada_mm, mod_done = sem("ada_mm"), sem("mod_done")
        sq_ready, ss_done, ms_done, root_done, diag_done, rb_done, t_done, h_hi_done, h_ready = (sem(n) for n in (
            "sq_ready", "ss_done", "ms_done", "root_done", "diag_done", "rb_done", "t_done", "h_hi_done", "h_ready"))
        att_mm, att_free_act, att_free_dve = sem("att_mm"), sem("att_free_act"), sem("att_free_dve")
        qkv_raw, q_roped, k_roped, v_done, smax, pexp, att_a = (sem(n) for n in (
            "qkv_raw", "q_roped", "k_roped", "v_done", "smax", "pexp", "att_a"))
        aT_done, o_copied, o_sqd, o_ms, o_root, o_dg, o_n, o_hi, pool_in, pool_y, pool_hi, g_ready = (sem(n) for n in (
            "aT_done", "o_copied", "o_sqd", "o_ms", "o_root", "o_dg", "o_n", "o_hi", "pool_in", "pool_y", "pool_hi",
            "mix_ready"))
        ffn_id, ffn_silu, hm_done, ffn_hi, f_ready = (sem(n) for n in ("ffn_id", "ffn_silu", "hm_done", "ffn_hi",
                                                                       "ffn_ready"))
        dt_mm, dt_xb, dt_exp, da_done, acs_mm, acs_done, tot_w, acs_exp, wst_done, acsT_ps, acsT_done = (
            sem(n) for n in ("dt_mm", "dt_xb", "dt_exp", "da_done", "acs_mm", "acs_done", "tot_w", "acs_exp",
                             "wst_done", "acsT_ps", "acsT_done"))
        ssd_mm, ssd_free_act, ssd_free_dve = sem("ssd_mm"), sem("ssd_free_act"), sem("ssd_free_dve")
        conv_id, conv_silu, zs_done, tok_done, xw_done, st_done, seg_done, seg_exp, cbm_done, W_done, y_done = (
            sem(n) for n in ("conv_id", "conv_silu", "zs_done", "tok_done", "xw_done", "st_done", "seg_done",
                             "seg_exp", "cbm_done", "W_done", "y_done"))
        st_copied, yg_done = sem("st_copied"), sem("yg_done")
        yn_hi, y_ready, y_sqd, y_ss, yr_ms, yr_root, yr_dg, yr_rb, yr_done = (sem(n) for n in (
            "yn_hi", "y_ready", "y_sqd", "y_ss", "yr_ms", "yr_root", "yr_dg", "yr_rb", "yr_done"))
        fin_ps, fin_y, so_x, da_read, pmat_in = sem("fin_ps"), sem("fin_y"), sem("so_x"), sem("da_read"), sem("pmat_in")
        y_stored = [sem("y_stored0"), sem("y_stored1")]

        block = ctx.enter_context(nc.Block())

        def pcol(name, i=0):
            return par[:, PARAM_AT[name] + i:PARAM_AT[name] + i + 1]

        def modc(layer, j, k, s):
            i = layer * 48 + j * 8 + k
            return mod[:, i, s:s + 1]

        def acc_free(a_):
            ends = acc_ends[a_]
            return (acc_free_act if ends[0] == "act" else acc_free_dve), ends[1]

        acc_ends, count = [], {"act": 0, "dve": 0}
        for a_ in range(A_F1 + FFN_TILES):
            who = "dve"
            if a_ < 12 or (A_E <= a_ < A_O and (a_ - A_E) % 10 >= 6):
                who = "act"
            count[who] += 1
            acc_ends.append((who, count[who]))

        def dve_accs(a_):
            assert acc_ends[a_][0] == "dve"
            return acc_ends[a_][1]

        def att_end(key):
            who, n = ATT_END[ATT_USE[key]]
            return (att_free_act if who == "act" else att_free_dve), n

        def ssd_end(key):
            who, n = SSD_END[SSD_USE[key]]
            return (ssd_free_act if who == "act" else ssd_free_dve), n

        def att_col(t):
            return (t % 3) * 512 + (t // 3) * P if t < 12 else 1536 + (t - 12) * P

        def ssd_tile(e):
            g, i = divmod(e, 10)
            return ("b", 16 + g) if i == 0 else ("c", 20 + g) if i == 1 else ("x", 4 * g + i - 2) if i < 6 else \
                ("z", 4 * g + i - 6)

        def ssd_col(e):
            kind, m = ssd_tile(e)
            return m * P if kind == "z" else DI + m * P

        kp = "(k p) m -> p k m"
        w_att = A["att_w_in"][0].rearrange(kp, p=P)
        w_ao = A["att_w_out"][0].rearrange(kp, p=P)
        w_ssd = A["ssd_w_in"][0].rearrange(kp, p=P)
        w_so = A["ssd_w_out"][0].rearrange(kp, p=P)
        w_up = [A["ffn_w_up"][l].rearrange(kp, p=P) for l in range(2)]
        w_dn = [A["ffn_w_down"][l].rearrange(kp, p=P) for l in range(2)]
        w_ada = [A["ada_w"][l].rearrange(kp, p=P) for l in range(2)]

        ADA_A, ADA_B, ADA_F = 8, 11, 20

        @block.sync
        def _(sp):
            def param_rows():
                n = 0
                srcs = {
                    "c_ctx": A["c_ctx"].rearrange("(r c) -> r c", c=P), "c": A["c"].rearrange("o (r c) -> (o r) c", c=P),
                    "norm_mix_g": A["norm_mix_g"].rearrange("l (r c) -> (l r) c", c=P),
                    "norm_ffn_g": A["norm_ffn_g"].rearrange("l (r c) -> (l r) c", c=P),
                    "pool_scale": A["pool_scale"].rearrange("l (r c) -> (l r) c", c=P),
                    "att_subln_g": A["att_subln_g"],
                    "ada_b": A["ada_b"].rearrange("l (r c) -> (l r) c", c=P),
                    "ssd_norm_g": A["ssd_norm_g"].rearrange("l (r c) -> (l r) c", c=P),
                    "ssd_conv_w": A["ssd_conv_w"][0].rearrange("l (r c) -> (l r) c", c=P),
                    "ssd_conv_b": A["ssd_conv_b"].rearrange("l (r c) -> (l r) c", c=P),
                    "ffn_conv_w": A["ffn_conv_w"].rearrange("l j (r c) -> (l j r) c", c=P),
                    "ffn_conv_b": A["ffn_conv_b"].rearrange("l (r c) -> (l r) c", c=P),
                }
                for name, rows in PARAM_ROWS:
                    r = 0
                    while r < rows:
                        i, p0 = divmod(PARAM_AT[name] + r, P)
                        m = min(rows - r, P - p0)
                        sp.dma_start(par_in[p0:p0 + m, i, :], srcs[name][r:r + m, :]).then_inc(par_dma, 16)
                        r += m
                        n += 1
                return n

            def ada(s):
                l, c0 = divmod(s * 256, 6 * D)
                src = w_ada[l][:, :, c0:c0 + 256]
                if s < 8:
                    if s >= 5:
                        sp.wait_ge(ada_mm, s - 4)
                    sp.dma_start(ada0[s % 5][:, :, :], src).then_inc(ada0_in[s % 5], 16)
                else:
                    if s > 8:
                        sp.wait_ge(ada_mm, s)
                    sp.dma_start(ada1[:, :, :], src).then_inc(ada1_in, 16)

            def weight(t, src, k):
                if not (isinstance(t, int) and t < 4):
                    sp.wait_ge(w_split, t - 3)

            def load(slot, t, src, k=KD):
                weight(t, src, k)
                sp.dma_start(raw[slot][:, 0:k, :], src).then_inc(raw_in[slot], 16)

            sp.dma_start(consts[:, :], A["tables"][:, 0:4 * P]).then_inc(consts_in, 16)
            assert param_rows() == N_PAR_DMA
            ada(0)
            for c in range(CHUNKS):
                src = A["x_prompt"][0] if c == 0 else A["x_sample"][0, (c - 1) * P:c * P, :]
                sp.dma_start(x_in[:, c, :], src).then_inc(x_dma, 16)
            for s in range(1, 5):
                ada(s)
            sp.dma_start(lam_in[:, :, :], A["att_lambda"][0].partition_broadcast(P)).then_inc(bcast_in, 16)
            sp.dma_start(dtb_bc[:, :], A["ssd_dt_bias"][0].rearrange("a b -> (a b)").partition_broadcast(P)
                         ).then_inc(bcast_in, 16)
            sp.dma_start(a_bc[:, :], A["ssd_a_log"][0].rearrange("a b -> (a b)").partition_broadcast(P)
                         ).then_inc(bcast_in, 16)
            sp.dma_start(d_bc[:, :], A["ssd_d"][0].partition_broadcast(P)).then_inc(bcast_in, 16)
            sp.dma_start(pmat[:, :, :], A["pool_w"][0].rearrange("g c d -> c g d")).then_inc(pmat_in, 16)
            sp.dma_start(wdt[:, :, :], w_ssd[:, :, DI + 3072:DI + 3072 + 64]).then_inc(wdt_in, 16)
            for t in range(4):
                load(t, t, w_att[:, :, att_col(t):att_col(t) + P])
            for s in range(5, 8):
                ada(s)
            ada(8)
            sp.wait_ge(h_ready, 8)
            sp.dma_start(scr_x, xT[:, :, :]).then_inc(x_spilled, 16)
            sp.wait_ge(x_spilled, 16)
            sp.dma_start(rope[:, :, :], A["tables"][:, 4 * P:4 * P + 2 * NS].rearrange("p (a b) -> p a b", a=2)
                         ).then_inc(rope_in, 16)
            sp.dma_start(ck_in[:, :, :], A["cache_k"][0, 0].rearrange("t h c d -> t h (c d)")).then_inc(ck_dma, 16)
            sp.dma_start(inv_n[:, :], A["inv_n"][0].partition_broadcast(P)).then_inc(inv_in, 16)
            for h in range(2):
                sp.dma_start(v_tok[h][:, CHUNKS, :], A["cache_v"][0, 0, :, h, :]).then_inc((cv_dma0, cv_dma1)[h], 16)
            for t in range(4, 16):
                load(t % 4, t, w_att[:, :, att_col(t):att_col(t) + P])
                if t < 6:
                    ada(t + 5)
                if t % 3 == 2 and t < 14:
                    h = t // 3 - 1
                    sp.wait_ge(*att_end(("trv", h)))
                    sp.dma_start(O["new_cache_v"][0, 0, :, h, :], v_tok[h % 2][:, 0, :]).then_inc(v_stored, 16)
                    sp.wait_ge(*att_end(("trk", h)))
                    sp.dma_start(O["new_cache_k"][0, 0, :, h, :, :].rearrange("t c d -> t (c d)"), k_out[:, :]
                                 ).then_inc(k_stored, 16)
                if t in (9, 12):
                    h = 2 + (t - 9) // 3
                    sp.wait_ge(*att_end(("PV", h - 2, 4)))
                    sp.dma_start(v_tok[h % 2][:, CHUNKS, :], A["cache_v"][0, 0, :, h, :]
                                 ).then_inc((cv_dma0, cv_dma1)[h % 2], 16)
            for t in range(16, 20):
                load(t % 4, t, w_ao[:, :, (t - 16) * P:(t - 15) * P])
                if t == 16:
                    ada(ADA_B)
                if t == 17:
                    sp.wait_ge(*att_end(("trv", 3)))
                    sp.dma_start(O["new_cache_v"][0, 0, :, 3, :], v_tok[1][:, 0, :]).then_inc(v_stored, 16)
                    sp.wait_ge(*att_end(("trk", 3)))
                    sp.dma_start(O["new_cache_k"][0, 0, :, 3, :, :].rearrange("t c d -> t (c d)"), k_out[:, :]
                                 ).then_inc(k_stored, 16)
                if t > 16:
                    sp.wait_ge(pool_y, t - 16)
                    sp.dma_start(inv_n[:, :], A["inv_n"][t - 16].partition_broadcast(P)).then_inc(inv_in, 16)
            sp.wait_ge(g_ready, 8)
            sp.wait_ge(k_stored, 64)
            sp.wait_ge(v_stored, 64)
            sp.dma_start(xT[:, :, :], scr_x).then_inc(x_back, 16)
            for t in range(20, 24):
                load(t % 4, t, w_ao[:, :, (t - 16) * P:(t - 15) * P])
                ada(ADA_B + t - 19)
            for s in range(5, 9):
                ada(ADA_B + s)

            def ffn(l, t0):
                for p, (m0, n) in enumerate(PARTS):
                    first = 2 * m0 + 8 * p + t0

                    def two_pairs(i):
                        for j in range(2):
                            for half in range(2):
                                col = half * FF + m0 * P + (2 * i + j) * P
                                load(2 * j + half, first + 4 * i + 2 * j + half, w_up[l][:, :, bass.ds(col, P)])
                            if l == 0:
                                for rep in range(2 if p == 2 else 1):
                                    yield_ada(p, i, j, rep)

                    def yield_ada(p, i, j, rep):
                        if p < 2:
                            s = ADA_F + 8 * p + 2 * i + j
                        else:
                            s = ADA_F + 16 + 4 * i + 2 * j + rep
                        sp.wait_ge(ada_mm, s)
                        c0 = (s - 24) * 256
                        sp.dma_start(ada1[:, :, :], w_ada[1][:, :, bass.ds(c0, 256)]).then_inc(ada1_in, 16)

                    if l == 0 and p == 0:
                        for i in range(4):
                            for j in range(2):
                                for half in range(2):
                                    col = half * FF + (2 * i + j) * P
                                    load(2 * j + half, first + 4 * i + 2 * j + half, w_up[l][:, :, col:col + P])
                                ada(ADA_F + 2 * i + j)
                    else:
                        with sp.Fori(0, n // 2) as i:
                            two_pairs(i)
                    down = first + 2 * n
                    with sp.Fori(0, 2) as i:
                        for j in range(4):
                            load(j, down + 4 * i + j, w_dn[l][:, m0:m0 + n, bass.ds((4 * i + j) * P, P)], n)

            ffn(0, T_F0)
            sp.wait_ge(h_ready, 24)
            sp.dma_start(scr_x, xT[:, :, :]).then_inc(x_spilled, 16)
            def row_loads(n, d_):
                g, c = divmod(n, CHUNKS)
                if n and d_ == 0:
                    sp.wait_ge(R_used, n)
                elif n:
                    sp.wait_ge(ssd_mm, SSD_USE[("yd", (n - 1) // CHUNKS, (n - 1) % CHUNKS)] + 1)
                src = scr_acs[c, 32 * d_ + g * GH:32 * d_ + (g + 1) * GH, :]
                sp.dma_start(R[:, d_, :, :], src.partition_broadcast(P)).then_inc(R_in[d_], 16)

            def state_loads(g):
                if g:
                    sp.wait_ge(ssd_mm, SSD_USE[("init", g - 1, 1)] + 1)
                for d_, name in enumerate(("state_ssm_fwd", "state_ssm_bwd")):
                    src = A[name][0, 0, g * GH:(g + 1) * GH].rearrange("(q r) p n -> (r p) q n", r=2)
                    sp.dma_start(st_in[:, d_, :, :], src).then_inc(st_in_dma, 16)

            def state_stores(g):
                for d_, name in enumerate(("new_state_fwd", "new_state_bwd")):
                    dst = O[name][0, 0, g * GH:(g + 1) * GH].rearrange("(q r) p n -> (r p) q n", r=2)
                    sp.wait_ge(*ssd_end(("stT", g, d_)))
                    sp.dma_start(dst, st_out[:, :, :]).then_inc(st_stored, 16)

            def beside(tile):
                for ev in SSD:
                    if SSD_TILE[ev] != tile:
                        continue
                    if ev[0] == "init" and ev[2] == 1 and ev[1] + 1 < GROUPS:
                        state_loads(ev[1] + 1)
                    if ev[0] == "yd" and ev[1:] != (GROUPS - 1, CHUNKS - 1):
                        for d_ in range(2):
                            row_loads(CHUNKS * ev[1] + ev[2] + 1, d_)
                    if ev[0] == "stT":
                        state_stores(ev[1])

            LEAD = 5
            for e in range(40):
                load(e % 4, T_E + e, w_ssd[:, :, ssd_col(e):ssd_col(e) + P])
                if e == 4:
                    sp.wait_ge(acsT_done, 2)
                    sp.dma_start(scr_acs.rearrange("c h i -> h c i"),
                                 acsT.rearrange("p (c i) -> p c i", c=CHUNKS)).then_inc(acs_stored, 16)
                    sp.wait_ge(acs_stored, 16)
                    state_loads(0)
                    sp.wait_ge(da_read, 1)
                    row_loads(0, 0)
                    row_loads(0, 1)
                beside(e - LEAD)
            for t in range(4):
                load(t, T_O + t, w_so[:, (t % 2) * 8:(t % 2) * 8 + 8, (t // 2) * P:(t // 2 + 1) * P])
                beside(40 + t - LEAD)
            for tile in range(40 + 4 - LEAD, max(SSD_TILE.values()) + 1):
                beside(tile)
            sp.wait_ge(*ssd_end(("yT", 3, 4)))
            sp.wait_ge(st_stored, 128)
            sp.dma_start(xT[:, :, :], scr_x).then_inc(x_back, 16)
            with sp.Fori(1, 4) as i:
                for j in range(4):
                    load(j, T_O + 4 * i + j, w_so[:, (j % 2) * 8:(j % 2) * 8 + 8, bass.ds((2 * i + j // 2) * P, P)])
            ffn(1, T_F1)
            sp.wait_ge(f_ready, 2 * FT)
            sp.dma_start(fg_bc[:, :], A["final_norm_g"].partition_broadcast(P)).then_inc(fg_in, 16)
            for c in range(CHUNKS):
                dst = O["y_prompt"][0] if c == 0 else O["y_sample"][0, (c - 1) * P:c * P, :]
                sp.wait_ge(fin_y, c + 1)
                sp.dma_start(dst, y_out[c % 2][:, :]).then_inc(y_stored[c % 2], 16)
            sp.wait_ge(y_stored[0], 48)
            sp.wait_ge(y_stored[1], 32)
            sp.wait_ge(k_stored, 64)
            sp.wait_ge(v_stored, 64)
            sp.wait_ge(st_stored, 128)

        @block.gpsimd
        def _(pool):
            nc.gpsimd.memset(ones[:, :], 1.0).then_inc(ones_done, 1)

            def split(j, t, i, k):
                loads, before = 16 * (i + 1), t - 1
                if not isinstance(t, int):
                    loads, before = (nc.snap(v, bass.OrderedEngineSet([pool.engine])) for v in (loads, before))
                pool.wait_ge(ones_done, 1)
                pool.wait_ge(raw_in[j], loads)
                if not (isinstance(t, int) and t < 2):
                    pool.wait_ge(mm_done, before)
                nc.gpsimd.tensor_scalar(w_hi[j % 2][:, 0:k, :], raw[j][:, 0:k, :], 1.0, None, ALU.mult
                                        ).then_inc(w_hi_done, 1)
                pool.wait_ge(w_hi_done, t + 1)
                nc.gpsimd.tensor_tensor(w_lo[j % 2][:, 0:k, :], raw[j][:, 0:k, :], w_hi[j % 2][:, 0:k, :].bitcast(F32),
                                        ALU.subtract).then_inc(w_split, 1)

            for j in range(4):
                split(j, j, 0, KD)
            last = PARTS[2][1]
            d0, d1 = T_E - 8, T_END - 8
            for lo_, hi_, k in ((4, d0, KD), (d0, T_E, last), (T_E, d1, KD), (d1, T_END, last)):
                with pool.Fori(lo_ // 4, hi_ // 4) as i:
                    for j in range(4):
                        split(j, 4 * i + j, i, k)

        @block.tensor
        def _(pe):
            mm, tr = nc.tensor.matmul, nc.tensor.transpose

            def steps(t, slot, aslot, x_hi, x_lo, ks, k_of=lambda k: k, first=True, last=True, n=KD, ready=None):
                out = acc(aslot)
                for k in ks:
                    if ready is not None:
                        ready(k)
                    for i, (w, x) in enumerate(((w_hi, x_hi), (w_hi, x_lo), (w_lo, x_hi))):
                        for cols in HALVES:
                            ins = mm(out[:, cols], w[slot][:, k, :], x[:, k_of(k), cols],
                                     start=first and k == 0 and i == 0, stop=last and k == n - 1 and i == 2)
                return ins

            def begin(t, a_):
                pe.wait_ge(w_split, t + 1)
                if isinstance(a_, int):
                    if a_ >= 2:
                        pe.wait_ge(*acc_free(a_ - 2))

            def h_wait(n):
                return lambda k: pe.wait_ge(h_ready, 8 * n + k + 1)

            def ada_step(s):
                buf = ada0[s % 5] if isinstance(s, int) and s < 8 else ada1
                if isinstance(s, int) and s < 8:
                    pe.wait_ge(ada0_in[s % 5], 16 * (s // 5 + 1))
                else:
                    pe.wait_ge(ada1_in, 16 * (s - 7))
                if not (isinstance(s, int) and s == 0):
                    pe.wait_ge(mod_done, s)
                for j in range(2):
                    for k in range(KD):
                        ins = mm(bank(6, 2, 2 * j), buf[:, k, j * P:(j + 1) * P], svec[:, k, :], start=k == 0,
                                 stop=k == KD - 1)
                ins.then_inc(ada_mm, 1)

            def ss(n, m, buf):
                pe.wait_ge(sq_ready, 8 * n + m + 1)
                for c in range(CHUNKS):
                    ins = mm(bank(7, 1, c), buf[:, chunk_col(c):chunk_col(c) + P], ones[:, 0:1],
                             start=isinstance(m, int) and m == 0 and c == 0,
                             stop=isinstance(m, int) and m == 7 and c == CHUNKS - 1, skip_group_check=True)
                ins.then_inc(ss_done, 1)

            def rb(src, pair=4):
                mm(bank(pair, P), ones[:, :], src[:, 0, :], start=True, stop=True)
                return mm(bank(pair + 1), ones[:, :], src[:, 1:CHUNKS, :], start=True, stop=True)

            def norm_rb(n):
                pe.wait_ge(diag_done, n + 1)
                rb(diag).then_inc(rb_done, 1)

            pe.wait_ge(consts_in, 16)
            pe.wait_ge(par_dma, 16 * N_PAR_DMA)
            for i in range(PARAM_TILES):
                m = min(P, N_PARAM - i * P)
                ins = tr(bank(4, m, i * P) if i < 4 else bank(5, m), par_in[0:m, i, :], ident[0:m, 0:m])
            ins.then_inc(par_ps, 1)
            pe.wait_ge(svec_done, 1)
            ada_step(0)
            pe.wait_ge(par_done, 1)
            pe.wait_ge(x_dma, 16 * CHUNKS)
            for k in range(KD):
                if k >= 2:
                    pe.wait_ge(xt_done, k - 1)
                b = 4 if k % 2 == 0 else 2
                for c in range(CHUNKS):
                    ins = tr(bank(b, P) if c == 0 else bank(b + 1, P, (c - 1) * P), x_in[:, c, k * P:(k + 1) * P],
                             ident)
                ins.then_inc(xt_ps, 1)
                if k >= 1:
                    ss(0, k - 1, sq[(k - 1) % 2])
            ss(0, 7, sq[1])
            for s in range(1, 8):
                ada_step(s)
            norm_rb(0)

            def att_begin(key):
                u = ATT_USE[key]
                if u >= 2:
                    who, n = ATT_END[u - 2]
                    pe.wait_ge(att_free_act if who == "act" else att_free_dve, n)
                else:
                    pe.wait_ge(mod_done, ADA_B)
                return 4 + 2 * (u % 2)

            for ev in ATT:
                kind = ev[0]
                if kind == "mm":
                    _, t, q = ev
                    if q == 0:
                        begin(t, t)
                    if t == 0 and q == 3:
                        pe.wait_ge(x_spilled, 16)
                    ins = steps(t, t % 2, t % 2, h_hi, h_lo, (2 * q, 2 * q + 1), ready=h_wait(0) if t == 0 else None)
                    if q == 3:
                        ins.then_inc(mm_done, 1)
                        if t < 3:
                            ada_step(ADA_A + t)
                    continue
                if kind == "S":
                    _, h, j = ev
                    if j == 0:
                        pe.wait_ge(q_roped, h + 1)
                        pe.wait_ge(k_roped, h + 1)
                        pe.wait_ge(*att_end(("trk", h)))
                    for c in range(2):
                        b = att_begin(ev + (c,))
                        if j == 0:
                            ins = mm(bank(b, P), qz[:, c, 0:P], kT[:, 0:P], start=True, stop=True)
                        else:
                            for half in range(2):
                                k0 = P + half * (KEYS // 2)
                                ins = mm(bank(b, KEYS // 2, 512 - KEYS // 2) if half == 0 else bank(b + 1, KEYS // 2),
                                         qz[:, c, j * P:(j + 1) * P], kT[:, k0:k0 + KEYS // 2], start=True, stop=True)
                        ins.then_inc(att_mm, 1)
                    continue
                b = att_begin(ev)
                if kind in ("rotq", "rotk"):
                    h = ev[1]
                    pe.wait_ge(acc_free_act, 3 * h + (1 if kind == "rotq" else 2))
                    src = q_raw if kind == "rotq" else k_raw
                    ins = mm(bank(b), perm, src[:, S0:S0 + NS], start=True, stop=True)
                elif kind == "trk":
                    h = ev[1]
                    if h == 0:
                        pe.wait_ge(ck_dma, 16)
                    tr(bank(b, P), k_raw[:, 0:P], ident)
                    ins = tr(bank(b, P, P), ck_in[:, h, :], ident)
                elif kind == "trv":
                    pe.wait_ge(acc_free_act, 3 * ev[1] + 3)
                    for c in range(CHUNKS):
                        ins = tr(bank(b, P, 3 * P) if c == 0 else bank(b + 1, P, (c - 1) * P),
                                 v_raw[:, chunk_col(c):chunk_col(c) + P], ident)
                elif kind == "T":
                    _, h, j = ev
                    pe.wait_ge(att_a, 5 * h + j + 1)
                    src = att[j % 2]
                    for c in range(CHUNKS if j else 1):
                        ins = tr(bank(b, P, 3 * P) if c == 0 else bank(b + 1, P, (c - 1) * P),
                                 src[:, c * P:(c + 1) * P], ident)
                elif kind == "PV":
                    _, h, j = ev
                    pe.wait_ge(*att_end(("T", h, j)))
                    pe.wait_ge(*att_end(("trv", h)))
                    if j == 1:
                        pe.wait_ge((cv_dma0, cv_dma1)[h % 2], 16 * (h // 2 + 1))
                    if j == 0:
                        ins = mm(bank(b, P), v_tok[h % 2][:, 0, :], attT[0][:, 0, :], start=True, stop=True)
                    else:
                        for c in range(CHUNKS):
                            ins = mm(bank(b, P), v_tok[h % 2][:, c + 1, :], attT[j % 2][:, c, :], start=c == 0,
                                     stop=c == CHUNKS - 1)
                elif kind == "ssO":
                    h = ev[1]
                    pe.wait_ge(o_sqd, h + 1)
                    for c in range(CHUNKS):
                        ins = mm(bank(b, 1, c), o_sq[:, chunk_col(c):chunk_col(c) + P], ones[:, 0:1], start=True,
                                 stop=True)
                elif kind == "rbO":
                    pe.wait_ge(o_dg, ev[1] + 1)
                    ins = rb(o_diag, b)
                elif kind == "pool":
                    g = ev[1]
                    pe.wait_ge(pmat_in, 16)
                    pe.wait_ge(pool_y, g + 1)
                    for half, cols in enumerate(HALVES):
                        ins = mm(bank(b, HALF, 512 - HALF) if half == 0 else bank(b + 1, W - HALF), pmat[:, g, :],
                                 pooled[:, cols], start=True, stop=True)
                ins.then_inc(att_mm, 1)

            def out_tile(m, slot, t, n, ready=None):
                begin(t, m + A_B if isinstance(m, int) else None)
                steps(t, slot, slot, g_hi, g_lo, range(KD), ready=ready).then_inc(mm_done, 1)

            def mix_wait(k):
                pe.wait_ge(g_ready, 8)

            for m in range(8):
                out_tile(m, m % 2, T_B + m, 1, mix_wait if m == 0 else None)
                ada_step(ADA_B + m)
                if m == 7:
                    ada_step(ADA_B + 8)
                if m:
                    ss(1, m - 1, sq[(m - 1) % 2])
            ss(1, 7, sq[1])
            norm_rb(1)

            def ffn(l, t0, a0):
                n_ = 2 * l + 1
                for p, (m0, n) in enumerate(PARTS):
                    tp, ap = t0 + 2 * m0 + 8 * p, a0 + 2 * m0 + 8 * p
                    ada0_s = ADA_F + (8 * p if p < 2 else 16)
                    per = (2 if p == 2 else 1) if l == 0 else 0

                    def pair(i, peeled):
                        for half in range(2):
                            t = tp + 2 * i + half
                            pe.wait_ge(w_split, t + 1)
                            pe.wait_ge(acc_free_dve, dve_accs(ap) + 2 * i + half - 2)
                            steps(t, half, half, h_hi, h_lo, range(KD),
                                  ready=h_wait(n_) if peeled and p == 0 and half == 0 else None
                                  ).then_inc(mm_done, 1)
                            if per == 2:
                                ada_step(ada0_s + 2 * i + half)
                        if per == 1:
                            ada_step(ada0_s + i)

                    pair(0, True)
                    with pe.Fori(1, n) as i:
                        pair(i, False)
                    td, ad = tp + 2 * n, ap + 2 * n

                    def down(i, peeled):
                        for half in range(2):
                            t = td + 2 * i + half
                            pe.wait_ge(w_split, t + 1)
                            pe.wait_ge(acc_free_dve, dve_accs(ad) + 2 * i + half - 2)
                            ready = (lambda k: pe.wait_ge(f_ready, FT * l + m0 + k + 1)) if peeled and half == 0 else None
                            steps(t, half, half, g_hi, g_lo, range(n), n=n, ready=ready).then_inc(mm_done, 1)
                            if p == 2 and not (peeled and half == 0):
                                ss(n_ + 1, 2 * i + half - 1, sq[(half + 1) % 2]) if peeled else \
                                    ss_later(n_ + 1, 2 * i + half - 1, sq[(half + 1) % 2])

                    down(0, True)
                    with pe.Fori(1, 4) as i:
                        down(i, False)
                ss_end(n_ + 1, 7, sq[1])

            def ss_later(n, m, buf, end=False):
                pe.wait_ge(sq_ready, m + (8 * n + 1))
                for c in range(CHUNKS):
                    ins = mm(bank(7, 1, c), buf[:, chunk_col(c):chunk_col(c) + P], ones[:, 0:1], start=False,
                             stop=end and c == CHUNKS - 1, skip_group_check=True)
                ins.then_inc(ss_done, 1)

            def ss_end(n, m, buf):
                ss_later(n, m, buf, True)

            ffn(0, T_F0, T_F0)
            norm_rb(2)

            for k in range(KD):
                pe.wait_ge(h_ready, 16 + k + 1)
            for c in range(CHUNKS):
                cols = slice(chunk_col(c), chunk_col(c) + P)
                for k in range(KD):
                    for i, (x, w) in enumerate(((h_hi, wdt_hi), (h_lo, wdt_hi), (h_hi, wdt_lo))):
                        ins = mm(bank(7, 64, 64 * c), x[:, k, cols], w[:, k, :], start=k == 0 and i == 0,
                                 stop=k == KD - 1 and i == 2)
            ins.then_inc(dt_mm, 1)

            def ssd_begin(key):
                u = SSD_USE[key]
                if u >= 4:
                    who, n = SSD_END[u - 4]
                    pe.wait_ge(ssd_free_act if who == "act" else ssd_free_dve, n)
                return 4 + u % 4

            for ev in SSD:
                kind = ev[0]
                if kind == "mm":
                    _, e, q = ev
                    t = T_E + e
                    if q == 0:
                        begin(t, t)
                    if e == 0 and q == 1:
                        pe.wait_ge(x_spilled, 32)
                    ins = steps(t, e % 2, e % 2, h_hi, h_lo, range(4 * q, 4 * q + 4))
                    if q == 1:
                        ins.then_inc(mm_done, 1)
                    if (e, q) == (0, 1):
                        pe.wait_ge(da_done, 1)
                        for c in range(CHUNKS):
                            for d_, m_ in enumerate((m_le, m_ge)):
                                mm(bank(4, 32, 64 * c + 32 * d_), m_, da3[:, c, 32 * d_:32 * d_ + 32], start=True,
                                   stop=True)
                        mm(bank(5, 320), ones[:, :], da, start=True, stop=True).then_inc(acs_mm, 1)
                    if (e, q) == (1, 0):
                        pe.wait_ge(acs_done, 1)
                        for c in range(CHUNKS):
                            ins = tr(ps[0:64, 512 * 6 + c * P:512 * 6 + (c + 1) * P] if c < 4 else
                                     ps[0:64, 512 * 7:512 * 7 + P], acs[:, c, :], ident)
                        ins.then_inc(acsT_ps, 1)
                        pe.wait_ge(acsT_done, 2)
                        pe.wait_ge(tot_w, 1)
                    continue
                g = ev[1]
                if kind == "trB":
                    pe.wait_ge(conv_silu, 6 * g + 1)
                    for i in range(2):
                        b = ssd_begin(ev + (i,))
                        for c in (range(1, CHUNKS) if i == 0 else (0,)):
                            ins = tr(bank(b, P, (c - 1) * P if i == 0 else 0),
                                     bT[g % 2][:, chunk_col(c):chunk_col(c) + P], ident)
                        ins.then_inc(ssd_mm, 1)
                elif kind == "trx":
                    j = ev[2]
                    pe.wait_ge(conv_silu, 6 * g + 3 + j)
                    for i in range(2):
                        b = ssd_begin(ev + (i,))
                        for c in (range(1, CHUNKS) if i == 0 else (0,)):
                            ins = tr(bank(b, P, (c - 1) * P if i == 0 else 0),
                                     cx[:, chunk_col(c):chunk_col(c) + P], ident)
                        ins.then_inc(ssd_mm, 1)
                elif kind == "init":
                    d_ = ev[2]
                    pe.wait_ge(st_in_dma, 32 * (g + 1))
                    b = ssd_begin(ev)
                    for q_ in range(4):
                        ins = tr(bank(b, P, q_ * P), st_in[:, d_, q_, :], ident)
                    ins.then_inc(ssd_mm, 1)
                elif kind in ("csb", "csf"):
                    pe.wait_ge(xw_done, CS_AT[ev] + 1)
                    pe.wait_ge(*ssd_end(("trB", g, 1)))
                    b = ssd_begin(ev)
                    mm(bank(b), b_tok[g % 2][:, ev[2], :], xw[CS_AT[ev] % 2][:, :], start=True, stop=True
                       ).then_inc(ssd_mm, 1)
                elif kind == "cb":
                    pe.wait_ge(conv_silu, 6 * g + 2)
                    b = ssd_begin(ev)
                    cols = slice(chunk_col(ev[2]), chunk_col(ev[2]) + P)
                    mm(bank(b, P), bT[g % 2][:, cols], cT[g % 2][:, cols], start=True, stop=True
                       ).then_inc(ssd_mm, 1)
                elif kind == "yd":
                    b = ssd_begin(ev)
                    for d_ in range(2):
                        pe.wait_ge(W_done, 2 * (CHUNKS * g + ev[2]) + d_ + 1)
                        for r in range(GH):
                            ins = mm(bank(b, HD, r * HD), R[:, d_, r, :], xdt[:, d_, r * HD:(r + 1) * HD],
                                     start=(d_, r) == (0, 0), stop=(d_, r) == (1, GH - 1), skip_group_check=True)
                        ins.then_inc((R_used, ssd_mm)[d_], 1)
                elif kind == "yo":
                    c = ev[2]
                    pe.wait_ge(*ssd_end(("init", g, 1)))
                    pe.wait_ge(st_done, CS_AT[("csb", g, 0) if c < 2 else ("csf", g, c - 1)] + 1)
                    cols = slice(chunk_col(c), chunk_col(c) + P)
                    for d_ in range(2):
                        b = ssd_begin(ev + (d_,))
                        src = st_f[c % 2][:, :] if d_ == 0 else st_b[:, c - 1, :]
                        mm(bank(b), cT[g % 2][:, cols], src, start=True, stop=True).then_inc(ssd_mm, 1)
                elif kind == "yT":
                    pe.wait_ge(y_done, 5 * g + ev[2] + 1)
                    b = ssd_begin(ev)
                    for q_ in range(4):
                        ins = tr(bank(b, P, q_ * P), y1[ev[2] % 2][:, q_ * P:(q_ + 1) * P], ident)
                    ins.then_inc(ssd_mm, 1)
                elif kind == "stT":
                    pe.wait_ge(st_done, CS_AT[("csf", g, 0)] + 1)
                    for d_ in range(2):
                        b = ssd_begin(ev + (d_,))
                        for q_ in range(4):
                            ins = tr(bank(b, P, q_ * P), st_p[:, d_, q_ * P:(q_ + 1) * P], ident)
                        ins.then_inc(ssd_mm, 1)

            def so_acc(i, half, peeled):
                a_ = 2 * i + half
                for part in range(2):
                    t = T_O + 2 * a_ + part
                    pe.wait_ge(w_split, t + 1)
                    if part == 0:
                        if peeled:
                            pe.wait_ge(*acc_free(A_O + a_ - 2))
                        else:
                            pe.wait_ge(acc_free_dve, a_ + (dve_accs(A_O) - 2))
                    out = acc(half)
                    for k in range(KD):
                        kk = 8 * part + k
                        if peeled and half == 0:
                            pe.wait_ge(y_ready, kk + 1)
                        for i_, (w, x) in enumerate(((w_hi, y_hi), (w_hi, y_lo), (w_lo, y_hi))):
                            for cols in HALVES:
                                ins = mm(out[:, cols], w[part][:, k, :], x[:, kk, cols], start=kk == 0 and i_ == 0,
                                         stop=kk == 15 and i_ == 2)
                        if k == KD - 1:
                            ins.then_inc(mm_done, 1)
                        if peeled and half == 0:
                            y_sum(kk)

            def y_sum(k):
                pe.wait_ge(y_sqd, k + 1)
                for c in range(CHUNKS):
                    ins = mm(bank(6, 1, c), sq[k % 2][:, chunk_col(c):chunk_col(c) + P], ones[:, 0:1],
                             start=k == 0 and c == 0, stop=k == 15 and c == 4, skip_group_check=True)
                ins.then_inc(y_ss, 1)

            def y_rb():
                pe.wait_ge(yr_dg, 1)
                rb(diag).then_inc(yr_rb, 1)

            def so_body(i, peeled):
                for half in range(2):
                    so_acc(i, half, peeled)
                    if peeled and half == 0:
                        y_rb()
                    elif peeled:
                        ss(3, 0, sq[0])
                    elif half == 0:
                        ss_later(3, 2 * i - 1, sq[1])
                    else:
                        ss_later(3, 2 * i, sq[0])

            so_body(0, True)
            with pe.Fori(1, 4) as i:
                so_body(i, False)
            ss_end(3, 7, sq[1])
            norm_rb(3)
            ffn(1, T_F1, A_F1)

            for c in range(CHUNKS):
                if c >= 2:
                    pe.wait_ge(fin_y, c - 1)
                b = 4 if c % 2 == 0 else 2
                for k in range(KD):
                    ins = tr(bank(b + k // 4, P, (k % 4) * P), xT[:, k, chunk_col(c):chunk_col(c) + P], ident)
                ins.then_inc(fin_ps, 1)

        @block.scalar
        def _(act):
            A_ = nc.scalar.activation
            step = Steps(act, act_step)
            SCALE = HD ** -0.5

            act.wait_ge(par_done, 1)
            for s_, name in enumerate(("c_ctx", "c")):
                ins = A_(svec[:, :, s_], par[:, PARAM_AT[name]:PARAM_AT[name] + KD], ACT.Silu)
            ins.then_inc(svec_done, 1)
            act.wait_ge(memset_done, 1)
            act.wait_ge(ones_done, 1)
            for k in range(KD):
                act.wait_ge(xt_ps, k + 1)
                b = 4 if k % 2 == 0 else 2
                A_(xT[:, k, 0:NP_], bank(b, P), ACT.Copy)
                A_(xT[:, k, S0:S0 + NS], bank(b + 1), ACT.Copy).then_inc(xt_done, 1)
                act.wait_ge(xt_done, k + 1)
                if k >= 2:
                    act.wait_ge(ss_done, k - 1)
                A_(sq[k % 2][:, :], xT[:, k, :], ACT.Square).then_inc(sq_ready, 1)

            def norm(n):
                act.wait_ge(ms_done, n + 1)
                A_(small[:, 8:13], small[:, 0:5], ACT.Sqrt).then_inc(root_done, 1)
                l, j = n // 2, 3 * (n % 2)
                for k in range(KD):
                    act.wait_ge(t_done, 8 * n + k + 1)
                    for s_, cols in enumerate((slice(0, NP_), slice(S0, S0 + NS))):
                        ins = A_(h_hi[:, k, cols], tn[k % 2][:, cols], ACT.Identity, bias=modc(l, j, k, s_))
                    ins.then_inc(h_hi_done, 1)

            act.wait_ge(wdt_in, 16)
            A_(wdt_hi[:, :, :], wdt[:, :, :], ACT.Copy).then_inc(wdt_hi_done, 1)
            norm(0)
            act.wait_ge(bcast_in, 64)
            A_(a_bc[:, :], a_bc[:, :], ACT.Exp).then_inc(abc_done, 1)
            act.wait_ge(lam_s, 1)
            A_(small[:, 18:20], small[:, 16:18], ACT.Exp).then_inc(lam_e, 1)

            def att_wait(key):
                act.wait_ge(att_mm, ATT_USE[key] + 1)
                return 4 + 2 * (ATT_USE[key] % 2)

            for ev in ATT:
                kind = ev[0]
                if kind == "mm":
                    _, t, q = ev
                    if q == 3 and t < 12:
                        h, i = divmod(t, 3)
                        act.wait_ge(mm_done, t + 1)
                        if h:
                            if i == 0:
                                act.wait_ge(q_roped, h)
                            elif i == 1:
                                act.wait_ge(k_roped, h)
                                act.wait_ge(*att_end(("trk", h - 1)))
                            else:
                                act.wait_ge(*att_end(("trv", h - 1)))
                        A_((q_raw, k_raw, v_raw)[i][:, :], acc(t % 2), ACT.Copy).then_inc(acc_free_act, 1)
                    continue
                if kind == "trk":
                    h = ev[1]
                    b = att_wait(ev)
                    if h:
                        act.wait_ge(k_stored, 16 * h)
                    A_(kT[:, NP_ + NS:], bank(b, P, P), ACT.Copy)
                    A_(k_out[:, :], bank(b, P), ACT.Copy).then_inc(att_free_act, 1)
                elif kind == "trv":
                    h = ev[1]
                    b = att_wait(ev)
                    if h >= 2:
                        act.wait_ge(v_stored, 16 * (h - 1))
                    A_(v_tok[h % 2][:, 0:CHUNKS, :], bank(b, CHUNKS * P, 3 * P), ACT.Copy).then_inc(att_free_act, 1)
                elif kind == "S":
                    _, h, j = ev
                    n = 5 * h + j
                    for c in range(2):
                        b = att_wait(ev + (c,))
                        act.wait_ge(smax, 2 * n + c + 1)
                        if n >= 2:
                            act.wait_ge(att_a, n - 1)
                        src = bank(b, P) if j == 0 else bank(b, KEYS, 512 - KEYS // 2)
                        i = 24 + 2 * (j % 2) + c
                        A_(prob[j % 2][:, c, 0:P if j == 0 else KEYS], src, ACT.Exp, bias=small[:, i:i + 1],
                           scale=SCALE, accum_out=small[:, i + 4:i + 5]).then_inc(att_free_act, 1)
                elif kind == "T":
                    _, h, j = ev
                    b = att_wait(ev)
                    n = CHUNKS if j else 1
                    A_(attT[j % 2][:, 0:n, :], bank(b, n * P, 3 * P), ACT.Copy).then_inc(att_free_act, 1)
                elif kind == "PV":
                    _, h, j = ev
                    b = att_wait(ev)
                    if j == 0 and h:
                        act.wait_ge(*att_end(("rbO", h - 1)))
                    col = chunk_col(j)
                    A_(o_sb[:, col:col + P], bank(b, P), ACT.Copy).then_inc(att_free_act, 1)
                    if j == 4:
                        act.wait_ge(*att_end(ev))
                        A_(o_sq[:, 0:NP_], o_sb[:, 0:NP_], ACT.Square)
                        A_(o_sq[:, S0:S0 + NS], o_sb[:, S0:S0 + NS], ACT.Square).then_inc(o_sqd, 1)
                elif kind == "ssO":
                    act.wait_ge(*att_end(ev))
                    A_(small[:, 40:45], small[:, 32:37], ACT.Sqrt).then_inc(o_root, 1)
                elif kind == "rbO":
                    h = ev[1]
                    act.wait_ge(*att_end(ev))
                    A_(g_hi[:, h, :], o_nrm[:, :], ACT.Copy).then_inc(o_hi, 1)
                elif kind == "pool":
                    g = ev[1]
                    act.wait_ge(*att_end(ev))
                    A_(g_hi[:, 4 + g, :], pmul[:, :], ACT.Copy).then_inc(pool_hi, 1)

            def square(n, m, free, buf):
                act.wait_ge(*free)
                act.wait_ge(ss_done, m + (8 * n - 1))
                A_(buf[:, :], xT_at(m), ACT.Square).then_inc(sq_ready, 1)

            def xT_at(m):
                return xT[:, m, :] if isinstance(m, int) else xT[:, bass.ds(m, 1), :]

            act.wait_ge(x_back, 16)
            for m in range(8):
                square(1, m, (acc_free_dve, dve_accs(A_B + m)), sq[m % 2])
            norm(1)

            def taps_of(name, row):
                return par[:, bass.ds(row, 1)] if not isinstance(row, int) else par[:, row:row + 1]

            def ffn(l, t0, a0):
                wc, bcol = PARAM_AT["ffn_conv_w"] + l * 132, PARAM_AT["ffn_conv_b"] + l * 44
                n_ = 2 * l + 1
                for p, (m0, n) in enumerate(PARTS):
                    tp, ap = t0 + 2 * m0 + 8 * p, a0 + 2 * m0 + 8 * p
                    f0 = FT * l + m0

                    def pair(i):
                        for half, buf in enumerate((cg, cv)):
                            act.wait_ge(mm_done, 2 * i + (tp + half + 1))
                            m = i + (m0 + FT * half)
                            if half == 0:
                                if isinstance(i, int) and f0 == 0:
                                    pass
                                else:
                                    act.wait_ge(ffn_silu, i + f0)
                            elif not (isinstance(i, int) and f0 == 0):
                                act.wait_ge(hm_done, i + f0)
                            A_(buf[:, :], acc(half), ACT.Identity, bias=taps_of("", m + bcol),
                               scale=taps_of("", m + (wc + 44))).then_inc(ffn_id, 1)
                        act.wait_ge(acc_free_dve, 2 * i + dve_accs(ap))
                        A_(sg[:, :], cg[:, :], ACT.Silu).then_inc(ffn_silu, 1)
                        act.wait_ge(hm_done, i + (f0 + 1))
                        dst = g_hi[:, i, :] if isinstance(i, int) else g_hi[:, bass.ds(i, 1), :]
                        A_(dst, hm[:, :], ACT.Copy).then_inc(ffn_hi, 1)

                    pair(0)
                    with act.Fori(1, n) as i:
                        pair(i)
                    if p == 2:
                        ad = ap + 2 * n

                        def down(i):
                            for half in range(2):
                                square(n_ + 1, 2 * i + half, (acc_free_dve, 2 * i + (dve_accs(ad) + half)), sq[half])

                        down(0)
                        with act.Fori(1, 4) as i:
                            down(i)

            ffn(0, T_F0, T_F0)
            norm(2)

            act.wait_ge(x_spilled, 32)
            act.wait_ge(dt_xb, 1)
            A_(dt_e, dt_x, ACT.Abs).then_inc(act_step, 1)
            step.n += 1
            step.wait()
            A_(dt_e, dt_e, ACT.Exp, scale=-1.0).then_inc(dt_exp, 1)
            act.wait_ge(tot_w, 1)
            A_(eacs[:, :, :], acs[:, :, :], ACT.Exp)
            A_(dec[:, :, :], dec[:, :, :], ACT.Exp)
            A_(wst[:, :, :], wst[:, :, :], ACT.Exp).then_inc(acs_exp, 1)
            act.wait_ge(acsT_ps, 1)
            A_(acsT[:, 0:512], ps[0:64, 512 * 6:512 * 7], ACT.Copy).then_inc(acsT_done, 1)
            A_(acsT[:, 512:640], ps[0:64, 512 * 7:512 * 7 + P], ACT.Copy).then_inc(acsT_done, 1)

            def ssd_wait(key):
                act.wait_ge(ssd_mm, SSD_USE[key] + 1)
                return 4 + SSD_USE[key] % 4

            def conv_row(name, i):
                return par[:, PARAM_AT[name] + i:PARAM_AT[name] + i + 1]

            def conv_buf(e):
                g, i = divmod(e, 10)
                return bT[g % 2] if i == 0 else cT[g % 2] if i == 1 else cx

            for ev in SSD:
                kind = ev[0]
                if kind == "mm":
                    _, e, q = ev
                    if q == 0:
                        continue
                    what, m = ssd_tile(e)
                    g, i = divmod(e, 10)
                    act.wait_ge(mm_done, T_E + e + 1)
                    if what == "z":
                        A_(yg[:, m, :], acc(e % 2), ACT.Silu).then_inc(acc_free_act, 1)
                        continue
                    if i < 2 and g >= 2:
                        act.wait_ge(y_done, 5 * (g - 1))
                    if i == 2 and g:
                        act.wait_ge(*ssd_end(("trx", g - 1, 3, 1)))
                    if i > 2:
                        act.wait_ge(*ssd_end(("trx", g, i - 3, 1)))
                    buf = conv_buf(e)
                    A_(buf[:, :], acc(e % 2), ACT.Identity, bias=conv_row("ssd_conv_b", m),
                       scale=conv_row("ssd_conv_w", 24 + m)).then_inc(conv_id, 1)
                    act.wait_ge(acc_free_dve, dve_accs(A_E + e))
                    A_(buf[:, :], buf[:, :], ACT.Silu).then_inc(conv_silu, 1)
                    continue
                g = ev[1]
                if kind in ("trB", "trx"):
                    for i in range(2):
                        b = ssd_wait(ev + (i,))
                        cs = slice(1, CHUNKS) if i == 0 else slice(0, 1)
                        dst = b_tok[g % 2][:, cs, :] if kind == "trB" else \
                            x_tok[g % 2][:, cs, ev[2] * P:(ev[2] + 1) * P]
                        if g >= 2 and i == 0 and (kind == "trB" or ev[2] == 0):
                            act.wait_ge(y_done, 5 * (g - 1))
                            act.wait_ge(st_done, CS_AT[("csf", g - 2, 3)] + 1)
                        A_(dst, bank(b, P * (4 if i == 0 else 1)).rearrange("p (c n) -> p c n", n=P), ACT.Copy
                           ).then_inc(ssd_free_act, 1)
                elif kind == "init":
                    d_ = ev[2]
                    b = ssd_wait(ev)
                    if g:
                        act.wait_ge(ssd_mm, SSD_USE[("yo", g - 1, 4, 1)] + 1)
                    A_(st_f[1][:, :] if d_ == 0 else st_b[:, 3, :], bank(b), ACT.Copy).then_inc(ssd_free_act, 1)
                elif kind == "cb":
                    n = 5 * g + ev[2]
                    c = ev[2]
                    for d_ in range(2):
                        act.wait_ge(R_in[d_], 16 * (n + 1))
                        for r in range(GH):
                            i = 32 * d_ + GH * g + r
                            ins = A_(R[:, d_, r, :], R[:, d_, r, :], ACT.Relu, bias=acs[:, c, i:i + 1], scale=-1.0)
                        step(ins)
                        step.wait()
                        A_(R[:, d_, :, :], R[:, d_, :, :], ACT.Exp, scale=-1.0).then_inc(seg_exp, 1)
                elif kind == "stT":
                    for d_ in range(2):
                        b = ssd_wait(ev + (d_,))
                        if g or d_:
                            act.wait_ge(st_stored, 16 * (2 * g + d_))
                        A_(st_out[:, :, :], bank(b).rearrange("p (q n) -> p q n", q=4), ACT.Copy
                           ).then_inc(ssd_free_act, 1)

            act.wait_ge(mm_done, T_E + 40)
            for k in range(16):
                act.wait_ge(*ssd_end(("yT", k // 4, 4)))
                A_(y_hi[:, k, :], yg[:, k, :], ACT.Copy, scale=pcol("ssd_norm_g", k)).then_inc(yn_hi, 1)
                if k == 0:
                    act.wait_ge(x_back, 32)
                if k >= 2:
                    act.wait_ge(y_ss, k - 1)
                A_(sq[k % 2][:, :], yg[:, k, :], ACT.Square).then_inc(y_sqd, 1)
            act.wait_ge(yr_ms, 1)
            A_(small[:, 8:13], small[:, 0:5], ACT.Sqrt).then_inc(yr_root, 1)

            def so_squares(i):
                for half in range(2):
                    square(3, 2 * i + half, (so_x, 2 * i + (half + 1)), sq[half])

            so_squares(0)
            with act.Fori(1, 4) as i:
                so_squares(i)
            norm(3)
            ffn(1, T_F1, A_F1)
            act.wait_ge(ms_done, 5)
            A_(small[:, 8:13], small[:, 0:5], ACT.Sqrt).then_inc(root_done, 1)

        @block.vector
        def _(dve):
            tt, ts, stt, cp = nc.vector.tensor_tensor, nc.vector.tensor_scalar, nc.vector.scalar_tensor_tensor, \
                nc.vector.tensor_copy
            step = Steps(dve, dve_step)
            RANGES = ((0, slice(0, NP_)), (1, slice(S0, S0 + NS)))
            f32 = lambda ap: ap.bitcast(F32)

            step(nc.vector.memset(xT[:, :, NP_:S0], 0.0))
            step(nc.vector.memset(xT[:, :, W - 1:W], 0.0))

            def h_zeros():
                for t_ in (h_hi, h_lo):
                    step(nc.vector.memset(t_[:, :, NP_:S0].bitcast(F32), 0.0))
                    step(nc.vector.memset(t_[:, :, W - 1:W].bitcast(F32), 0.0))
                step.wait()

            h_zeros()
            nc.vector.memset(small[:, 63:64], 0.0).then_inc(memset_done, 1)
            dve.wait_ge(par_ps, 1)
            step(cp(par[:, 0:512], bank(4)))
            step.wait()
            cp(par[:, 512:N_PARAM], bank(5, N_PARAM - 512)).then_inc(par_done, 1)

            def mod_evac(s):
                dve.wait_ge(ada_mm, s + 1)
                if isinstance(s, int):
                    dst, bias = mod[:, 2 * s:2 * s + 2, :], par[:, PARAM_AT["ada_b"] + 2 * s:PARAM_AT["ada_b"] + 2 * s + 2]
                else:
                    dst, bias = mod[:, bass.ds(2 * s, 2), :], par[:, bass.ds(2 * s + PARAM_AT["ada_b"], 2)]
                tt(dst, bank(6, 4).rearrange("p (a b) -> p a b", b=2), bc(bias, 2, 2), ALU.add).then_inc(mod_done, 1)

            def gains(n, after):
                dve.wait_ge(mod_done, after)
                l, j = n // 2, 1 + 3 * (n % 2)
                name = "norm_mix_g" if n % 2 == 0 else "norm_ffn_g"
                g0 = PARAM_AT[name] + 8 * l
                step(stt(gain1[:, n, :, :], mod[:, l * 48 + j * 8:l * 48 + j * 8 + 8, :], 1.0,
                         bc(par[:, g0:g0 + 8], 2, 2), ALU.add, ALU.mult))

            def inv_root(n):
                dve.wait_ge(ss_done, 8 * n + 8)
                ts(small[:, 0:5], bank(7, 5), 1.0 / D, EPS, ALU.mult, ALU.add).then_inc(ms_done, 1)
                dve.wait_ge(root_done, n + 1)
                step(nc.vector.reciprocal(small[:, 48:53], small[:, 8:13]))
                step.wait()

            def norm(n):
                inv_root(n)
                tt(diag[:, :, :], bc(ident, 1, CHUNKS), bc(small[:, 48:53], 2, P), ALU.mult).then_inc(diag_done, 1)
                dve.wait_ge(rb_done, n + 1)
                l, j = n // 2, 3 * (n % 2)

                def low(k):
                    dve.wait_ge(h_hi_done, 8 * n + k + 1)
                    for s_, cols in RANGES:
                        ins = stt(h_lo[:, k, cols], tn[k % 2][:, cols], modc(l, j, k, s_), f32(h_hi[:, k, cols]),
                                  ALU.add, ALU.subtract)
                        (step(ins) if s_ == 0 else ins.then_inc(h_ready, 1))

                for k in range(KD):
                    if k >= 2:
                        dve.wait_ge(h_ready, 8 * n + k - 1)
                    for s_, cols in RANGES:
                        rbp = bank(4, P) if s_ == 0 else bank(5)
                        ins = stt(tn[k % 2][:, cols], xT[:, k, cols], gain1[:, n, k, s_:s_ + 1], rbp, ALU.mult,
                                  ALU.mult)
                        (step(ins) if s_ == 0 else ins.then_inc(t_done, 1))
                    if k:
                        low(k - 1)
                low(KD - 1)

            mod_evac(0)
            dve.wait_ge(wdt_hi_done, 1)
            step(tt(wdt_lo[:, :, :], wdt[:, :, :], f32(wdt_hi[:, :, :]), ALU.subtract))
            dve.wait_ge(bcast_in, 64)
            step(tt(lam_in[:, 0, :], lam_in[:, 0, :], lam_in[:, 1, :], ALU.mult))
            step(tt(lam_in[:, 2, :], lam_in[:, 2, :], lam_in[:, 3, :], ALU.mult))
            step.wait()
            step(nc.vector.tensor_reduce(small[:, 16:17], lam_in[:, 0, :], AXX, ALU.add))
            nc.vector.tensor_reduce(small[:, 17:18], lam_in[:, 2, :], AXX, ALU.add).then_inc(lam_s, 1)
            for s in range(1, 8):
                mod_evac(s)
            gains(0, 8)
            step(ts(small[:, 22:23], pcol("att_subln_g"), 1.0 - LAM_INIT, None, ALU.mult))
            step.wait()
            norm(0)
            dve.wait_ge(abc_done, 1)
            step(ts(a_bc[:, :], a_bc[:, :], -1.0, None, ALU.mult))
            dve.wait_ge(lam_e, 1)
            step(tt(small[:, 20:21], small[:, 19:20], small[:, 18:19], ALU.subtract))
            step.wait()
            step(ts(small[:, 21:22], small[:, 20:21], -LAM_INIT, None, ALU.add))
            step.wait()

            dve.wait_ge(x_spilled, 16)
            for t_ in (pb[0], pb[1], pb[2]):
                step(nc.vector.memset(t_[:, :], 0.0))
            step(nc.vector.memset(qz[0:64, 1, :], 0.0))
            step(nc.vector.memset(qz[64:128, 0, :], 0.0))
            for t_ in (pooled, o_nrm):
                step(nc.vector.memset(t_[:, NP_:S0], 0.0))
                step(nc.vector.memset(t_[:, W - 1:W], 0.0))
            step.wait()

            def att_wait(key):
                dve.wait_ge(att_mm, ATT_USE[key] + 1)
                return 4 + 2 * (ATT_USE[key] % 2)

            t_before = {}
            for ev in ATT:
                kind = ev[0]
                if kind == "mm":
                    _, t, q = ev
                    if q != 3:
                        continue
                    if t < 3:
                        mod_evac(ADA_A + t)
                    if t >= 12:
                        g = t - 12
                        dve.wait_ge(mm_done, t + 1)
                        src = acc(t % 2)
                        if g:
                            step.wait()
                        step(cp(pb[0][:, 8:8 + NP_], src[:, 0:NP_]))
                        cp(pb[0][:, 152:152 + NS], src[:, S0:S0 + NS]).then_inc(acc_free_dve, 1)
                        dve.wait_ge(acc_free_dve, dve_accs(t))
                        s_, lo_ = pb[0], 0
                        for d_ in range(g + 1):
                            r = 1 << d_ >> 1
                            nlo = lo_ + max(r, 1)
                            nhi = 672 - (0 if d_ == 0 else nlo - 1)
                            dst = pb[1 + d_ % 2]
                            a0_, b0_ = (-1, 0) if d_ == 0 else (-r, r)
                            step(tt(dst[:, nlo:nhi], s_[:, nlo + a0_:nhi + a0_], s_[:, nlo + b0_:nhi + b0_], ALU.add))
                            step.wait()
                            s_, lo_ = dst, nlo
                        dve.wait_ge(inv_in, 16 * (g + 1))
                        if g:
                            dve.wait_ge(att_mm, ATT_USE[("pool", g - 1)] + 1)
                        step(tt(pooled[:, 0:NP_], s_[:, 8:8 + NP_], inv_n[:, 0:NP_], ALU.mult))
                        step(tt(pooled[:, S0:S0 + NS], s_[:, 152:152 + NS], inv_n[:, NP_:], ALU.mult))
                        step.wait()
                        step(tt(pooled[:, 0:NP_], pooled[:, 0:NP_], pb[0][:, 8:8 + NP_], ALU.subtract))
                        tt(pooled[:, S0:S0 + NS], pooled[:, S0:S0 + NS], pb[0][:, 152:152 + NS], ALU.subtract
                           ).then_inc(pool_y, 1)
                        dve.wait_ge(pool_y, g + 1)
                    continue
                if kind in ("rotq", "rotk"):
                    h = ev[1]
                    b = att_wait(ev)
                    if h == 0:
                        dve.wait_ge(rope_in, 16)
                    src = q_raw if kind == "rotq" else k_raw
                    sam = src[:, S0:S0 + NS]
                    step.wait()
                    tt(rtmp, bank(b), rope[:, 1, :], ALU.mult).then_inc(att_free_dve, 1)
                    step(tt(sam, sam, rope[:, 0, :], ALU.mult))
                    if kind == "rotq":
                        step(cp(qz[0:64, 0, 0:P], src[0:64, 0:P]))
                        step(cp(qz[64:128, 1, 0:P], src[64:128, 0:P]))
                        step.wait()
                        step(tt(qz[0:64, 0, P:], sam[0:64, :], rtmp[0:64, :], ALU.add))
                        step(tt(qz[64:128, 1, P:], sam[64:128, :], rtmp[64:128, :], ALU.add))
                        step.wait()
                        nc.vector.memset(small[:, 62:63], 0.0).then_inc(q_roped, 1)
                    else:
                        dve.wait_ge(att_mm, ATT_USE[("trk", h)] + 1)
                        step(cp(kT[:, 0:P], src[:, 0:P]))
                        step.wait()
                        step(tt(kT[:, P:P + NS], sam, rtmp, ALU.add))
                        step.wait()
                        nc.vector.memset(small[:, 61:62], 0.0).then_inc(k_roped, 1)
                elif kind == "S":
                    _, h, j = ev
                    for c in range(2):
                        b = att_wait(ev + (c,))
                        src = bank(b, P) if j == 0 else bank(b, KEYS, 512 - KEYS // 2)
                        i = 24 + 2 * (j % 2) + c
                        step(nc.vector.tensor_reduce(small[:, 54 + c:55 + c], src, AXX, ALU.max))
                        step.wait()
                        ts(small[:, i:i + 1], small[:, 54 + c:55 + c], -HD ** -0.5, None, ALU.mult
                           ).then_inc(smax, 1)
                elif kind == "T":
                    _, h, j = ev
                    n = P if j == 0 else KEYS
                    i = 28 + 2 * (j % 2)
                    dve.wait_ge(*att_end(("S", h, j, 1)))
                    step(nc.vector.reciprocal(small[:, 56:58], small[:, i:i + 2]))
                    step.wait()
                    step(tt(small[:, 58:59], small[:, 57:58], small[:, 21:22], ALU.mult))
                    if j % 2 in t_before:
                        dve.wait_ge(att_mm, t_before[j % 2] + 1)
                    step(ts(att[j % 2][:, 0:n], prob[j % 2][:, 0, 0:n], small[:, 56:57], None, ALU.mult))
                    step.wait()
                    stt(att[j % 2][:, 0:n], prob[j % 2][:, 1, 0:n], small[:, 58:59], att[j % 2][:, 0:n], ALU.mult,
                        ALU.add).then_inc(att_a, 1)
                    dve.wait_ge(att_a, 5 * h + j + 1)
                    t_before[j % 2] = ATT_USE[ev]
                elif kind == "ssO":
                    h = ev[1]
                    b = att_wait(ev)
                    ts(small[:, 32:37], bank(b, 5), 1.0 / P, EPS, ALU.mult, ALU.add).then_inc(att_free_dve, 1)
                    dve.wait_ge(o_root, h + 1)
                    step(nc.vector.reciprocal(small[:, 45:50], small[:, 40:45]))
                    step.wait()
                    if h:
                        dve.wait_ge(att_mm, ATT_USE[("rbO", h - 1)] + 1)
                    tt(o_diag[:, :, :], bc(ident, 1, CHUNKS), bc(small[:, 45:50], 2, P), ALU.mult
                       ).then_inc(o_dg, 1)
                elif kind == "rbO":
                    h = ev[1]
                    b = att_wait(ev)
                    if h:
                        dve.wait_ge(g_ready, G_AT[("rbO", h - 1)])
                    for s_, cols in RANGES:
                        rbp = bank(b, P) if s_ == 0 else bank(b + 1)
                        ins = stt(o_nrm[:, cols], o_sb[:, cols], small[:, 22:23], rbp, ALU.mult, ALU.mult)
                        (step(ins) if s_ == 0 else ins.then_inc(att_free_dve, 1))
                    dve.wait_ge(o_hi, h + 1)
                    tt(g_lo[:, h, :], o_nrm[:, :], f32(g_hi[:, h, :]), ALU.subtract).then_inc(g_ready, 1)
                elif kind == "pool":
                    g = ev[1]
                    b = att_wait(ev)
                    if g:
                        dve.wait_ge(g_ready, G_AT[("pool", g - 1)])
                    ts(pmul[:, :], bank(b, W, 512 - HALF), pcol("pool_scale", g), None, ALU.mult
                       ).then_inc(att_free_dve, 1)
                    dve.wait_ge(pool_hi, g + 1)
                    tt(g_lo[:, 4 + g, :], pmul[:, :], f32(g_hi[:, 4 + g, :]), ALU.subtract).then_inc(g_ready, 1)

            def col(t_, m):
                return t_[:, m, :] if isinstance(m, int) else t_[:, bass.ds(m, 1), :]

            def residual(l, j, m, slot):
                for s_, cols in RANGES:
                    if isinstance(m, int):
                        x_, gate = xT[:, m, cols], modc(l, j, m, s_)
                    else:
                        x_ = xT[:, bass.ds(m, 1), cols]
                        gate = mod[:, bass.ds(m + (l * 48 + j * 8), 1), s_:s_ + 1]
                    ins = stt(x_, acc(slot)[:, cols], gate, x_, ALU.mult, ALU.add)
                    (step(ins) if s_ == 0 else ins.then_inc(acc_free_dve, 1))

            dve.wait_ge(x_back, 16)
            for m in range(8):
                dve.wait_ge(mm_done, T_B + m + 1)
                if m == 0:
                    mod_evac(ADA_B)
                residual(0, 2, m, m % 2)
                if m:
                    mod_evac(ADA_B + m)
            mod_evac(ADA_B + 8)
            gains(1, 20)
            norm(1)

            def ffn(l, t0, a0):
                wc = PARAM_AT["ffn_conv_w"] + l * 132
                n_ = 2 * l + 1
                for p, (m0, n) in enumerate(PARTS):
                    tp, ap = t0 + 2 * m0 + 8 * p, a0 + 2 * m0 + 8 * p
                    f0 = FT * l + m0
                    ada0_s = ADA_F + (8 * p if p < 2 else 16)
                    per = (2 if p == 2 else 1) if l == 0 else 0

                    def pcol_at(r):
                        return par[:, r:r + 1] if isinstance(r, int) else par[:, bass.ds(r, 1)]

                    def pair(i):
                        for half, buf in enumerate((cg, cv)):
                            m = i + (m0 + FT * half)
                            dve.wait_ge(ffn_id, 2 * i + (2 * f0 + half + 1))
                            src = acc(half)
                            step(stt(buf[:, 1:W], src[:, 0:W - 1], pcol_at(m + wc), buf[:, 1:W], ALU.mult, ALU.add))
                            step.wait()
                            stt(buf[:, 0:W - 1], src[:, 1:W], pcol_at(m + (wc + 88)), buf[:, 0:W - 1], ALU.mult,
                                ALU.add).then_inc(acc_free_dve, 1)
                            if per == 2:
                                mod_evac(2 * i + (ada0_s + half))
                        if per == 1:
                            mod_evac(i + ada0_s)
                        dve.wait_ge(ffn_silu, i + (f0 + 1))
                        if not (isinstance(i, int) and f0 == 0):
                            dve.wait_ge(f_ready, i + f0)
                        dve.wait_ge(acc_free_dve, 2 * i + (dve_accs(ap) + 1))
                        tt(hm[:, :], sg[:, :], cv[:, :], ALU.mult).then_inc(hm_done, 1)
                        dve.wait_ge(ffn_hi, i + (f0 + 1))
                        tt(col(g_lo, i), hm[:, :], f32(col(g_hi, i)), ALU.subtract).then_inc(f_ready, 1)

                    pair(0)
                    with dve.Fori(1, n) as i:
                        step.turn(i - 1, 2)
                        pair(i)
                    step.leave(n - 1)
                    td = tp + 2 * n

                    def down(i):
                        for half in range(2):
                            dve.wait_ge(mm_done, 2 * i + (td + half + 1))
                            residual(l, 5, 2 * i + half, half)

                    down(0)
                    with dve.Fori(1, 4) as i:
                        step.turn(i - 1, 2)
                        down(i)
                    step.leave(3)

            ffn(0, T_F0, T_F0)
            gains(2, 48)
            gains(3, 48)
            step.wait()
            norm(2)

            dve.wait_ge(x_spilled, 32)
            dve.wait_ge(dt_mm, 1)
            c64 = lambda ap: ap.rearrange("p (c x) -> p c x", c=CHUNKS)
            tt(c64(dt_x), c64(bank(7, 320)), bc(dtb_bc[:, :], 1, CHUNKS), ALU.add).then_inc(dt_xb, 1)
            dve.wait_ge(dt_exp, 1)

            def chain(ins):
                step(ins)
                step.wait()

            chain(ts(dt_s, dt_e, 2.0, None, ALU.add))
            chain(nc.vector.reciprocal(dt_z, dt_s))
            chain(tt(dt_s, dt_e, dt_z, ALU.mult))
            chain(tt(dt_z, dt_s, dt_s, ALU.mult))
            chain(ts(dt_p, dt_z, 1.0 / 17, 1.0 / 15, ALU.mult, ALU.add))
            for k in (13, 11, 9, 7, 5, 3, 1):
                chain(tt(dt_p, dt_p, dt_z, ALU.mult))
                chain(ts(dt_p, dt_p, 1.0 / k, None, ALU.add))
            chain(stt(dt_p, dt_p, 2.0, dt_s, ALU.mult, ALU.mult))
            chain(stt(dt[:, :, :], c64(dt_x), 0.0, c64(dt_p), ALU.max, ALU.add))
            tt(da3, dt[:, :, :], bc(a_bc[:, :], 1, CHUNKS), ALU.mult).then_inc(da_done, 1)
            dve.wait_ge(acs_mm, 1)
            cp(acs[:, :, :], c64(bank(4, 320))).then_inc(acs_done, 1)
            chain(cp(dec[:, :, :], c64(bank(5, 320))))
            dve.wait_ge(acs_done, 1)
            tt(wst[:, :, :], dec[:, :, :], acs[:, :, :], ALU.subtract).then_inc(tot_w, 1)
            dve.wait_ge(acs_exp, 1)
            step(tt(wst[:, :, :], wst[:, :, :], dt[:, :, :], ALU.mult))
            step.wait()
            nc.vector.memset(small[:, 60:61], 0.0).then_inc(da_read, 1)
            dve.wait_ge(acs_stored, 16)

            def ssd_wait(key):
                dve.wait_ge(ssd_mm, SSD_USE[key] + 1)
                return 4 + SSD_USE[key] % 4

            def per_head(t_, c, d_, g):
                return bc(t_[:, c, 32 * d_ + GH * g:32 * d_ + GH * (g + 1)], 2, HD)

            h64 = lambda ap: ap.rearrange("p (r x) -> p r x", x=HD)

            def weigh(ev):
                kind, g, c = ev
                i = CS_AT[ev]
                if i >= 2:
                    dve.wait_ge(ssd_mm, SSD_USE[CS_LIST[i - 2]] + 1)
                tt(h64(xw[i % 2][:, :]), h64(x_tok[g % 2][:, c, :]), per_head(wst, c, 0 if kind == "csf" else 1, g),
                   ALU.mult).then_inc(xw_done, 1)

            n_id = 0
            for ev in SSD:
                kind = ev[0]
                if kind == "mm":
                    _, e, q = ev
                    what, m = ssd_tile(e)
                    if q == 0 or what == "z":
                        continue
                    g, i = divmod(e, 10)
                    buf = bT[g % 2] if i == 0 else cT[g % 2] if i == 1 else cx
                    n_id += 1
                    dve.wait_ge(conv_id, n_id)
                    src = acc(e % 2)
                    row = PARAM_AT["ssd_conv_w"] + m
                    chain(stt(buf[:, 1:W], src[:, 0:W - 1], par[:, row:row + 1], buf[:, 1:W], ALU.mult, ALU.add))
                    stt(buf[:, 0:W - 1], src[:, 1:W], par[:, row + 48:row + 49], buf[:, 0:W - 1], ALU.mult, ALU.add
                        ).then_inc(acc_free_dve, 1)
                    continue
                g = ev[1]
                c = ev[2] if len(ev) > 2 else 0
                xt = x_tok[g % 2][:, c, :]
                if kind == "init" and c == 0:
                    dve.wait_ge(*ssd_end(("trx", g, 3, 1)))
                    weigh(("csb", g, 4))
                elif kind in ("csb", "csf"):
                    if kind == "csb" and c == 4:
                        dve.wait_ge(*ssd_end(("init", g, 1)))
                    d_ = 0 if kind == "csf" else 1
                    if CS_LIST.index(ev) + 1 < len(CS_LIST):
                        after = CS_LIST[CS_LIST.index(ev) + 1]
                        if after[1] == g:
                            weigh(after)
                    b = ssd_wait(ev)
                    if c == 0:
                        if g:
                            dve.wait_ge(ssd_mm, SSD_USE[("stT", g - 1, 1)] + 1)
                        cp(st_p[:, d_, :], bank(b)).then_inc(ssd_free_dve, 1)
                        dve.wait_ge(*ssd_end(ev))
                        nc.vector.memset(small[:, 60:61], 0.0).then_inc(st_done, 1)
                    else:
                        old = st_f[c % 2][:, :] if d_ == 0 else st_b[:, c - 1, :]
                        new = st_f[(c + 1) % 2][:, :] if d_ == 0 else st_b[:, c - 2, :]
                        chain(tt(h64(st_tmp[:, :]), h64(old), per_head(dec, c, d_, g), ALU.mult))
                        tt(new, st_tmp[:, :], bank(b), ALU.add).then_inc(ssd_free_dve, 1)
                        dve.wait_ge(*ssd_end(ev))
                        nc.vector.memset(small[:, 60:61], 0.0).then_inc(st_done, 1)
                elif kind == "cb":
                    n = 5 * g + c
                    b = ssd_wait(ev)
                    if n:
                        dve.wait_ge(W_done, 2 * n)
                    tt(cbm[:, :, :], bc(bank(b, P), 1, 2), masks, ALU.mult).then_inc(ssd_free_dve, 1)
                    if n:
                        dve.wait_ge(ssd_mm, SSD_USE[("yd", g, c - 1) if c else ("yd", g - 1, 4)] + 1)
                    for d_ in range(2):
                        step(tt(h64(xdt[:, d_, :]), h64(xt), per_head(dt, c, d_, g), ALU.mult))
                    dve.wait_ge(*ssd_end(ev))
                    step.wait()
                    for d_ in range(2):
                        dve.wait_ge(seg_exp, 2 * n + d_ + 1)
                        tt(R[:, d_, :, :], R[:, d_, :, :], bc(cbm[:, d_, :], 1, GH), ALU.mult).then_inc(W_done, 1)
                elif kind == "yd":
                    n = 5 * g + c
                    y_ = y1[c % 2][:, :]
                    if c >= 2:
                        dve.wait_ge(ssd_mm, SSD_USE[("yT", g, c - 2)] + 1)
                    elif g:
                        dve.wait_ge(ssd_mm, SSD_USE[("yT", g - 1, 4)] + 1)
                    chain(tt(h64(y_), h64(xt), bc(d_bc[:, GH * g:GH * (g + 1)], 2, HD), ALU.mult))
                    b = ssd_wait(ev)
                    tt(y_, y_, bank(b), ALU.add).then_inc(ssd_free_dve, 1)
                    dve.wait_ge(*ssd_end(ev))
                    if c == 0:
                        nc.vector.memset(small[:, 60:61], 0.0).then_inc(y_done, 1)
                elif kind == "yo":
                    y_ = y1[c % 2][:, :]
                    for d_ in range(2):
                        b = ssd_wait(ev + (d_,))
                        tt(h64(y2[:, :]), h64(bank(b)), per_head(eacs, c, d_, g), ALU.mult).then_inc(ssd_free_dve, 1)
                        dve.wait_ge(*ssd_end(ev + (d_,)))
                        ins = tt(y_, y_, y2[:, :], ALU.add)
                        if d_ == 0:
                            chain(ins)
                        else:
                            ins.then_inc(y_done, 1)
                            dve.wait_ge(y_done, 5 * g + c + 1)
                elif kind == "yT":
                    b = ssd_wait(ev)
                    if c == 0:
                        dve.wait_ge(acc_free_act, acc_ends[A_E + 10 * g + 9][1])
                    dst = yg[:, 4 * g:4 * g + 4, chunk_col(c):chunk_col(c) + P]
                    tt(dst, bank(b).rearrange("p (q n) -> p q n", q=4), dst, ALU.mult).then_inc(ssd_free_dve, 1)

            for k in range(16):
                dve.wait_ge(yn_hi, k + 1)
                dve.wait_ge(y_sqd, k + 1)
                stt(y_lo[:, k, :], yg[:, k, :], pcol("ssd_norm_g", k), f32(y_hi[:, k, :]), ALU.mult, ALU.subtract
                    ).then_inc(y_ready, 1)
            dve.wait_ge(y_ss, 16)
            ts(small[:, 0:5], bank(6, 5), 1.0 / DI, EPS, ALU.mult, ALU.add).then_inc(yr_ms, 1)
            dve.wait_ge(yr_root, 1)
            chain(nc.vector.reciprocal(small[:, 48:53], small[:, 8:13]))
            tt(diag[:, :, :], bc(ident, 1, CHUNKS), bc(small[:, 48:53], 2, P), ALU.mult).then_inc(yr_dg, 1)
            dve.wait_ge(yr_rb, 1)
            step(cp(rbs[:, 0:NP_], bank(4, P)))
            step(cp(rbs[:, S0:S0 + NS], bank(5)))
            step.wait()
            dve.wait_ge(x_back, 32)

            def so_residual(i):
                for half in range(2):
                    m = 2 * i + half
                    dve.wait_ge(mm_done, 4 * i + (T_O + 2 * half + 2))
                    buf = tn[half]
                    for s_, cols in RANGES:
                        gate = modc(1, 2, m, s_) if isinstance(m, int) else \
                            mod[:, bass.ds(m + (48 + 16), 1), s_:s_ + 1]
                        ins = stt(buf[:, cols], acc(half)[:, cols], gate, rbs[:, cols], ALU.mult, ALU.mult)
                        (step(ins) if s_ == 0 else ins.then_inc(acc_free_dve, 1))
                    dve.wait_ge(acc_free_dve, 2 * i + (dve_accs(A_O) + half))
                    for s_, cols in RANGES:
                        x_ = xT[:, m, cols] if isinstance(m, int) else xT[:, bass.ds(m, 1), cols]
                        ins = tt(x_, x_, buf[:, cols], ALU.add)
                        (step(ins) if s_ == 0 else ins.then_inc(so_x, 1))

            so_residual(0)
            with dve.Fori(1, 4) as i:
                step.turn(i - 1, 4)
                dve.wait_ge(so_x, 2 * i)
                so_residual(i)
            step.leave(3)
            h_zeros()
            norm(3)
            ffn(1, T_F1, A_F1)

            inv_root(4)
            dve.wait_ge(fg_in, 16)
            for c in range(CHUNKS):
                dve.wait_ge(fin_ps, c + 1)
                if c >= 2:
                    dve.wait_ge(y_stored[c % 2], 16 * (c // 2))
                src = bank(4, D) if c % 2 == 0 else bank(2, D)
                stt(y_out[c % 2][:, :], src, small[:, 48 + c:49 + c], fg_bc[:, :], ALU.mult, ALU.mult
                    ).then_inc(fin_y, 1)


_INS = ["x_prompt", "x_sample", "cache_k", "cache_v", "state_ssm_fwd", "state_ssm_bwd", "c", "c_ctx", "ada_w",
        "ada_b", "norm_mix_g", "norm_ffn_g", "att_w_in", "att_lambda", "att_subln_g", "pool_w", "pool_scale",
        "att_w_out", "ssd_w_in", "ssd_conv_w", "ssd_conv_b", "ssd_dt_bias", "ssd_a_log", "ssd_d", "ssd_norm_g",
        "ssd_w_out", "ffn_w_up", "ffn_conv_w", "ffn_conv_b", "ffn_w_down", "final_norm_g"]
_OUTS = [("y_prompt", (1, NP_, D)), ("y_sample", (1, NS, D)), ("new_cache_k", (1, 1, NP_, HEADS, 2, HD)),
         ("new_cache_v", (1, 1, NP_, HEADS, 2 * HD)), ("new_state_fwd", (1, 1, 32, 64, 128)),
         ("new_state_bwd", (1, 1, 32, 64, 128))]


def tables():
    eye = np.eye(P, dtype=np.float32)
    rot = np.zeros((P, P), np.float32)
    for ch in range(P):
        base, f = ch - ch % 32, ch % 16
        if ch % 32 < 16:
            rot[base + 16 + f, ch] = -1.0
        else:
            rot[base + f, ch] = 1.0
    i = np.arange(P)
    le = (i[:, None] <= i[None, :]).astype(np.float32)
    inv = np.float32(10000.0) ** (-np.arange(16, dtype=np.float32) / np.float32(16))
    tok = np.arange(NS)
    pos = np.stack([tok // 64, tok % 64]).astype(np.float32)
    ch = np.arange(P)
    ang = (pos[(ch % 64) // 32, :] * inv[ch % 16][:, None]).astype(np.float32)
    inv_n = np.zeros((4, NP_ + NS), np.float32)
    for g, w in enumerate(POOL_WINDOWS):
        for at, n in ((0, NP_), (NP_, NS)):
            t = np.arange(n)
            inv_n[g, at:at + n] = 1.0 / (np.clip(t + w // 2, 0, n) - np.clip(t - w // 2, 0, n))
    return np.concatenate([eye, le, le.T, rot, np.cos(ang), np.sin(ang)], axis=1).astype(np.float32), inv_n


def kernel(**inputs):
    import concourse.bacc as bacc
    from concourse.bass_utils import run_bass_kernel_spmd

    nc = bacc.Bacc("TRN2", target_bir_lowering=False, num_devices=1)
    arrays, A, O = {}, {}, {}
    table, inv_n = tables()
    for name, a in [(n, inputs[n]) for n in _INS] + [("tables", table), ("inv_n", inv_n)]:
        a = np.ascontiguousarray(a)
        arrays[f"in_{name}"] = a
        A[name] = nc.dram_tensor(f"in_{name}", a.shape, mybir.dt.from_np(a.dtype), kind="ExternalInput").ap()
    for name, shape in _OUTS:
        O[name] = nc.dram_tensor(f"out_{name}", shape, F32, kind="ExternalOutput").ap()
    build(nc, A, O)
    r = run_bass_kernel_spmd(nc, [arrays], core_ids=[0])
    return tuple(r.results[0][f"out_{name}"] for name, _ in _OUTS)
```

```python
import math
from contextlib import ExitStack

import numpy as np
import concourse.bass as bass
from concourse import mybir

F32 = mybir.dt.float32
F32R = mybir.dt.float32r
ALU = mybir.AluOpType
ACT = mybir.ActivationFunctionType
AXX = mybir.AxisListType.X

P = 128
D = 1024
KD = D // P
NP_, NS = 128, 512
W = NP_ + 1 + NS + 1
HALF = W // 4 * 2 + 2
HALVES = (slice(0, HALF), slice(HALF, W))
S0 = NP_ + 1
CHUNKS = 1 + NS // P
HEADS = 4
HD = 64
KEYS = NS + P
FF = 2816
FT = FF // P
PARTS = ((0, 8), (8, 8), (16, 6))
DI = 2048
GROUPS = 4
GH = 8
EPS = 1e-6
LAM_INIT = 0.8 - 0.6 * math.exp(0.0)
POOL_WINDOWS = (2, 4, 8, 16)

T_A, T_B, T_F0 = 0, 16, 24
FFN_TILES = 2 * FT + 3 * KD
T_E = T_F0 + FFN_TILES
T_O = T_E + 40
T_F1 = T_O + 16
T_END = T_F1 + FFN_TILES
A_B, A_E, A_O = T_B, T_E, T_O
A_F1 = A_O + 8


END = 229344


def chunk_col(c):
    return 0 if c == 0 else S0 + (c - 1) * P


PARAM_ROWS = (("c_ctx", 8), ("c", 8), ("norm_mix_g", 16), ("norm_ffn_g", 16), ("pool_scale", 4), ("att_subln_g", 1),
              ("ada_b", 96), ("ssd_norm_g", 16), ("ssd_conv_w", 72), ("ssd_conv_b", 24), ("ffn_conv_w", 264),
              ("ffn_conv_b", 88))
PARAM_AT = {}
_n = 0
for _name, _rows in PARAM_ROWS:
    PARAM_AT[_name] = _n
    _n += _rows
N_PARAM = _n
PARAM_TILES = -(-N_PARAM // P)
N_PAR_DMA = sum((PARAM_AT[n_] + r_ - 1) // P - PARAM_AT[n_] // P + 1 for n_, r_ in PARAM_ROWS)


def att_schedule():
    after = {}

    def put(t, q, *ev):
        after.setdefault((t, q), []).append(ev)

    for h in range(HEADS):
        def at(i, *ev):
            put(3 * h + 3 + i // 4, i % 4, *ev)

        for kind in ("rotq", "rotk", "trk"):
            at(-1, kind, h)
        at(0, "trv", h)
        for j in range(CHUNKS):
            at(1 + 2 * j, "S", h, j)
            at(2 + 2 * j, "mix", h, j)
            at(4 + 2 * j, "T", h, j)
            at(5 + 2 * j, "PV", h, j)
        at(14, "ssO", h)
        at(16, "rbO", h)
    for g in range(3):
        put(13 + g, 2, "pool", g)
    after[(15, 3)] = after.get((15, 3), []) + [("out", 0), ("out", 1)] + after.pop((16, 0)) + [("out", 2), ("pool", 3)]
    out = []
    for t in range(16):
        for q in range(4):
            out.append(("mm", t, q))
            out += after.get((t, q), [])
    return out


ATT = att_schedule()
OUT_FIRST = (0, 1, 2, 4, 5, 6, 3, 7)
ATT_READER = {"rotq": "dve", "rotk": "dve", "trk": "act", "trv": "act", "S": "act", "T": "act", "PV": "act",
              "ssO": "dve", "rbO": "dve", "pool": "dve"}


def uses_of(schedule, readers, expand):
    index, ends, count = {}, [], {"act": 0, "dve": 0}
    for ev in schedule:
        if ev[0] in readers:
            for key in expand(ev):
                index[key] = len(ends)
                r = readers[ev[0]]
                count[r] += 1
                ends.append((r, count[r]))
    return index, ends


ATT_USE, ATT_END = uses_of(ATT, ATT_READER, lambda ev: [ev + (0,), ev + (1,)] if ev[0] == "S" else [ev])


def ssd_schedule():
    after = {}

    def put(e, q, *ev):
        after.setdefault((e, q), []).append(ev)

    put(0, 1, "dtT", 0)
    put(3, 1, "sum", 0)
    put(4, 1, "acsT", 0)
    for g in range(GROUPS):
        b = 10 * g
        put(b + 1, 1, "trB", g)
        for j in range(4):
            put(b + 3 + j, 0, "trx", g, j)
        put(b + 7, 0, "init", g, 0)
        put(b + 7, 0, "init", g, 1)
        slots = [(b + 7 + i // 2, i % 2) for i in range(0, 40)]
        for i, c in enumerate((4, 3, 2, 0)):
            put(*slots[i], "csb", g, c)
        for c in range(CHUNKS):
            at = (3, 6, 10, 13, 16)[c]
            put(*slots[at], "cb", g, c)
            if c < 4:
                put(*slots[at], "csf", g, c)
            put(*slots[at + 2], "yd", g, c)
            if c:
                put(*slots[at + 3], "yo", g, c)
            put(*slots[at + 6], "yT", g, c)
        put(*slots[10], "stT", g)
        if g == GROUPS - 1:
            for i, ks in ((6, (0, 1, 2, 3)), (10, (4, 5, 6)), (13, (7, 8, 9)), (16, (10, 11))):
                for k in ks:
                    put(*slots[i], "ynorm", g, k)
            for k, i in enumerate((9, 10, 11, 11, 13, 14, 14, 16, 17, 17, 19, 20)):
                put(*slots[i], "yout", g, k)
    out = []
    for e in range(40):
        for q in range(2):
            out.append(("mm", e, q))
            out += sorted(after.pop((e, q), []), key=lambda ev: ev[1])
    for k in sorted(after):
        out += after[k]
    return out


SSD = ssd_schedule()
SSD_READER = {"dtT": "dve", "sum": "dve", "acsT": "act", "trB": "act", "trx": "act", "init": "act", "csb": "dve", "csf": "dve", "cb": "dve", "yd": "dve",
              "yo": "dve", "yT": "dve", "stT": "act"}
SSD_USE, SSD_END = uses_of(
    SSD, SSD_READER,
    lambda ev: [ev + (0,), ev + (1,)] if ev[0] in ("sum", "acsT", "trB", "trx", "yo", "stT") else [ev])
G_AT = {ev: i + 1 for i, ev in enumerate(ev for ev in ATT if ev[0] in ("rbO", "pool"))}
SSD_TILE, _e = {}, 0
for _ev in SSD:
    _e = _ev[1] if _ev[0] == "mm" else _e
    SSD_TILE[_ev] = _e
CS_LIST = [ev for ev in SSD if ev[0] in ("csb", "csf")]
CS_AT = {ev: i for i, ev in enumerate(CS_LIST)}


class Steps:

    def __init__(self, eng, sem):
        self.eng, self.sem, self.n, self.off = eng, sem, 0, 0

    def __call__(self, instruction):
        instruction.then_inc(self.sem, 1)
        self.n += 1

    def wait(self):
        self.eng.wait_ge(self.sem, self.off + self.n)

    def turn(self, i, per):
        self.mark, self.per, self.off = self.n, per, i * per

    def leave(self, turns):
        assert self.n - self.mark == self.per, (self.n - self.mark, self.per)
        self.n, self.off = self.mark + turns * self.per, 0


def bc(ap, at, n):
    shape = list(ap.shape)
    return ap.unsqueeze(at).broadcast_to(shape[:at] + [n] + shape[at:])


def build(nc, A, O):
    with ExitStack() as ctx:
        base = -(-nc.sbuf_base // 32) * 32
        top = [base]

        def at(name, shape, dt, offset):
            t = nc.alloc_sbuf_tensor_at(name, shape, dt, offset=offset)
            return t, offset + -(-4 * int(np.prod(shape[1:])) // 32) * 32

        def fixed(name, shape, dt=F32):
            t, top[0] = at(name, shape, dt, top[0])
            return t

        def phase(start, end=END):
            here = [start]

            def alloc(name, shape, dt=F32):
                t, here[0] = at(name, shape, dt, here[0])
                assert here[0] <= end, (name, here[0])
                return t
            return alloc

        consts = fixed("consts", [P, 4 * P])
        ident, m_le, m_ge, perm = (consts[:, i * P:(i + 1) * P] for i in range(4))
        masks = consts[:, P:3 * P].rearrange("p (a b) -> p a b", a=2)
        early_at = top[0] - 4 * P
        pmat = fixed("pmat", [P, 4, P])
        wdt_hi = fixed("wdt_hi", [P, KD, 64], F32R)
        wdt_lo = fixed("wdt_lo", [P, KD, 64], F32R)
        early_end = top[0]
        ones = fixed("ones", [P, P])
        pick = fixed("pick", [P, 8])
        par = fixed("par", [P, N_PARAM])
        svec4 = fixed("svec4", [P, KD, 4], F32R)
        mod = fixed("mod", [P, 96, 2])
        gain1 = fixed("gain1", [P, 4, KD, 2])
        small = fixed("small", [P, 64])
        dtb_bc = fixed("dtb_bc", [P, 64])
        a_bc = fixed("a_bc", [P, 64])
        d_bc = fixed("d_bc", [P, 32])
        h_at = top[0]
        h_hi = fixed("h_hi", [P, KD, W], F32R)
        h_lo = fixed("h_lo", [P, KD, W], F32R)
        y_hi, _ = at("y_hi", [P, 2 * KD, W], F32R, h_at)
        sums0, _ = at("sums0", [P, W], F32, (h_at + (2 * KD - 1) * W * 4) // 32 * 32)
        g_at = top[0]
        g_hi = fixed("g_hi", [P, KD, W], F32R)
        g_lo = fixed("g_lo", [P, KD, W], F32R)
        yg, _ = at("yg", [P, 2 * KD, W], F32, g_at)
        dt_T, _ = at("dt_T", [64, W], F32, g_at)
        y_lo, _ = at("y_lo", [P, 2 * KD, W], F32R, g_at)
        ada0 = [at(f"ada0_{i}", [P, KD, 2 * P], F32, g_at + i * KD * 2 * P * 4)[0] for i in range(5)]
        ada0_lo = [at(f"ada0_lo{i}", [P, KD, 2 * P], F32R, g_at + i * KD * 2 * P * 4)[0] for i in range(5)]
        raw = [fixed(f"raw{i}", [P, KD, P]) for i in range(4)]
        w_hi = [fixed(f"w_hi{i}", [P, KD, P], F32R) for i in range(2)]
        w_lo = [fixed(f"w_lo{i}", [P, KD, P], F32R) for i in range(2)]
        ada_at = top[0]
        ada_size = KD * 2 * P * 4
        ada1 = [fixed("ada1_0", [P, KD, 2 * P]), at("ada1_1", [P, KD, 2 * P], F32, END - 3 * ada_size)[0]]
        ada1_lo = [at(f"ada1_lo{i}", [P, KD, 2 * P], F32R, (ada_at, END - 3 * ada_size)[i])[0] for i in range(2)]
        ada_hi = [at(f"ada_hi{i}", [P, KD, 2 * P], F32R, END - (2 - i) * ada_size)[0] for i in range(2)]
        x_at = top[0]
        xT = fixed("xT", [P, KD, W])
        rest_at = top[0]

        a = phase(rest_at)
        sq = [a(f"sq{i}", [P, W]) for i in range(2)]
        diag = a("diag", [P, CHUNKS, P])
        tn = [a(f"tn{i}", [P, W]) for i in range(2)]
        cg, cv, sg, hm = (a(n, [P, W]) for n in ("cg", "cv", "sg", "hm"))
        rbs = a("rbs", [P, W])
        ada_row = [a(f"ada_row{i}", [P, 2 * P]) for i in range(2)]
        sums_ = a("sums", [P, W])
        a = phase(rest_at, END - 2 * ada_size)
        for _i in range(2):
            a(f"_pad{_i}", [P, W])
        a("_pad_d", [P, CHUNKS, P])
        for _i in range(2):
            a(f"_padt{_i}", [P, W])
        x_in = a("x_in", [P, CHUNKS, D])
        par_in = a("par_in", [P, PARAM_TILES, P])
        wdt = a("wdt", [P, KD, 64])
        lam_in = a("lam_in", [P, 4, HD])
        svec = a("svec", [P, KD, 2])
        a = phase(rest_at)
        a("_pad2", [P, 2 * W])
        a("_pad3", [P, CHUNKS, P])
        fg_bc = a("fg_bc", [P, D])
        y_out = [a(f"y_out{i}", [P, D]) for i in range(2)]
        a = phase(x_at)
        rope = a("rope", [P, 2, NS])
        inv_n = a("inv_n", [P, NP_ + NS])
        qz = a("qz", [P, 2, NP_ + NS])
        kT = a("kT", [P, NP_ + KEYS])
        v_tok = [a(f"v_tok{i}", [P, CHUNKS + 1, P]) for i in range(2)]
        q_raw, k_raw, v_raw = (a(n, [P, W]) for n in ("q_raw", "k_raw", "v_raw"))
        ck_in = a("ck_in", [P, HEADS, P])
        k_out = a("k_out", [P, P])
        prob = [a(f"prob{i}", [P, 2, KEYS]) for i in range(2)]
        att = [a(f"att{i}", [P, KEYS]) for i in range(2)]
        attT = [a(f"attT{i}", [P, CHUNKS, P]) for i in range(2)]
        pb = [a(f"pb{i}", [P, 672]) for i in range(3)]
        pooled = a("pooled", [P, W])
        pmul = a("pmul", [P, W])
        rtmp = pmul[:, 0:NS]
        o_sb = a("o_sb", [P, W])
        o_sq = a("o_sq", [P, W])
        o_diag = a("o_diag", [P, CHUNKS, P])
        o_nrm = a("o_nrm", [P, W])
        a = phase(ada_at)
        bT = [a(f"bT{i}", [P, W]) for i in range(2)]
        cT = [a(f"cT{i}", [P, W]) for i in range(2)]
        b_tok = [a(f"b_tok{i}", [P, CHUNKS, P]) for i in range(2)]
        x_tok = [a(f"x_tok{i}", [P, CHUNKS, 512]) for i in range(2)]
        cx = a("cx", [P, W])
        y_sums, y_sq = bT[0], (cT[0], x_tok[0][:, :, :].rearrange("p c n -> p (c n)")[:, 0:W])
        y_sq_end = (cT[0], bT[1])
        R = a("R", [P, 2, GH, P])
        xdt = a("xdt", [P, 2, 512])
        xw = [a(f"xw{i}", [P, 512]) for i in range(2)]
        st_b = a("st_b", [P, 4, 512])
        st_f = [a(f"st_f{i}", [P, 512]) for i in range(2)]
        st_in = a("st_in", [P, 2, 4, P])
        st_p = a("st_p", [P, 2, 512])
        st_out = a("st_out", [P, 4, P])
        y2 = a("y2", [P, 512])
        st_tmp = y2
        dt, acs, dec, wst = (a(n, [P, CHUNKS, 64]) for n in ("dt", "acs", "dec", "wst"))
        a = phase(early_at, early_end)
        cbm = a("cbm", [P, 2, P])
        y1 = [a(f"y1_{i}", [P, 512]) for i in range(2)]
        eacs = a("eacs", [P, CHUNKS, 64])
        dt_x, dt_e, dt_s, dt_z, dt_p, da = (R[:, :, :, :].rearrange("p a b c -> p (a b c)")[:, i * 320:(i + 1) * 320]
                                            for i in range(6))
        da3 = da.rearrange("p (c x) -> p c x", c=CHUNKS)
        acsT = xdt[0:64, :, :].rearrange("p a b -> p (a b)")[:, 0:CHUNKS * P]

        scr_x = nc.dram_tensor("scr_x", (P, KD, W), F32, kind="Internal").ap()
        scr_acs = nc.dram_tensor("scr_acs", (CHUNKS, 64, P), F32, kind="Internal").ap()

        ps = ctx.enter_context(nc.psum_tensor("ps", [P, 8 * 512], F32))

        def acc(slot):
            at0 = 1024 * slot + 512 - HALF
            return ps[:, at0:at0 + W]

        def bank(b, n=512, o=0):
            return ps[:, 512 * b + o:512 * b + o + n]

        def sem(name):
            return ctx.enter_context(nc.semaphore(name))

        raw_in = [sem(f"raw_in{i}") for i in range(4)]
        ada0_in = [sem(f"ada0_in{i}") for i in range(5)]
        ada1_in = [sem("ada1_in0"), sem("ada1_in1")]
        consts_in, par_dma, x_dma, bcast_in, wdt_in, ones_done = (sem(n) for n in
                                                       ("consts_in", "par_dma", "x_dma", "bcast_in", "wdt_in", "ones_done"))
        x_spilled, x_back, rope_in, ck_dma, cv_dma0, cv_dma1 = (sem(n) for n in (
            "x_spilled", "x_back", "rope_in", "ck_dma", "cv_dma0", "cv_dma1"))
        inv_in = sem("inv_in")
        k_stored, v_stored, acs_stored, st_in_dma, st_stored, fg_in = (sem(n) for n in (
            "k_stored", "v_stored", "acs_stored", "st_in_dma", "st_stored", "fg_in"))
        R_in, R_used = [sem("R_in0"), sem("R_in1")], sem("R_used")
        w_hi_done, w_split, mm_done = sem("w_hi_done"), sem("w_split"), sem("mm_done")
        acc_free_dve, acc_free_act = sem("acc_free_dve"), sem("acc_free_act")
        dve_step = sem("dve_step")
        act_step = sem("act_step")
        par_ps = sem("par_ps")
        par_done = sem("par_done")
        svec_done = sem("svec_done")
        memset_done = sem("memset_done")
        xt_ps = sem("xt_ps")
        xt_done = sem("xt_done")
        wdt_hi_done = sem("wdt_hi_done")
        lam_e = sem("lam_e")
        abc_done = sem("abc_done")
        lam_s = sem("lam_s")
        ada_hi_done = sem("ada_hi_done")
        ada_split = sem("ada_split")
        ada_mm = sem("ada_mm")
        ada_rows = sem("ada_rows")
        ada_cols = sem("ada_cols")
        mod_done = sem("mod_done")
        sq_added = sem("sq_added")
        y_added = sem("y_added")
        sq_ready = sem("sq_ready")
        ss_done = sem("ss_done")
        ms_done = sem("ms_done")
        root_done = sem("root_done")
        diag_done = sem("diag_done")
        rb_done = sem("rb_done")
        t_done = sem("t_done")
        h_hi_done = sem("h_hi_done")
        h_ready = sem("h_ready")
        att_mm = sem("att_mm")
        att_free_act = sem("att_free_act")
        att_free_dve = sem("att_free_dve")
        q_roped = sem("q_roped")
        k_roped = sem("k_roped")
        smax = sem("smax")
        att_a = sem("att_a")
        o_sqd = sem("o_sqd")
        o_root = sem("o_root")
        o_dg = sem("o_dg")
        o_hi = sem("o_hi")
        pool_y = sem("pool_y")
        pool_hi = sem("pool_hi")
        g_ready = sem("mix_ready")
        ffn_id = sem("ffn_id")
        ffn_silu = sem("ffn_silu")
        hm_done = sem("hm_done")
        ffn_hi = sem("ffn_hi")
        f_ready = sem("ffn_ready")
        dtT_mm = sem("dtT_mm")
        dtT_copied = sem("dtT_copied")
        dt_xb = sem("dt_xb")
        dt_exp = sem("dt_exp")
        da_done = sem("da_done")
        acs_done = sem("acs_done")
        tot_w = sem("tot_w")
        acs_exp = sem("acs_exp")
        ssd_mm = sem("ssd_mm")
        ssd_free_act = sem("ssd_free_act")
        ssd_free_dve = sem("ssd_free_dve")
        conv_id = sem("conv_id")
        conv_silu = sem("conv_silu")
        xw_done = sem("xw_done")
        st_done = sem("st_done")
        seg_exp = sem("seg_exp")
        W_done = sem("W_done")
        y_done = sem("y_done")
        yn_hi = sem("yn_hi")
        y_ready = sem("y_ready")
        y_sqd = sem("y_sqd")
        y_ss = sem("y_ss")
        yr_ms = sem("yr_ms")
        yr_root = sem("yr_root")
        yr_dg = sem("yr_dg")
        yr_rb = sem("yr_rb")
        fin_ps = sem("fin_ps")
        fin_y = sem("fin_y")
        so_x = sem("so_x")
        da_read = sem("da_read")
        pmat_in = sem("pmat_in")
        y_stored = [sem("y_stored0"), sem("y_stored1")]

        block = ctx.enter_context(nc.Block())

        def pcol(name, i=0):
            return par[:, PARAM_AT[name] + i:PARAM_AT[name] + i + 1]

        def modc(layer, j, k, s):
            i = layer * 48 + j * 8 + k
            return mod[:, i, s:s + 1]

        def h_done(n, k):
            return h_ready, 8 * n + k + 1

        def sums(n):
            return sums0[:, :] if n == 0 else sums_[:, :]

        def acc_free(a_):
            ends = acc_ends[a_]
            return (acc_free_act if ends[0] == "act" else acc_free_dve), ends[1]

        acc_ends, count = [], {"act": 0, "dve": 0}
        for a_ in range(A_F1 + FFN_TILES):
            who = "dve"
            if a_ < 12 or (A_E <= a_ < A_O and (a_ - A_E) % 10 >= 6):
                who = "act"
            count[who] += 1
            acc_ends.append((who, count[who]))

        def dve_accs(a_):
            assert acc_ends[a_][0] == "dve"
            return acc_ends[a_][1]

        def y_squares(k):
            return y_sums[:, :] if k == 0 else (y_sq if k < 12 else y_sq_end)[k % 2][:, 0:W]

        def att_end(key):
            who, n = ATT_END[ATT_USE[key]]
            return (att_free_act if who == "act" else att_free_dve), n

        def ssd_end(key):
            who, n = SSD_END[SSD_USE[key]]
            return (ssd_free_act if who == "act" else ssd_free_dve), n

        def att_col(t):
            return (t % 3) * 512 + (t // 3) * P if t < 12 else 1536 + (t - 12) * P

        def ssd_tile(e):
            g, i = divmod(e, 10)
            return ("b", 16 + g) if i == 0 else ("c", 20 + g) if i == 1 else ("x", 4 * g + i - 2) if i < 6 else \
                ("z", 4 * g + i - 6)

        def ssd_col(e):
            kind, m = ssd_tile(e)
            return m * P if kind == "z" else DI + m * P

        kp = "(k p) m -> p k m"
        w_att = A["att_w_in"][0].rearrange(kp, p=P)
        w_ao = A["att_w_out"][0].rearrange(kp, p=P)
        w_ssd = A["ssd_w_in"][0].rearrange(kp, p=P)
        w_so = A["ssd_w_out"][0].rearrange(kp, p=P)
        w_up = [A["ffn_w_up"][l].rearrange(kp, p=P) for l in range(2)]
        w_dn = [A["ffn_w_down"][l].rearrange(kp, p=P) for l in range(2)]
        w_ada = [A["ada_w"][l].rearrange(kp, p=P) for l in range(2)]

        ADA_F = 20
        ADA_B = ((8, 9), (10, 11), (12, 13), (14, 15), (16,), (17,), (18,), (19,))
        ADA_PAIRS = (8, 6, 0)

        def ada_bufs(s, half=None):
            j = s % 2 if half is None else half
            if half is None and s < 8:
                return ada0[s % 5], ada_hi[j], ada0_lo[s % 5], tn[j]
            return ada1[j], ada_hi[j], ada1_lo[j], ada_row[j]

        def ada_landed(s, half=None):
            if half is None and s < 8:
                return ada0_in[s % 5], 16 * (s // 5 + 1)
            return (ada1_in[s % 2], 16 * ((s - 8) // 2 + 1)) if half is None else \
                (ada1_in[half], 8 * (s + (2 - half)) - 64)

        @block.sync
        def _(sp):
            def param_rows():
                n = 0
                srcs = {
                    "c_ctx": A["c_ctx"].rearrange("(r c) -> r c", c=P), "c": A["c"].rearrange("o (r c) -> (o r) c", c=P),
                    "norm_mix_g": A["norm_mix_g"].rearrange("l (r c) -> (l r) c", c=P),
                    "norm_ffn_g": A["norm_ffn_g"].rearrange("l (r c) -> (l r) c", c=P),
                    "pool_scale": A["pool_scale"].rearrange("l (r c) -> (l r) c", c=P),
                    "att_subln_g": A["att_subln_g"],
                    "ada_b": A["ada_b"].rearrange("l (r c) -> (l r) c", c=P),
                    "ssd_norm_g": A["ssd_norm_g"].rearrange("l (r c) -> (l r) c", c=P),
                    "ssd_conv_w": A["ssd_conv_w"][0].rearrange("l (r c) -> (l r) c", c=P),
                    "ssd_conv_b": A["ssd_conv_b"].rearrange("l (r c) -> (l r) c", c=P),
                    "ffn_conv_w": A["ffn_conv_w"].rearrange("l j (r c) -> (l j r) c", c=P),
                    "ffn_conv_b": A["ffn_conv_b"].rearrange("l (r c) -> (l r) c", c=P),
                }
                for name, rows in PARAM_ROWS:
                    r = 0
                    while r < rows:
                        i, p0 = divmod(PARAM_AT[name] + r, P)
                        m = min(rows - r, P - p0)
                        sp.dma_start(par_in[p0:p0 + m, i, :], srcs[name][r:r + m, :]).then_inc(par_dma, 16)
                        r += m
                        n += 1
                return n

            def ada(s):
                l, c0 = divmod(s * 256, 6 * D)
                src = w_ada[l][:, :, c0:c0 + 256]
                if s < 8:
                    if s >= 5:
                        sp.wait_ge(ada_mm, s - 4)
                    sp.dma_start(ada0[s % 5][:, :, :], src).then_inc(ada0_in[s % 5], 16)
                else:
                    if s > 9:
                        sp.wait_ge(ada_mm, s - 1)
                    sp.dma_start(ada1[s % 2][:, :, :], src).then_inc(ada1_in[s % 2], 16)

            def load(slot, t, src, k=KD):
                if not (isinstance(t, int) and t < 4):
                    sp.wait_ge(w_split, t - 3)
                sp.dma_start(raw[slot][:, 0:k, :], src).then_inc(raw_in[slot], 16)

            sp.dma_start(consts[:, :], A["tables"][:, 0:4 * P]).then_inc(consts_in, 16)
            sp.dma_start(pick[0:4, 0:2], A["pick"]).then_inc(consts_in, 16)
            assert param_rows() == N_PAR_DMA
            ada(0)
            for c in range(CHUNKS):
                src = A["x_prompt"][0] if c == 0 else A["x_sample"][0, (c - 1) * P:c * P, :]
                sp.dma_start(x_in[:, c, :], src).then_inc(x_dma, 16)
            for s in range(1, 5):
                ada(s)
            sp.dma_start(lam_in[:, :, :], A["att_lambda"][0].partition_broadcast(P)).then_inc(bcast_in, 16)
            sp.dma_start(dtb_bc[:, :], A["ssd_dt_bias"][0].rearrange("a b -> (a b)").partition_broadcast(P)
                         ).then_inc(bcast_in, 16)
            sp.dma_start(a_bc[:, :], A["ssd_a_log"][0].rearrange("a b -> (a b)").partition_broadcast(P)
                         ).then_inc(bcast_in, 16)
            sp.dma_start(d_bc[:, :], A["ssd_d"][0].partition_broadcast(P)).then_inc(bcast_in, 16)
            sp.dma_start(pmat[:, :, :], A["pool_w"][0].rearrange("g c d -> c g d")).then_inc(pmat_in, 16)
            sp.dma_start(wdt[:, :, :], w_ssd[:, :, DI + 3072:DI + 3072 + 64]).then_inc(wdt_in, 16)
            for t in range(4):
                load(t, t, w_att[:, :, att_col(t):att_col(t) + P])
            for s in range(5, 9):
                ada(s)
            sp.wait_ge(xt_done, KD)
            sp.dma_start(scr_x, xT[:, :, :]).then_inc(x_spilled, 16)
            sp.wait_ge(*h_done(0, KD - 1))
            sp.wait_ge(x_spilled, 16)
            sp.dma_start(rope[:, :, :], A["tables"][:, 4 * P:4 * P + 2 * NS].rearrange("p (a b) -> p a b", a=2)
                         ).then_inc(rope_in, 16)
            sp.dma_start(ck_in[:, :, :], A["cache_k"][0, 0].rearrange("t h c d -> t h (c d)")).then_inc(ck_dma, 16)
            sp.dma_start(inv_n[:, :], A["inv_n"][0].partition_broadcast(P)).then_inc(inv_in, 16)
            for h in range(2):
                sp.dma_start(v_tok[h][:, CHUNKS, :], A["cache_v"][0, 0, :, h, :]).then_inc((cv_dma0, cv_dma1)[h], 16)
            for t in range(4, 16):
                load(t % 4, t, w_att[:, :, att_col(t):att_col(t) + P])
                if t % 3 == 2 and t < 14:
                    h = t // 3 - 1
                    sp.wait_ge(*att_end(("trv", h)))
                    sp.dma_start(O["new_cache_v"][0, 0, :, h, :], v_tok[h % 2][:, 0, :]).then_inc(v_stored, 16)
                    sp.wait_ge(*att_end(("trk", h)))
                    sp.dma_start(O["new_cache_k"][0, 0, :, h, :, :].rearrange("t c d -> t (c d)"), k_out[:, :]
                                 ).then_inc(k_stored, 16)
                if t in (9, 12):
                    h = 2 + (t - 9) // 3
                    sp.wait_ge(*att_end(("PV", h - 2, 4)))
                    sp.dma_start(v_tok[h % 2][:, CHUNKS, :], A["cache_v"][0, 0, :, h, :]
                                 ).then_inc((cv_dma0, cv_dma1)[h % 2], 16)
            for t in range(16, 20):
                load(t % 4, t, w_ao[:, :, (t - 16) * P:(t - 15) * P])
                if t == 17:
                    sp.wait_ge(*att_end(("trv", 3)))
                    sp.dma_start(O["new_cache_v"][0, 0, :, 3, :], v_tok[1][:, 0, :]).then_inc(v_stored, 16)
                    sp.wait_ge(*att_end(("trk", 3)))
                    sp.dma_start(O["new_cache_k"][0, 0, :, 3, :, :].rearrange("t c d -> t (c d)"), k_out[:, :]
                                 ).then_inc(k_stored, 16)
                if t > 16:
                    sp.wait_ge(pool_y, t - 16)
                    sp.dma_start(inv_n[:, :], A["inv_n"][t - 16].partition_broadcast(P)).then_inc(inv_in, 16)
            sp.wait_ge(g_ready, 8)
            sp.wait_ge(k_stored, 64)
            sp.wait_ge(v_stored, 64)
            ada(9)
            sp.dma_start(xT[:, :, :], scr_x).then_inc(x_back, 16)
            for t in range(20, 24):
                load(t % 4, t, w_ao[:, :, (t - 16) * P:(t - 15) * P])
                if t > 20:
                    ada(2 * t - 32)
                    ada(2 * t - 31)
            ada(16)

            def ffn(l, t0):
                for p, (m0, n) in enumerate(PARTS):
                    first = 2 * m0 + 8 * p + t0

                    def two_pairs(i):
                        for j in range(2):
                            for half in range(2):
                                col = half * FF + m0 * P + (2 * i + j) * P
                                load(2 * j + half, first + 4 * i + 2 * j + half, w_up[l][:, :, bass.ds(col, P)])

                    if l == 0 and p < 2:
                        for i in range(2 * n):
                            col = (i % 2) * FF + (m0 + i // 2) * P
                            load(i % 4, first + i, w_up[l][:, :, col:col + P])
                            if p == 0:
                                ada(17 + i)
                            elif 5 <= i < 15:
                                ada(33 + i)
                    else:
                        with sp.Fori(0, n // 2) as i:
                            two_pairs(i)
                    down = first + 2 * n
                    if l == 0 and p == 0:
                        for i in range(8):
                            load(i % 4, down + i, w_dn[l][:, m0:m0 + n, i * P:(i + 1) * P], n)
                            if i < 5:
                                ada(33 + i)
                    else:
                        with sp.Fori(0, 2) as i:
                            for j in range(4):
                                load(j, down + 4 * i + j, w_dn[l][:, m0:m0 + n, bass.ds((4 * i + j) * P, P)], n)

            ffn(0, T_F0)
            def row_loads(n, d_):
                g, c = divmod(n, CHUNKS)
                if n and d_ == 0:
                    sp.wait_ge(R_used, n)
                elif n:
                    sp.wait_ge(ssd_mm, SSD_USE[("yd", (n - 1) // CHUNKS, (n - 1) % CHUNKS)] + 1)
                src = scr_acs[c, 32 * d_ + g * GH:32 * d_ + (g + 1) * GH, :]
                sp.dma_start(R[:, d_, :, :], src.partition_broadcast(P)).then_inc(R_in[d_], 16)

            def state_loads(g):
                if g:
                    sp.wait_ge(ssd_mm, SSD_USE[("init", g - 1, 1)] + 1)
                for d_, name in enumerate(("state_ssm_fwd", "state_ssm_bwd")):
                    src = A[name][0, 0, g * GH:(g + 1) * GH].rearrange("(q r) p n -> (r p) q n", r=2)
                    sp.dma_start(st_in[:, d_, :, :], src).then_inc(st_in_dma, 16)

            def state_stores(g):
                for d_, name in enumerate(("new_state_fwd", "new_state_bwd")):
                    dst = O[name][0, 0, g * GH:(g + 1) * GH].rearrange("(q r) p n -> (r p) q n", r=2)
                    sp.wait_ge(*ssd_end(("stT", g, d_)))
                    sp.dma_start(dst, st_out[:, :, :]).then_inc(st_stored, 16)

            def beside(tile):
                for ev in SSD:
                    if SSD_TILE[ev] != tile:
                        continue
                    if ev[0] == "init" and ev[2] == 1 and ev[1] + 1 < GROUPS:
                        state_loads(ev[1] + 1)
                    if ev[0] == "yd" and ev[1:] != (GROUPS - 1, CHUNKS - 1):
                        for d_ in range(2):
                            row_loads(CHUNKS * ev[1] + ev[2] + 1, d_)
                    if ev[0] == "stT":
                        state_stores(ev[1])

            LEAD = 5
            for e in range(40):
                load(e % 4, T_E + e, w_ssd[:, :, ssd_col(e):ssd_col(e) + P])
                if e == 3:
                    sp.wait_ge(acc_free_dve, dve_accs(A_E - 1))
                    sp.dma_start(scr_x, xT[:, :, :]).then_inc(x_spilled, 16)
                if e == 4 + LEAD:
                    sp.wait_ge(*ssd_end(("acsT", 0, 1)))
                    sp.dma_start(scr_acs.rearrange("c h i -> h c i"),
                                 acsT.rearrange("p (c i) -> p c i", c=CHUNKS)).then_inc(acs_stored, 16)
                    sp.wait_ge(acs_stored, 16)
                    state_loads(0)
                    sp.wait_ge(da_read, 1)
                    row_loads(0, 0)
                    row_loads(0, 1)
                beside(e - LEAD)
            for t in range(4):
                load(t, T_O + t, w_so[:, (t // 2) * 8:(t // 2) * 8 + 8, (t % 2) * P:(t % 2 + 1) * P])
                beside(40 + t - LEAD)
            for tile in range(40 + 4 - LEAD, max(SSD_TILE.values()) + 1):
                beside(tile)
            sp.wait_ge(*ssd_end(("yT", 3, 4)))
            sp.wait_ge(st_stored, 128)
            sp.dma_start(xT[:, :, :], scr_x).then_inc(x_back, 16)
            with sp.Fori(1, 4) as i:
                for j in range(4):
                    load(j, T_O + 4 * i + j, w_so[:, (j // 2) * 8:(j // 2) * 8 + 8, bass.ds((2 * i + j % 2) * P, P)])
            ffn(1, T_F1)
            sp.wait_ge(f_ready, 2 * FT)
            sp.dma_start(fg_bc[:, :], A["final_norm_g"].partition_broadcast(P)).then_inc(fg_in, 16)
            for c in range(CHUNKS):
                dst = O["y_prompt"][0] if c == 0 else O["y_sample"][0, (c - 1) * P:c * P, :]
                sp.wait_ge(fin_y, c + 1)
                sp.dma_start(dst, y_out[c % 2][:, :]).then_inc(y_stored[c % 2], 16)
            sp.wait_ge(y_stored[0], 48)
            sp.wait_ge(y_stored[1], 32)
            sp.wait_ge(k_stored, 64)
            sp.wait_ge(v_stored, 64)
            sp.wait_ge(st_stored, 128)

        @block.gpsimd
        def _(pool):
            nc.gpsimd.memset(ones[:, :], 1.0).then_inc(ones_done, 1)

            def split(j, t, i, k):
                loads, before = 16 * (i + 1), t - 1
                if not isinstance(t, int):
                    loads, before = (nc.snap(v, bass.OrderedEngineSet([pool.engine])) for v in (loads, before))
                pool.wait_ge(ones_done, 1)
                pool.wait_ge(raw_in[j], loads)
                if not (isinstance(t, int) and t < 2):
                    pool.wait_ge(mm_done, before)
                nc.gpsimd.tensor_scalar(w_hi[j % 2][:, 0:k, :], raw[j][:, 0:k, :], 1.0, None, ALU.mult
                                        ).then_inc(w_hi_done, 1)
                pool.wait_ge(w_hi_done, t + 1)
                nc.gpsimd.tensor_tensor(w_lo[j % 2][:, 0:k, :], raw[j][:, 0:k, :], w_hi[j % 2][:, 0:k, :].bitcast(F32),
                                        ALU.subtract).then_inc(w_split, 1)

            def splits(t0, t1, k=KD):
                with pool.Fori(t0 // 4, t1 // 4) as i:
                    for j in range(4):
                        split(j, 4 * i + j, i, k)

            last = PARTS[2][1]
            for j in range(4):
                split(j, j, 0, KD)
            splits(4, T_E - 8)
            splits(T_E - 8, T_E, last)
            splits(T_E, T_END - 8)
            splits(T_END - 8, T_END, last)

        @block.tensor
        def _(pe):
            mm, tr = nc.tensor.matmul, nc.tensor.transpose

            def steps(t, slot, aslot, x_hi, x_lo, ks, k_of=lambda k: k, first=True, last=True, n=KD, ready=None):
                out = acc(aslot)
                for k in ks:
                    if ready is not None:
                        ready(k)
                    for i, (w, x) in enumerate(((w_hi, x_hi), (w_hi, x_lo), (w_lo, x_hi))):
                        for cols in HALVES:
                            ins = mm(out[:, cols], w[slot][:, k, :], x[:, k_of(k), cols],
                                     start=first and k == 0 and i == 0, stop=last and k == n - 1 and i == 2)
                return ins

            def begin(t, a_):
                pe.wait_ge(w_split, t + 1)
                if isinstance(a_, int):
                    if a_ >= 2:
                        pe.wait_ge(*acc_free(a_ - 2))

            def h_wait(n):
                return lambda k: pe.wait_ge(*h_done(n, k))

            def ada_step(s, half=None):
                _, hi, lo, _ = ada_bufs(s, half)
                pe.wait_ge(ada_split, s + 1)
                if not (isinstance(s, int) and s == 0):
                    pe.wait_ge(ada_rows, s)
                for k in range(KD):
                    if k:
                        mm(bank(6, 2 * P)[0:2, :], svec4[:, k, 0:2], lo[:, k, :], start=False, stop=False)
                    ins = mm(bank(6, 2 * P)[0:4, :], svec4[:, k, :], hi[:, k, :], start=k == 0, stop=k == KD - 1)
                    if not k:
                        mm(bank(6, 2 * P)[0:2, :], svec4[:, k, 0:2], lo[:, k, :], start=False, stop=False)
                ins.then_inc(ada_mm, 1)

            def ada_turn(s, half=None, b=5):
                row = ada_bufs(s, half)[3]
                pe.wait_ge(ada_rows, s + 1)
                if not (isinstance(s, int) and s == 0):
                    pe.wait_ge(mod_done, s)
                for j in range(2):
                    ins = mm(bank(b, 2, 2 * j), row[0:4, j * P:(j + 1) * P], pick[0:4, 0:2], start=True, stop=True)
                ins.then_inc(ada_cols, 1)

            def ss(n):
                pe.wait_ge(sq_added, 7 * n + 7)
                for c in range(CHUNKS):
                    ins = mm(bank(7, 1, c), sums(n)[:, chunk_col(c):chunk_col(c) + P], ones[:, 0:1], start=True,
                             stop=True)
                ins.then_inc(ss_done, 1)

            def rb(src, pair=4):
                mm(bank(pair, P), ones[:, :], src[:, 0, :], start=True, stop=True)
                return mm(bank(pair + 1), ones[:, :], src[:, 1:CHUNKS, :], start=True, stop=True)

            def norm_rb(n):
                pe.wait_ge(diag_done, n + 1)
                rb(diag).then_inc(rb_done, 1)

            pe.wait_ge(consts_in, 32)
            pe.wait_ge(par_dma, 16 * N_PAR_DMA)
            for i in range(PARAM_TILES):
                m = min(P, N_PARAM - i * P)
                ins = tr(bank(4, m, i * P) if i < 4 else bank(5, m), par_in[0:m, i, :], ident[0:m, 0:m])
            ins.then_inc(par_ps, 1)
            ada_step(0)
            pe.wait_ge(par_done, 1)
            pe.wait_ge(x_dma, 16 * CHUNKS)
            for k in range(KD):
                if k >= 2:
                    pe.wait_ge(xt_done, k - 1)
                b = 4 if k % 2 == 0 else 2
                for c in range(CHUNKS):
                    ins = tr(bank(b, P) if c == 0 else bank(b + 1, P, (c - 1) * P), x_in[:, c, k * P:(k + 1) * P],
                             ident)
                ins.then_inc(xt_ps, 1)
            ss(0)
            for s in range(1, 8):
                ada_step(s)
                ada_turn(s - 1, b=0)
            ada_turn(7, b=0)
            norm_rb(0)

            def att_begin(key):
                u = ATT_USE[key]
                if u >= 2:
                    who, n = ATT_END[u - 2]
                    pe.wait_ge(att_free_act if who == "act" else att_free_dve, n)
                return 4 + 2 * (u % 2)

            def out_first(ks):
                for k in ks:
                    pe.wait_ge(g_ready, G_AT[("rbO", k) if k < 4 else ("pool", k - 4)])
                    if k == OUT_FIRST[0]:
                        begin(T_B, A_B)
                    for i, (w, x) in enumerate(((w_hi, g_hi), (w_hi, g_lo), (w_lo, g_hi))):
                        for cols in HALVES:
                            ins = mm(acc(0)[:, cols], w[0][:, k, :], x[:, k, cols],
                                     start=k == OUT_FIRST[0] and i == 0, stop=k == OUT_FIRST[-1] and i == 2)
                return ins

            for ev in ATT:
                kind = ev[0]
                if kind == "mm":
                    _, t, q = ev
                    if q == 0:
                        begin(t, t)
                    if t == 0 and q == 3:
                        pe.wait_ge(x_spilled, 16)
                    ins = steps(t, t % 2, t % 2, h_hi, h_lo, (2 * q, 2 * q + 1), ready=h_wait(0) if t == 0 else None)
                    if q == 3:
                        ins.then_inc(mm_done, 1)
                    continue
                if kind == "mix":
                    continue
                if kind == "out":
                    out_first(OUT_FIRST[2 * ev[1]:2 * ev[1] + 2])
                    continue
                if kind == "S":
                    _, h, j = ev
                    if j == 0:
                        pe.wait_ge(q_roped, h + 1)
                        pe.wait_ge(k_roped, h + 1)
                        pe.wait_ge(*att_end(("trk", h)))
                    for c in range(2):
                        b = att_begin(ev + (c,))
                        if j == 0:
                            ins = mm(bank(b, P), qz[:, c, 0:P], kT[:, 0:P], start=True, stop=True)
                        else:
                            for half in range(2):
                                k0 = P + half * (KEYS // 2)
                                ins = mm(bank(b, KEYS // 2, 512 - KEYS // 2) if half == 0 else bank(b + 1, KEYS // 2),
                                         qz[:, c, j * P:(j + 1) * P], kT[:, k0:k0 + KEYS // 2], start=True, stop=True)
                        ins.then_inc(att_mm, 1)
                    continue
                b = att_begin(ev)
                if kind in ("rotq", "rotk"):
                    h = ev[1]
                    pe.wait_ge(acc_free_act, 3 * h + (1 if kind == "rotq" else 2))
                    src = q_raw if kind == "rotq" else k_raw
                    ins = mm(bank(b), perm, src[:, S0:S0 + NS], start=True, stop=True)
                elif kind == "trk":
                    h = ev[1]
                    if h == 0:
                        pe.wait_ge(ck_dma, 16)
                    tr(bank(b, P), k_raw[:, 0:P], ident)
                    ins = tr(bank(b, P, P), ck_in[:, h, :], ident)
                elif kind == "trv":
                    pe.wait_ge(acc_free_act, 3 * ev[1] + 3)
                    for c in range(CHUNKS):
                        ins = tr(bank(b, P, 3 * P) if c == 0 else bank(b + 1, P, (c - 1) * P),
                                 v_raw[:, chunk_col(c):chunk_col(c) + P], ident)
                elif kind == "T":
                    _, h, j = ev
                    pe.wait_ge(att_a, 5 * h + j + 1)
                    src = att[j % 2]
                    for c in range(CHUNKS if j else 1):
                        ins = tr(bank(b, P, 3 * P) if c == 0 else bank(b + 1, P, (c - 1) * P),
                                 src[:, c * P:(c + 1) * P], ident)
                elif kind == "PV":
                    _, h, j = ev
                    pe.wait_ge(*att_end(("T", h, j)))
                    pe.wait_ge(*att_end(("trv", h)))
                    if j == 1:
                        pe.wait_ge((cv_dma0, cv_dma1)[h % 2], 16 * (h // 2 + 1))
                    if j == 0:
                        ins = mm(bank(b, P), v_tok[h % 2][:, 0, :], attT[0][:, 0, :], start=True, stop=True)
                    else:
                        for c in range(CHUNKS):
                            ins = mm(bank(b, P), v_tok[h % 2][:, c + 1, :], attT[j % 2][:, c, :], start=c == 0,
                                     stop=c == CHUNKS - 1)
                elif kind == "ssO":
                    h = ev[1]
                    pe.wait_ge(o_sqd, h + 1)
                    for c in range(CHUNKS):
                        ins = mm(bank(b, 1, c), o_sq[:, chunk_col(c):chunk_col(c) + P], ones[:, 0:1], start=True,
                                 stop=True)
                elif kind == "rbO":
                    pe.wait_ge(o_dg, ev[1] + 1)
                    ins = rb(o_diag, b)
                elif kind == "pool":
                    g = ev[1]
                    pe.wait_ge(pmat_in, 16)
                    pe.wait_ge(pool_y, g + 1)
                    for half, cols in enumerate(HALVES):
                        ins = mm(bank(b, HALF, 512 - HALF) if half == 0 else bank(b + 1, W - HALF), pmat[:, g, :],
                                 pooled[:, cols], start=True, stop=True)
                ins.then_inc(att_mm, 1)

            for m in range(8):
                if m == 0:
                    out_first(OUT_FIRST[6:]).then_inc(mm_done, 1)
                else:
                    begin(T_B + m, A_B + m)
                    steps(T_B + m, m % 2, m % 2, g_hi, g_lo, range(KD)).then_inc(mm_done, 1)
                for s in ADA_B[m]:
                    ada_step(s)
                    if s > 8:
                        ada_turn(s - 1)
            ada_turn(19)
            ss(1)
            norm_rb(1)

            def ffn(l, t0, a0):
                n_ = 2 * l + 1
                for p, (m0, n) in enumerate(PARTS):
                    tp, ap = t0 + 2 * m0 + 8 * p, a0 + 2 * m0 + 8 * p
                    s0 = ADA_F + 16 * p

                    def pair(i, peeled, ada):
                        for half in range(2):
                            t = tp + 2 * i + half
                            pe.wait_ge(w_split, t + 1)
                            pe.wait_ge(acc_free_dve, dve_accs(ap) + 2 * i + half - 2)
                            steps(t, half, half, h_hi, h_lo, range(KD),
                                  ready=h_wait(n_) if peeled and p == 0 and half == 0 else None
                                  ).then_inc(mm_done, 1)
                            if ada:
                                s = 2 * i + (s0 + half)
                                ada_step(s, half)
                                if not (peeled and s == ADA_F):
                                    ada_turn(2 * i + (s0 + half - 1), 1 - half)

                    n_ada = ADA_PAIRS[p] if l == 0 else 0
                    pair(0, True, n_ada > 0)
                    if n_ada:
                        with pe.Fori(1, n_ada) as i:
                            pair(i, False, True)
                    if p == 1 and n_ada:
                        ada_turn(47)
                    if max(n_ada, 1) < n:
                        with pe.Fori(max(n_ada, 1), n) as i:
                            pair(i, False, False)
                    td, ad = tp + 2 * n, ap + 2 * n

                    def down(i, peeled):
                        for half in range(2):
                            t = td + 2 * i + half
                            pe.wait_ge(w_split, t + 1)
                            pe.wait_ge(acc_free_dve, dve_accs(ad) + 2 * i + half - 2)
                            ready = (lambda k: pe.wait_ge(f_ready, FT * l + m0 + k + 1)) if peeled and half == 0 else None
                            steps(t, half, half, g_hi, g_lo, range(n), n=n, ready=ready).then_inc(mm_done, 1)

                    down(0, True)
                    with pe.Fori(1, 4) as i:
                        down(i, False)
                ss(n_ + 1)

            ffn(0, T_F0, T_F0)
            norm_rb(2)

            def y_part(k):
                pe.wait_ge(y_ready, k + 1)
                part = k // KD
                for half in range(2):
                    if k % KD == 0:
                        pe.wait_ge(w_split, T_O + 2 * part + half + 1)
                    if k == 0:
                        pe.wait_ge(*acc_free(A_O + half - 2))
                    ins = steps(None, half, half, y_hi, y_lo, (k % KD,), k_of=lambda _: k, first=part == 0,
                                last=part == 1)
                    if k % KD == KD - 1:
                        ins.then_inc(mm_done, 1)

            def ssd_begin(key):
                u = SSD_USE[key]
                if u >= 4:
                    who, n = SSD_END[u - 4]
                    pe.wait_ge(ssd_free_act if who == "act" else ssd_free_dve, n)
                return 4 + u % 4

            for ev in SSD:
                kind = ev[0]
                if kind == "mm":
                    _, e, q = ev
                    t = T_E + e
                    if q == 0:
                        begin(t, t)
                    for k in range(4 * q, 4 * q + 4):
                        if e == 0:
                            pe.wait_ge(*h_done(2, k))
                        ins = steps(t, e % 2, e % 2, h_hi, h_lo, (k,))
                        if e == 0:
                            for i, (w, x) in enumerate(((wdt_hi, h_hi), (wdt_hi, h_lo), (wdt_lo, h_hi))):
                                for half, cols in enumerate(HALVES):
                                    out = bank(6, HALF, 512 - HALF) if half == 0 else bank(7, W - HALF)
                                    raw_dt = mm(out[0:64, :], w[:, k, :], x[:, k, cols], start=k == 0 and i == 0,
                                                stop=k == KD - 1 and i == 2)
                    if q == 1:
                        ins.then_inc(mm_done, 1)
                    if (e, q) == (0, 1):
                        raw_dt.then_inc(dtT_mm, 1)
                    continue
                if kind == "dtT":
                    pe.wait_ge(dtT_copied, 1)
                    b = ssd_begin(ev)
                    for c in range(CHUNKS):
                        ins = tr(bank(b, 64, 64 * c), dt_T[:, chunk_col(c):chunk_col(c) + P], ident[0:64, 0:64])
                    ins.then_inc(ssd_mm, 1)
                    continue
                if kind == "sum":
                    pe.wait_ge(da_done, 1)
                    b = ssd_begin(ev + (0,))
                    for c in range(CHUNKS):
                        for d_, m_ in enumerate((m_le, m_ge)):
                            ins = mm(bank(b, 32, 64 * c + 32 * d_), m_, da3[:, c, 32 * d_:32 * d_ + 32], start=True,
                                     stop=True)
                    ins.then_inc(ssd_mm, 1)
                    b = ssd_begin(ev + (1,))
                    mm(bank(b, 320), ones[:, :], da, start=True, stop=True).then_inc(ssd_mm, 1)
                    continue
                if kind == "acsT":
                    pe.wait_ge(acs_done, 1)
                    for i in range(2):
                        b = ssd_begin(ev + (i,))
                        for c in (range(4) if i == 0 else (4,)):
                            ins = tr(bank(b, P, P * (c % 4))[0:64, :], acs[:, c, :], ident)
                        ins.then_inc(ssd_mm, 1)
                    continue
                g = ev[1]
                if kind == "yout":
                    y_part(ev[2])
                elif kind == "trB":
                    pe.wait_ge(conv_silu, 6 * g + 1)
                    for i in range(2):
                        b = ssd_begin(ev + (i,))
                        for c in (range(1, CHUNKS) if i == 0 else (0,)):
                            ins = tr(bank(b, P, (c - 1) * P if i == 0 else 0),
                                     bT[g % 2][:, chunk_col(c):chunk_col(c) + P], ident)
                        ins.then_inc(ssd_mm, 1)
                elif kind == "trx":
                    j = ev[2]
                    pe.wait_ge(conv_silu, 6 * g + 3 + j)
                    for i in range(2):
                        b = ssd_begin(ev + (i,))
                        for c in (range(1, CHUNKS) if i == 0 else (0,)):
                            ins = tr(bank(b, P, (c - 1) * P if i == 0 else 0),
                                     cx[:, chunk_col(c):chunk_col(c) + P], ident)
                        ins.then_inc(ssd_mm, 1)
                elif kind == "init":
                    d_ = ev[2]
                    pe.wait_ge(st_in_dma, 32 * (g + 1))
                    b = ssd_begin(ev)
                    for q_ in range(4):
                        ins = tr(bank(b, P, q_ * P), st_in[:, d_, q_, :], ident)
                    ins.then_inc(ssd_mm, 1)
                elif kind in ("csb", "csf"):
                    pe.wait_ge(xw_done, CS_AT[ev] + 1)
                    pe.wait_ge(*ssd_end(("trB", g, 1)))
                    b = ssd_begin(ev)
                    mm(bank(b), b_tok[g % 2][:, ev[2], :], xw[CS_AT[ev] % 2][:, :], start=True, stop=True
                       ).then_inc(ssd_mm, 1)
                elif kind == "cb":
                    pe.wait_ge(conv_silu, 6 * g + 2)
                    b = ssd_begin(ev)
                    cols = slice(chunk_col(ev[2]), chunk_col(ev[2]) + P)
                    mm(bank(b, P), bT[g % 2][:, cols], cT[g % 2][:, cols], start=True, stop=True
                       ).then_inc(ssd_mm, 1)
                elif kind == "yd":
                    b = ssd_begin(ev)
                    for d_ in range(2):
                        pe.wait_ge(W_done, 2 * (CHUNKS * g + ev[2]) + d_ + 1)
                        for r in range(GH):
                            ins = mm(bank(b, HD, r * HD), R[:, d_, r, :], xdt[:, d_, r * HD:(r + 1) * HD],
                                     start=(d_, r) == (0, 0), stop=(d_, r) == (1, GH - 1), skip_group_check=True)
                        ins.then_inc((R_used, ssd_mm)[d_], 1)
                elif kind == "yo":
                    c = ev[2]
                    pe.wait_ge(*ssd_end(("init", g, 1)))
                    pe.wait_ge(st_done, CS_AT[("csb", g, 0) if c < 2 else ("csf", g, c - 1)] + 1)
                    cols = slice(chunk_col(c), chunk_col(c) + P)
                    for d_ in range(2):
                        b = ssd_begin(ev + (d_,))
                        src = st_f[c % 2][:, :] if d_ == 0 else st_b[:, c - 1, :]
                        mm(bank(b), cT[g % 2][:, cols], src, start=True, stop=True).then_inc(ssd_mm, 1)
                elif kind == "yT":
                    pe.wait_ge(y_done, 5 * g + ev[2] + 1)
                    b = ssd_begin(ev)
                    for q_ in range(4):
                        ins = tr(bank(b, P, q_ * P), y1[ev[2] % 2][:, q_ * P:(q_ + 1) * P], ident)
                    ins.then_inc(ssd_mm, 1)
                elif kind == "stT":
                    pe.wait_ge(st_done, CS_AT[("csf", g, 0)] + 1)
                    for d_ in range(2):
                        b = ssd_begin(ev + (d_,))
                        for q_ in range(4):
                            ins = tr(bank(b, P, q_ * P), st_p[:, d_, q_ * P:(q_ + 1) * P], ident)
                        ins.then_inc(ssd_mm, 1)

            def y_rb():
                pe.wait_ge(yr_dg, 1)
                rb(diag).then_inc(yr_rb, 1)

            def so_pair(i):
                for part in range(2):
                    for half in range(2):
                        pe.wait_ge(w_split, 4 * i + (T_O + 2 * part + half + 1))
                        if part == 0:
                            pe.wait_ge(acc_free_dve, 2 * i + (half + dve_accs(A_O) - 2))
                        steps(None, half, half, y_hi, y_lo, range(KD), k_of=lambda k: 8 * part + k, first=part == 0,
                              last=part == 1).then_inc(mm_done, 1)

            for k in range(12, 16):
                y_part(k)
            pe.wait_ge(y_added, 15)
            for c in range(CHUNKS):
                ins = mm(bank(6, 1, c), y_sums[:, chunk_col(c):chunk_col(c) + P], ones[:, 0:1], start=True, stop=True)
            ins.then_inc(y_ss, 1)
            y_rb()
            with pe.Fori(1, 4) as i:
                so_pair(i)
            ss(3)
            norm_rb(3)
            ffn(1, T_F1, A_F1)

            for c in range(CHUNKS):
                if c >= 2:
                    pe.wait_ge(fin_y, c - 1)
                b = 4 if c % 2 == 0 else 2
                for k in range(KD):
                    ins = tr(bank(b + k // 4, P, (k % 4) * P), xT[:, k, chunk_col(c):chunk_col(c) + P], ident)
                ins.then_inc(fin_ps, 1)

        @block.scalar
        def _(act):
            A_ = nc.scalar.activation
            step = Steps(act, act_step)
            SCALE = HD ** -0.5

            act.wait_ge(par_done, 1)
            for s_, name in enumerate(("c_ctx", "c")):
                ins = A_(svec[:, :, s_], par[:, PARAM_AT[name]:PARAM_AT[name] + KD], ACT.Silu)
            ins.then_inc(svec_done, 1)
            act.wait_ge(svec_done, 1)
            A_(svec4[:, :, 0:2], svec[:, :, :], ACT.Copy).then_inc(svec_done, 1)

            def ada_high(s, half=None):
                raw_, hi, _, _ = ada_bufs(s, half)
                act.wait_ge(*ada_landed(s, half))
                if not (isinstance(s, int) and s < 2):
                    act.wait_ge(ada_mm, s - 1)
                A_(hi[:, :, :], raw_[:, :, :], ACT.Copy).then_inc(ada_hi_done, 1)

            ada_high(0)
            act.wait_ge(memset_done, 1)
            act.wait_ge(ones_done, 1)
            for k in range(KD):
                act.wait_ge(xt_ps, k + 1)
                b = 4 if k % 2 == 0 else 2
                A_(xT[:, k, 0:NP_], bank(b, P), ACT.Copy)
                A_(xT[:, k, S0:S0 + NS], bank(b + 1), ACT.Copy).then_inc(xt_done, 1)
                act.wait_ge(xt_done, k + 1)
                if k >= 3:
                    act.wait_ge(sq_added, k - 2)
                A_(sq[k % 2][:, :] if k else sums(0), xT[:, k, :], ACT.Square).then_inc(sq_ready, 1)

            def norm(n):
                act.wait_ge(ms_done, n + 1)
                A_(small[:, 8:13], small[:, 0:5], ACT.Sqrt).then_inc(root_done, 1)
                l, j = n // 2, 3 * (n % 2)
                for k in range(KD):
                    act.wait_ge(t_done, 8 * n + k + 1)
                    for s_, cols in enumerate((slice(0, NP_), slice(S0, S0 + NS))):
                        ins = A_(h_hi[:, k, cols], tn[k % 2][:, cols], ACT.Identity, bias=modc(l, j, k, s_))
                    ins.then_inc(h_hi_done, 1)

            for s in range(1, 8):
                ada_high(s)
            act.wait_ge(wdt_in, 16)
            A_(wdt_hi[:, :, :], wdt[:, :, :], ACT.Copy).then_inc(wdt_hi_done, 1)
            norm(0)
            act.wait_ge(bcast_in, 64)
            A_(a_bc[:, :], a_bc[:, :], ACT.Exp).then_inc(abc_done, 1)
            act.wait_ge(lam_s, 1)
            A_(small[:, 18:20], small[:, 16:18], ACT.Exp).then_inc(lam_e, 1)

            def att_wait(key):
                act.wait_ge(att_mm, ATT_USE[key] + 1)
                return 4 + 2 * (ATT_USE[key] % 2)

            for ev in ATT:
                kind = ev[0]
                if kind == "mm":
                    _, t, q = ev
                    if q == 3 and t < 12:
                        h, i = divmod(t, 3)
                        act.wait_ge(mm_done, t + 1)
                        if h:
                            if i == 0:
                                act.wait_ge(q_roped, h)
                            elif i == 1:
                                act.wait_ge(k_roped, h)
                                act.wait_ge(*att_end(("trk", h - 1)))
                            else:
                                act.wait_ge(*att_end(("trv", h - 1)))
                        A_((q_raw, k_raw, v_raw)[i][:, :], acc(t % 2), ACT.Copy).then_inc(acc_free_act, 1)
                    continue
                if kind == "trk":
                    h = ev[1]
                    b = att_wait(ev)
                    if h:
                        act.wait_ge(k_stored, 16 * h)
                    A_(kT[:, NP_ + NS:], bank(b, P, P), ACT.Copy)
                    A_(k_out[:, :], bank(b, P), ACT.Copy).then_inc(att_free_act, 1)
                elif kind == "trv":
                    h = ev[1]
                    b = att_wait(ev)
                    if h >= 2:
                        act.wait_ge(v_stored, 16 * (h - 1))
                    A_(v_tok[h % 2][:, 0:CHUNKS, :], bank(b, CHUNKS * P, 3 * P), ACT.Copy).then_inc(att_free_act, 1)
                elif kind == "S":
                    _, h, j = ev
                    n = 5 * h + j
                    for c in range(2):
                        b = att_wait(ev + (c,))
                        act.wait_ge(smax, 2 * n + c + 1)
                        if n >= 2:
                            act.wait_ge(att_a, n - 1)
                        src = bank(b, P) if j == 0 else bank(b, KEYS, 512 - KEYS // 2)
                        i = 24 + 2 * (j % 2) + c
                        A_(prob[j % 2][:, c, 0:P if j == 0 else KEYS], src, ACT.Exp, bias=small[:, i:i + 1],
                           scale=SCALE, accum_out=small[:, i + 4:i + 5]).then_inc(att_free_act, 1)
                elif kind == "T":
                    _, h, j = ev
                    b = att_wait(ev)
                    n = CHUNKS if j else 1
                    A_(attT[j % 2][:, 0:n, :], bank(b, n * P, 3 * P), ACT.Copy).then_inc(att_free_act, 1)
                elif kind == "PV":
                    _, h, j = ev
                    b = att_wait(ev)
                    if j == 0 and h:
                        act.wait_ge(*att_end(("rbO", h - 1)))
                    col = chunk_col(j)
                    A_(o_sb[:, col:col + P], bank(b, P), ACT.Copy).then_inc(att_free_act, 1)
                    if j == 4:
                        act.wait_ge(*att_end(ev))
                        A_(o_sq[:, 0:NP_], o_sb[:, 0:NP_], ACT.Square)
                        A_(o_sq[:, S0:S0 + NS], o_sb[:, S0:S0 + NS], ACT.Square).then_inc(o_sqd, 1)
                elif kind == "ssO":
                    act.wait_ge(*att_end(ev))
                    A_(small[:, 40:45], small[:, 32:37], ACT.Sqrt).then_inc(o_root, 1)
                elif kind == "rbO":
                    h = ev[1]
                    act.wait_ge(*att_end(ev))
                    A_(g_hi[:, h, :], o_nrm[:, :], ACT.Copy).then_inc(o_hi, 1)
                elif kind == "pool":
                    g = ev[1]
                    act.wait_ge(*att_end(ev))
                    A_(g_hi[:, 4 + g, :], pmul[:, :], ACT.Copy).then_inc(pool_hi, 1)

            def square(n, m, free, buf):
                act.wait_ge(*free)
                if isinstance(m, int) and m == 0:
                    act.wait_ge(ss_done, n)
                    buf = sums(n)
                else:
                    act.wait_ge(sq_added, 7 * n if isinstance(m, int) and m < 2 else m + (7 * n - 2))
                A_(buf, xT_at(m), ACT.Square).then_inc(sq_ready, 1)

            def xT_at(m):
                return xT[:, m, :] if isinstance(m, int) else xT[:, bass.ds(m, 1), :]

            act.wait_ge(g_ready, 8)
            for m in range(8):
                for s in ADA_B[m]:
                    ada_high(s)
                if m == 0:
                    act.wait_ge(x_back, 16)
                square(1, m, (acc_free_dve, dve_accs(A_B + m)), sq[m % 2][:, :])
            norm(1)

            def param_at(row):
                return par[:, bass.ds(row, 1)] if not isinstance(row, int) else par[:, row:row + 1]

            def ffn(l, t0, a0):
                wc, bcol = PARAM_AT["ffn_conv_w"] + l * 132, PARAM_AT["ffn_conv_b"] + l * 44
                n_ = 2 * l + 1
                for p, (m0, n) in enumerate(PARTS):
                    tp, ap = t0 + 2 * m0 + 8 * p, a0 + 2 * m0 + 8 * p
                    f0 = FT * l + m0

                    def pair(i, ada):
                        for half, buf in enumerate((cg, cv)):
                            if ada:
                                ada_high(2 * i + (ADA_F + 16 * p + half), half)
                            act.wait_ge(mm_done, 2 * i + (tp + half + 1))
                            m = i + (m0 + FT * half)
                            if half == 0:
                                if isinstance(i, int) and f0 == 0:
                                    pass
                                else:
                                    act.wait_ge(ffn_silu, i + f0)
                            elif not (isinstance(i, int) and f0 == 0):
                                act.wait_ge(hm_done, i + f0)
                            A_(buf[:, :], acc(half), ACT.Identity, bias=param_at(m + bcol),
                               scale=param_at(m + (wc + 44))).then_inc(ffn_id, 1)
                        act.wait_ge(acc_free_dve, 2 * i + dve_accs(ap))
                        A_(sg[:, :], cg[:, :], ACT.Silu).then_inc(ffn_silu, 1)
                        act.wait_ge(hm_done, i + (f0 + 1))
                        dst = g_hi[:, i, :] if isinstance(i, int) else g_hi[:, bass.ds(i, 1), :]
                        A_(dst, hm[:, :], ACT.Copy).then_inc(ffn_hi, 1)

                    n_ada = ADA_PAIRS[p] if l == 0 else 0
                    pair(0, n_ada > 0)
                    for lo_, hi_ in ((1, n_ada), (max(n_ada, 1), n)):
                        if lo_ < hi_:
                            with act.Fori(lo_, hi_) as i:
                                pair(i, lo_ < n_ada)
                    if p == 2:
                        ad = ap + 2 * n

                        def down(i):
                            for half in range(2):
                                square(n_ + 1, 2 * i + half, (acc_free_dve, 2 * i + (dve_accs(ad) + half)), sq[half][:, :])

                        down(0)
                        with act.Fori(1, 4) as i:
                            down(i)

            ffn(0, T_F0, T_F0)
            norm(2)

            act.wait_ge(dtT_mm, 1)
            A_(dt_T[:, :], bank(6, W, 512 - HALF)[0:64, :], ACT.Copy).then_inc(dtT_copied, 1)
            act.wait_ge(x_spilled, 32)

            def ssd_wait(key):
                act.wait_ge(ssd_mm, SSD_USE[key] + 1)
                return 4 + SSD_USE[key] % 4

            def conv_row(name, i):
                return par[:, PARAM_AT[name] + i:PARAM_AT[name] + i + 1]

            def y_high(k):
                if k == 0:
                    act.wait_ge(mm_done, T_E + 40)
                act.wait_ge(*ssd_end(("yT", k // 4, 4)))
                A_(y_hi[:, k, :], yg[:, k, :], ACT.Copy, scale=pcol("ssd_norm_g", k)).then_inc(yn_hi, 1)
                if k >= 3:
                    act.wait_ge(y_added, k - 2)
                A_(y_squares(k), yg[:, k, :], ACT.Square).then_inc(y_sqd, 1)

            def conv_buf(e):
                g, i = divmod(e, 10)
                return bT[g % 2] if i == 0 else cT[g % 2] if i == 1 else cx

            for ev in SSD:
                kind = ev[0]
                if kind == "mm":
                    _, e, q = ev
                    if q == 0:
                        continue
                    what, m = ssd_tile(e)
                    g, i = divmod(e, 10)
                    act.wait_ge(mm_done, T_E + e + 1)
                    if what == "z":
                        A_(yg[:, m, :], acc(e % 2), ACT.Silu).then_inc(acc_free_act, 1)
                        continue
                    if i < 2 and g >= 2:
                        act.wait_ge(y_done, 5 * (g - 1))
                    if i == 2 and g:
                        act.wait_ge(*ssd_end(("trx", g - 1, 3, 1)))
                    if i > 2:
                        act.wait_ge(*ssd_end(("trx", g, i - 3, 1)))
                    buf = conv_buf(e)
                    A_(buf[:, :], acc(e % 2), ACT.Identity, bias=conv_row("ssd_conv_b", m),
                       scale=conv_row("ssd_conv_w", 24 + m)).then_inc(conv_id, 1)
                    act.wait_ge(acc_free_dve, dve_accs(A_E + e))
                    A_(buf[:, :], buf[:, :], ACT.Silu).then_inc(conv_silu, 1)
                    continue
                g = ev[1]
                if kind == "ynorm":
                    y_high(ev[2])
                elif kind == "dtT":
                    act.wait_ge(dt_xb, 1)
                    step(A_(dt_e, dt_x, ACT.Abs))
                    step.wait()
                    A_(dt_e, dt_e, ACT.Exp, scale=-1.0).then_inc(dt_exp, 1)
                elif kind == "acsT":
                    act.wait_ge(tot_w, 1)
                    A_(eacs[:, :, :], acs[:, :, :], ACT.Exp)
                    A_(dec[:, :, :], dec[:, :, :], ACT.Exp)
                    A_(wst[:, :, :], wst[:, :, :], ACT.Exp).then_inc(acs_exp, 1)
                    for i in range(2):
                        b = ssd_wait(ev + (i,))
                        A_(acsT[:, 512 * i:512 + 128 * i], bank(b, 512 - 384 * i)[0:64, :], ACT.Copy
                           ).then_inc(ssd_free_act, 1)
                elif kind in ("trB", "trx"):
                    for i in range(2):
                        b = ssd_wait(ev + (i,))
                        cs = slice(1, CHUNKS) if i == 0 else slice(0, 1)
                        dst = b_tok[g % 2][:, cs, :] if kind == "trB" else \
                            x_tok[g % 2][:, cs, ev[2] * P:(ev[2] + 1) * P]
                        if g >= 2 and i == 0 and (kind == "trB" or ev[2] == 0):
                            act.wait_ge(y_done, 5 * (g - 1))
                            act.wait_ge(st_done, CS_AT[("csf", g - 2, 3)] + 1)
                        A_(dst, bank(b, P * (4 if i == 0 else 1)).rearrange("p (c n) -> p c n", n=P), ACT.Copy
                           ).then_inc(ssd_free_act, 1)
                elif kind == "init":
                    d_ = ev[2]
                    b = ssd_wait(ev)
                    if g:
                        act.wait_ge(ssd_mm, SSD_USE[("yo", g - 1, 4, 1)] + 1)
                    A_(st_f[1][:, :] if d_ == 0 else st_b[:, 3, :], bank(b), ACT.Copy).then_inc(ssd_free_act, 1)
                elif kind == "cb":
                    n = 5 * g + ev[2]
                    c = ev[2]
                    for d_ in range(2):
                        act.wait_ge(R_in[d_], 16 * (n + 1))
                        for r in range(GH):
                            i = 32 * d_ + GH * g + r
                            ins = A_(R[:, d_, r, :], R[:, d_, r, :], ACT.Relu, bias=acs[:, c, i:i + 1], scale=-1.0)
                        step(ins)
                        step.wait()
                        A_(R[:, d_, :, :], R[:, d_, :, :], ACT.Exp, scale=-1.0).then_inc(seg_exp, 1)
                elif kind == "stT":
                    for d_ in range(2):
                        b = ssd_wait(ev + (d_,))
                        if g or d_:
                            act.wait_ge(st_stored, 16 * (2 * g + d_))
                        A_(st_out[:, :, :], bank(b).rearrange("p (q n) -> p q n", q=4), ACT.Copy
                           ).then_inc(ssd_free_act, 1)

            for k in range(12, 16):
                y_high(k)
            act.wait_ge(yr_ms, 1)
            A_(small[:, 8:13], small[:, 0:5], ACT.Sqrt).then_inc(yr_root, 1)

            def so_squares(i):
                for half in range(2):
                    square(3, 2 * i + half, (so_x, 2 * i + (half + 1)), sq[half][:, :])

            so_squares(0)
            with act.Fori(1, 4) as i:
                so_squares(i)
            norm(3)
            ffn(1, T_F1, A_F1)
            act.wait_ge(ms_done, 5)
            A_(small[:, 8:13], small[:, 0:5], ACT.Sqrt).then_inc(root_done, 1)

        @block.vector
        def _(dve):
            tt, ts, stt, cp = nc.vector.tensor_tensor, nc.vector.tensor_scalar, nc.vector.scalar_tensor_tensor, \
                nc.vector.tensor_copy
            step = Steps(dve, dve_step)
            RANGES = ((0, slice(0, NP_)), (1, slice(S0, S0 + NS)))
            f32 = lambda ap: ap.bitcast(F32)

            step(nc.vector.memset(xT[:, :, NP_:S0], 0.0))
            step(nc.vector.memset(xT[:, :, W - 1:W], 0.0))

            def h_zeros():
                for t_ in (h_hi, h_lo):
                    step(nc.vector.memset(t_[:, :, NP_:S0].bitcast(F32), 0.0))
                    step(nc.vector.memset(t_[:, :, W - 1:W].bitcast(F32), 0.0))
                step.wait()

            nc.vector.memset(small[:, 63:64], 0.0).then_inc(memset_done, 1)
            dve.wait_ge(par_ps, 1)
            step(cp(par[:, 0:512], bank(4)))
            step.wait()
            cp(par[:, 512:N_PARAM], bank(5, N_PARAM - 512)).then_inc(par_done, 1)

            def ada_low(s, half=None):
                raw_, hi, lo, _ = ada_bufs(s, half)
                dve.wait_ge(ada_hi_done, s + 1)
                tt(lo[:, :, :], raw_[:, :, :], f32(hi[:, :, :]), ALU.subtract).then_inc(ada_split, 1)

            def ada_row_out(s, half=None):
                dve.wait_ge(ada_mm, s + 1)
                cp(ada_bufs(s, half)[3][0:4, 0:2 * P], bank(6, 2 * P)[0:4, :]).then_inc(ada_rows, 1)

            def mod_evac(s, b=5):
                dve.wait_ge(ada_cols, s + 1)
                if isinstance(s, int):
                    dst, bias = mod[:, 2 * s:2 * s + 2, :], par[:, PARAM_AT["ada_b"] + 2 * s:PARAM_AT["ada_b"] + 2 * s + 2]
                else:
                    dst, bias = mod[:, bass.ds(2 * s, 2), :], par[:, bass.ds(2 * s + PARAM_AT["ada_b"], 2)]
                tt(dst, bank(b, 4).rearrange("p (a b) -> p a b", b=2), bc(bias, 2, 2), ALU.add).then_inc(mod_done, 1)

            def gains(n, after):
                dve.wait_ge(mod_done, after)
                l, j = n // 2, 1 + 3 * (n % 2)
                name = "norm_mix_g" if n % 2 == 0 else "norm_ffn_g"
                g0 = PARAM_AT[name] + 8 * l
                step(stt(gain1[:, n, :, :], mod[:, l * 48 + j * 8:l * 48 + j * 8 + 8, :], 1.0,
                         bc(par[:, g0:g0 + 8], 2, 2), ALU.add, ALU.mult))

            def inv_root(n):
                dve.wait_ge(ss_done, n + 1)
                ts(small[:, 0:5], bank(7, 5), 1.0 / D, EPS, ALU.mult, ALU.add).then_inc(ms_done, 1)
                dve.wait_ge(root_done, n + 1)
                step(nc.vector.reciprocal(small[:, 48:53], small[:, 8:13]))
                step.wait()

            def add_square(n, m, buf):
                dve.wait_ge(sq_ready, m + (8 * n + 1))
                if not (isinstance(m, int) and m == 1):
                    dve.wait_ge(sq_added, m + (7 * n - 1))
                tt(sums(n), sums(n), buf[:, :], ALU.add).then_inc(sq_added, 1)

            def norm(n):
                inv_root(n)
                if n in (0, 3):
                    h_zeros()
                tt(diag[:, :, :], bc(ident, 1, CHUNKS), bc(small[:, 48:53], 2, P), ALU.mult).then_inc(diag_done, 1)
                dve.wait_ge(rb_done, n + 1)
                l, j = n // 2, 3 * (n % 2)

                def low(k):
                    dve.wait_ge(h_hi_done, 8 * n + k + 1)
                    for s_, cols in RANGES:
                        ins = stt(h_lo[:, k, cols], tn[k % 2][:, cols], modc(l, j, k, s_), f32(h_hi[:, k, cols]),
                                  ALU.add, ALU.subtract)
                        (step(ins) if s_ == 0 else ins.then_inc(h_ready, 1))

                for k in range(KD):
                    if k >= 2:
                        dve.wait_ge(*h_done(n, k - 2))
                    for s_, cols in RANGES:
                        rbp = bank(4, P) if s_ == 0 else bank(5)
                        ins = stt(tn[k % 2][:, cols], xT[:, k, cols], gain1[:, n, k, s_:s_ + 1], rbp, ALU.mult,
                                  ALU.mult)
                        (step(ins) if s_ == 0 else ins.then_inc(t_done, 1))
                    if k:
                        low(k - 1)
                low(KD - 1)

            dve.wait_ge(svec_done, 2)
            step(tt(svec4[:, :, 2:4], svec[:, :, :], f32(svec4[:, :, 0:2]), ALU.subtract))
            ada_low(0)
            ada_row_out(0)
            for k in range(1, KD):
                add_square(0, k, sq[k % 2])
            ada_low(1)
            dve.wait_ge(bcast_in, 64)
            step(tt(lam_in[:, 0, :], lam_in[:, 0, :], lam_in[:, 1, :], ALU.mult))
            step(tt(lam_in[:, 2, :], lam_in[:, 2, :], lam_in[:, 3, :], ALU.mult))
            step.wait()
            step(nc.vector.tensor_reduce(small[:, 16:17], lam_in[:, 0, :], AXX, ALU.add))
            nc.vector.tensor_reduce(small[:, 17:18], lam_in[:, 2, :], AXX, ALU.add).then_inc(lam_s, 1)
            for s in range(1, 8):
                if s < 7:
                    ada_low(s + 1)
                ada_row_out(s)
                mod_evac(s - 1, 0)
            mod_evac(7, 0)
            dve.wait_ge(wdt_hi_done, 1)
            step(tt(wdt_lo[:, :, :], wdt[:, :, :], f32(wdt_hi[:, :, :]), ALU.subtract))
            gains(0, 8)
            step(ts(small[:, 22:23], pcol("att_subln_g"), 1.0 - LAM_INIT, None, ALU.mult))
            step.wait()
            norm(0)
            dve.wait_ge(abc_done, 1)
            step(ts(a_bc[:, :], a_bc[:, :], -1.0, None, ALU.mult))
            dve.wait_ge(lam_e, 1)
            step(tt(small[:, 20:21], small[:, 19:20], small[:, 18:19], ALU.subtract))
            step.wait()
            step(ts(small[:, 21:22], small[:, 20:21], -LAM_INIT, None, ALU.add))
            step.wait()

            dve.wait_ge(x_spilled, 16)
            for t_ in (pb[0], pb[1], pb[2]):
                step(nc.vector.memset(t_[:, :], 0.0))
            step(nc.vector.memset(qz[0:64, 1, :], 0.0))
            step(nc.vector.memset(qz[64:128, 0, :], 0.0))
            for t_ in (pooled, o_nrm):
                step(nc.vector.memset(t_[:, NP_:S0], 0.0))
                step(nc.vector.memset(t_[:, W - 1:W], 0.0))
            step.wait()

            def att_wait(key):
                dve.wait_ge(att_mm, ATT_USE[key] + 1)
                return 4 + 2 * (ATT_USE[key] % 2)

            t_before = {}
            for ev in ATT:
                kind = ev[0]
                if kind == "mm":
                    _, t, q = ev
                    if q != 3:
                        continue
                    if t >= 12:
                        g = t - 12
                        dve.wait_ge(mm_done, t + 1)
                        src = acc(t % 2)
                        if g:
                            step.wait()
                        step(cp(pb[0][:, 8:8 + NP_], src[:, 0:NP_]))
                        cp(pb[0][:, 152:152 + NS], src[:, S0:S0 + NS]).then_inc(acc_free_dve, 1)
                        dve.wait_ge(acc_free_dve, dve_accs(t))
                        s_, lo_ = pb[0], 0
                        for d_ in range(g + 1):
                            r = 1 << d_ >> 1
                            nlo = lo_ + max(r, 1)
                            nhi = 672 - (0 if d_ == 0 else nlo - 1)
                            dst = pb[1 + d_ % 2]
                            a0_, b0_ = (-1, 0) if d_ == 0 else (-r, r)
                            step(tt(dst[:, nlo:nhi], s_[:, nlo + a0_:nhi + a0_], s_[:, nlo + b0_:nhi + b0_], ALU.add))
                            step.wait()
                            s_, lo_ = dst, nlo
                        dve.wait_ge(inv_in, 16 * (g + 1))
                        if g:
                            dve.wait_ge(att_mm, ATT_USE[("pool", g - 1)] + 1)
                        step(tt(pooled[:, 0:NP_], s_[:, 8:8 + NP_], inv_n[:, 0:NP_], ALU.mult))
                        step(tt(pooled[:, S0:S0 + NS], s_[:, 152:152 + NS], inv_n[:, NP_:], ALU.mult))
                        step.wait()
                        step(tt(pooled[:, 0:NP_], pooled[:, 0:NP_], pb[0][:, 8:8 + NP_], ALU.subtract))
                        tt(pooled[:, S0:S0 + NS], pooled[:, S0:S0 + NS], pb[0][:, 152:152 + NS], ALU.subtract
                           ).then_inc(pool_y, 1)
                        dve.wait_ge(pool_y, g + 1)
                    continue
                if kind in ("rotq", "rotk"):
                    h = ev[1]
                    b = att_wait(ev)
                    if h == 0:
                        dve.wait_ge(rope_in, 16)
                    src = q_raw if kind == "rotq" else k_raw
                    sam = src[:, S0:S0 + NS]
                    step.wait()
                    tt(rtmp, bank(b), rope[:, 1, :], ALU.mult).then_inc(att_free_dve, 1)
                    step(tt(sam, sam, rope[:, 0, :], ALU.mult))
                    if kind == "rotq":
                        step(cp(qz[0:64, 0, 0:P], src[0:64, 0:P]))
                        step(cp(qz[64:128, 1, 0:P], src[64:128, 0:P]))
                        step.wait()
                        step(tt(qz[0:64, 0, P:], sam[0:64, :], rtmp[0:64, :], ALU.add))
                        step(tt(qz[64:128, 1, P:], sam[64:128, :], rtmp[64:128, :], ALU.add))
                        step.wait()
                        nc.vector.memset(small[:, 62:63], 0.0).then_inc(q_roped, 1)
                    else:
                        dve.wait_ge(att_mm, ATT_USE[("trk", h)] + 1)
                        step(cp(kT[:, 0:P], src[:, 0:P]))
                        step.wait()
                        step(tt(kT[:, P:P + NS], sam, rtmp, ALU.add))
                        step.wait()
                        nc.vector.memset(small[:, 61:62], 0.0).then_inc(k_roped, 1)
                elif kind == "S":
                    _, h, j = ev
                    for c in range(2):
                        b = att_wait(ev + (c,))
                        src = bank(b, P) if j == 0 else bank(b, KEYS, 512 - KEYS // 2)
                        i = 24 + 2 * (j % 2) + c
                        step(nc.vector.tensor_reduce(small[:, 54 + c:55 + c], src, AXX, ALU.max))
                        step.wait()
                        ts(small[:, i:i + 1], small[:, 54 + c:55 + c], -HD ** -0.5, None, ALU.mult
                           ).then_inc(smax, 1)
                elif kind == "mix":
                    _, h, j = ev
                    n = P if j == 0 else KEYS
                    i = 28 + 2 * (j % 2)
                    dve.wait_ge(*att_end(("S", h, j, 1)))
                    step(nc.vector.reciprocal(small[:, 56:58], small[:, i:i + 2]))
                    step.wait()
                    step(tt(small[:, 58:59], small[:, 57:58], small[:, 21:22], ALU.mult))
                    if j % 2 in t_before:
                        dve.wait_ge(att_mm, t_before[j % 2] + 1)
                    step(ts(att[j % 2][:, 0:n], prob[j % 2][:, 0, 0:n], small[:, 56:57], None, ALU.mult))
                    step.wait()
                    stt(att[j % 2][:, 0:n], prob[j % 2][:, 1, 0:n], small[:, 58:59], att[j % 2][:, 0:n], ALU.mult,
                        ALU.add).then_inc(att_a, 1)
                    dve.wait_ge(att_a, 5 * h + j + 1)
                    t_before[j % 2] = ATT_USE[("T", h, j)]
                elif kind == "ssO":
                    h = ev[1]
                    b = att_wait(ev)
                    ts(small[:, 32:37], bank(b, 5), 1.0 / P, EPS, ALU.mult, ALU.add).then_inc(att_free_dve, 1)
                    dve.wait_ge(o_root, h + 1)
                    step(nc.vector.reciprocal(small[:, 45:50], small[:, 40:45]))
                    step.wait()
                    if h:
                        dve.wait_ge(att_mm, ATT_USE[("rbO", h - 1)] + 1)
                    tt(o_diag[:, :, :], bc(ident, 1, CHUNKS), bc(small[:, 45:50], 2, P), ALU.mult
                       ).then_inc(o_dg, 1)
                elif kind == "rbO":
                    h = ev[1]
                    b = att_wait(ev)
                    if h:
                        dve.wait_ge(g_ready, G_AT[("rbO", h - 1)])
                    for s_, cols in RANGES:
                        rbp = bank(b, P) if s_ == 0 else bank(b + 1)
                        ins = stt(o_nrm[:, cols], o_sb[:, cols], small[:, 22:23], rbp, ALU.mult, ALU.mult)
                        (step(ins) if s_ == 0 else ins.then_inc(att_free_dve, 1))
                    dve.wait_ge(o_hi, h + 1)
                    tt(g_lo[:, h, :], o_nrm[:, :], f32(g_hi[:, h, :]), ALU.subtract).then_inc(g_ready, 1)
                elif kind == "pool":
                    g = ev[1]
                    b = att_wait(ev)
                    if g:
                        dve.wait_ge(g_ready, G_AT[("pool", g - 1)])
                    ts(pmul[:, :], bank(b, W, 512 - HALF), pcol("pool_scale", g), None, ALU.mult
                       ).then_inc(att_free_dve, 1)
                    dve.wait_ge(pool_hi, g + 1)
                    tt(g_lo[:, 4 + g, :], pmul[:, :], f32(g_hi[:, 4 + g, :]), ALU.subtract).then_inc(g_ready, 1)

            def col(t_, m):
                return t_[:, m, :] if isinstance(m, int) else t_[:, bass.ds(m, 1), :]

            def residual(l, j, m, slot):
                for s_, cols in RANGES:
                    if isinstance(m, int):
                        x_, gate = xT[:, m, cols], modc(l, j, m, s_)
                    else:
                        x_ = xT[:, bass.ds(m, 1), cols]
                        gate = mod[:, bass.ds(m + (l * 48 + j * 8), 1), s_:s_ + 1]
                    ins = stt(x_, acc(slot)[:, cols], gate, x_, ALU.mult, ALU.add)
                    (step(ins) if s_ == 0 else ins.then_inc(acc_free_dve, 1))

            for m in range(8):
                for s in ADA_B[m]:
                    ada_low(s)
                for s in ADA_B[m]:
                    ada_row_out(s)
                    if s > 8:
                        mod_evac(s - 1)
                if m == 0:
                    dve.wait_ge(x_back, 16)
                dve.wait_ge(mod_done, ADA_B[m][-1])
                dve.wait_ge(mm_done, T_B + m + 1)
                residual(0, 2, m, m % 2)
                if m >= 2:
                    add_square(1, m - 1, sq[(m - 1) % 2])
            mod_evac(19)
            add_square(1, 7, sq[1])
            gains(1, 20)
            norm(1)

            def ffn(l, t0, a0):
                wc = PARAM_AT["ffn_conv_w"] + l * 132
                n_ = 2 * l + 1
                for p, (m0, n) in enumerate(PARTS):
                    tp, ap = t0 + 2 * m0 + 8 * p, a0 + 2 * m0 + 8 * p
                    f0 = FT * l + m0
                    s0 = ADA_F + 16 * p

                    def pcol_at(r):
                        return par[:, r:r + 1] if isinstance(r, int) else par[:, bass.ds(r, 1)]

                    def pair(i, ada):
                        for half, buf in enumerate((cg, cv)):
                            if ada:
                                ada_low(2 * i + (s0 + half), half)
                            m = i + (m0 + FT * half)
                            dve.wait_ge(ffn_id, 2 * i + (2 * f0 + half + 1))
                            src = acc(half)
                            step(stt(buf[:, 1:W], src[:, 0:W - 1], pcol_at(m + wc), buf[:, 1:W], ALU.mult, ALU.add))
                            step.wait()
                            stt(buf[:, 0:W - 1], src[:, 1:W], pcol_at(m + (wc + 88)), buf[:, 0:W - 1], ALU.mult,
                                ALU.add).then_inc(acc_free_dve, 1)
                            if ada:
                                ada_row_out(2 * i + (s0 + half), half)
                                if not (isinstance(i, int) and s0 + half == ADA_F):
                                    mod_evac(2 * i + (s0 + half - 1))
                        dve.wait_ge(ffn_silu, i + (f0 + 1))
                        if not (isinstance(i, int) and f0 == 0):
                            dve.wait_ge(f_ready, i + f0)
                        dve.wait_ge(acc_free_dve, 2 * i + (dve_accs(ap) + 1))
                        tt(hm[:, :], sg[:, :], cv[:, :], ALU.mult).then_inc(hm_done, 1)
                        dve.wait_ge(ffn_hi, i + (f0 + 1))
                        tt(col(g_lo, i), hm[:, :], f32(col(g_hi, i)), ALU.subtract).then_inc(f_ready, 1)

                    n_ada = ADA_PAIRS[p] if l == 0 else 0
                    pair(0, n_ada > 0)
                    for lo_, hi_ in ((1, n_ada), (max(n_ada, 1), n)):
                        if lo_ < hi_:
                            with dve.Fori(lo_, hi_) as i:
                                step.turn(i - lo_, 2)
                                pair(i, lo_ < n_ada)
                            step.leave(hi_ - lo_)
                        if p == 1 and n_ada and lo_ == 1:
                            mod_evac(47)
                    td = tp + 2 * n

                    def down(i):
                        for half in range(2):
                            dve.wait_ge(mm_done, 2 * i + (td + half + 1))
                            residual(l, 5, 2 * i + half, half)
                            if p == 2 and not isinstance(i, int):
                                add_square(n_ + 1, 2 * i + (half - 1), sq[1 - half])

                    down(0)
                    with dve.Fori(1, 4) as i:
                        step.turn(i - 1, 2)
                        down(i)
                    step.leave(3)
                add_square(n_ + 1, 7, sq[1])

            ffn(0, T_F0, T_F0)
            gains(2, 48)
            gains(3, 48)
            step.wait()
            norm(2)

            dve.wait_ge(x_spilled, 32)
            c64 = lambda ap: ap.rearrange("p (c x) -> p c x", c=CHUNKS)

            def chain(ins):
                step(ins)
                step.wait()

            def series(powers):
                for k in powers:
                    chain(tt(dt_p, dt_p, dt_z, ALU.mult))
                    chain(ts(dt_p, dt_p, 1.0 / k, None, ALU.add))

            def time_steps(e):
                if e == 0:
                    dve.wait_ge(dt_exp, 1)
                    chain(ts(dt_s, dt_e, 2.0, None, ALU.add))
                    chain(nc.vector.reciprocal(dt_z, dt_s))
                    chain(tt(dt_s, dt_e, dt_z, ALU.mult))
                    chain(tt(dt_z, dt_s, dt_s, ALU.mult))
                    chain(ts(dt_p, dt_z, 1.0 / 17, 1.0 / 15, ALU.mult, ALU.add))
                elif e == 1:
                    series((13, 11, 9, 7))
                elif e == 2:
                    series((5, 3, 1))
                    chain(stt(dt_p, dt_p, 2.0, dt_s, ALU.mult, ALU.mult))
                    chain(stt(dt[:, :, :], c64(dt_x), 0.0, c64(dt_p), ALU.max, ALU.add))
                    tt(da3, dt[:, :, :], bc(a_bc[:, :], 1, CHUNKS), ALU.mult).then_inc(da_done, 1)

            def ssd_wait(key):
                dve.wait_ge(ssd_mm, SSD_USE[key] + 1)
                return 4 + SSD_USE[key] % 4

            def per_head(t_, c, d_, g):
                return bc(t_[:, c, 32 * d_ + GH * g:32 * d_ + GH * (g + 1)], 2, HD)

            h64 = lambda ap: ap.rearrange("p (r x) -> p r x", x=HD)

            def y_low(k):
                dve.wait_ge(yn_hi, k + 1)
                dve.wait_ge(y_sqd, k + 1)
                stt(y_lo[:, k, :], yg[:, k, :], pcol("ssd_norm_g", k), f32(y_hi[:, k, :]), ALU.mult, ALU.subtract
                    ).then_inc(y_ready, 1)
                if k:
                    if k > 1:
                        dve.wait_ge(y_added, k - 1)
                    tt(y_sums[:, :], y_sums[:, :], y_squares(k), ALU.add).then_inc(y_added, 1)

            def weigh(ev):
                kind, g, c = ev
                i = CS_AT[ev]
                if i >= 2:
                    dve.wait_ge(ssd_mm, SSD_USE[CS_LIST[i - 2]] + 1)
                tt(h64(xw[i % 2][:, :]), h64(x_tok[g % 2][:, c, :]), per_head(wst, c, 0 if kind == "csf" else 1, g),
                   ALU.mult).then_inc(xw_done, 1)

            n_id = 0
            for ev in SSD:
                kind = ev[0]
                if kind == "mm":
                    _, e, q = ev
                    what, m = ssd_tile(e)
                    if q == 0 or what == "z":
                        continue
                    g, i = divmod(e, 10)
                    buf = bT[g % 2] if i == 0 else cT[g % 2] if i == 1 else cx
                    n_id += 1
                    dve.wait_ge(conv_id, n_id)
                    src = acc(e % 2)
                    row = PARAM_AT["ssd_conv_w"] + m
                    chain(stt(buf[:, 1:W], src[:, 0:W - 1], par[:, row:row + 1], buf[:, 1:W], ALU.mult, ALU.add))
                    stt(buf[:, 0:W - 1], src[:, 1:W], par[:, row + 48:row + 49], buf[:, 0:W - 1], ALU.mult, ALU.add
                        ).then_inc(acc_free_dve, 1)
                    if e in (1, 2):
                        time_steps(e)
                    continue
                if kind == "dtT":
                    b = ssd_wait(ev)
                    tt(c64(dt_x), c64(bank(b, 320)), bc(dtb_bc[:, :], 1, CHUNKS), ALU.add).then_inc(ssd_free_dve, 1)
                    dve.wait_ge(*ssd_end(ev))
                    nc.vector.memset(small[:, 60:61], 0.0).then_inc(dt_xb, 1)
                    time_steps(0)
                    continue
                if kind == "sum":
                    b = ssd_wait(ev + (0,))
                    cp(acs[:, :, :], c64(bank(b, 320))).then_inc(ssd_free_dve, 1)
                    b = ssd_wait(ev + (1,))
                    cp(dec[:, :, :], c64(bank(b, 320))).then_inc(ssd_free_dve, 1)
                    dve.wait_ge(*ssd_end(ev + (1,)))
                    tt(wst[:, :, :], dec[:, :, :], acs[:, :, :], ALU.subtract).then_inc(tot_w, 1)
                    nc.vector.memset(small[:, 60:61], 0.0).then_inc(acs_done, 1)
                    continue
                if kind == "acsT":
                    dve.wait_ge(acs_exp, 1)
                    tt(wst[:, :, :], wst[:, :, :], dt[:, :, :], ALU.mult).then_inc(da_read, 1)
                    dve.wait_ge(da_read, 1)
                    continue
                if kind == "ynorm":
                    y_low(ev[2])
                if kind in ("ynorm", "yout"):
                    continue
                g = ev[1]
                c = ev[2] if len(ev) > 2 else 0
                xt = x_tok[g % 2][:, c, :]
                if kind == "init" and c == 0:
                    dve.wait_ge(*ssd_end(("trx", g, 3, 1)))
                    weigh(("csb", g, 4))
                elif kind in ("csb", "csf"):
                    if kind == "csb" and c == 4:
                        dve.wait_ge(*ssd_end(("init", g, 1)))
                    d_ = 0 if kind == "csf" else 1
                    if CS_LIST.index(ev) + 1 < len(CS_LIST):
                        after = CS_LIST[CS_LIST.index(ev) + 1]
                        if after[1] == g:
                            weigh(after)
                    b = ssd_wait(ev)
                    if c == 0:
                        if g:
                            dve.wait_ge(ssd_mm, SSD_USE[("stT", g - 1, 1)] + 1)
                        cp(st_p[:, d_, :], bank(b)).then_inc(ssd_free_dve, 1)
                        dve.wait_ge(*ssd_end(ev))
                        nc.vector.memset(small[:, 60:61], 0.0).then_inc(st_done, 1)
                    else:
                        old = st_f[c % 2][:, :] if d_ == 0 else st_b[:, c - 1, :]
                        new = st_f[(c + 1) % 2][:, :] if d_ == 0 else st_b[:, c - 2, :]
                        chain(tt(h64(st_tmp[:, :]), h64(old), per_head(dec, c, d_, g), ALU.mult))
                        tt(new, st_tmp[:, :], bank(b), ALU.add).then_inc(ssd_free_dve, 1)
                        dve.wait_ge(*ssd_end(ev))
                        nc.vector.memset(small[:, 60:61], 0.0).then_inc(st_done, 1)
                elif kind == "cb":
                    n = 5 * g + c
                    b = ssd_wait(ev)
                    if n:
                        dve.wait_ge(W_done, 2 * n)
                    tt(cbm[:, :, :], bc(bank(b, P), 1, 2), masks, ALU.mult).then_inc(ssd_free_dve, 1)
                    if n:
                        dve.wait_ge(ssd_mm, SSD_USE[("yd", g, c - 1) if c else ("yd", g - 1, 4)] + 1)
                    else:
                        dve.wait_ge(acs_stored, 16)
                    for d_ in range(2):
                        step(tt(h64(xdt[:, d_, :]), h64(xt), per_head(dt, c, d_, g), ALU.mult))
                    dve.wait_ge(*ssd_end(ev))
                    step.wait()
                    for d_ in range(2):
                        dve.wait_ge(seg_exp, 2 * n + d_ + 1)
                        tt(R[:, d_, :, :], R[:, d_, :, :], bc(cbm[:, d_, :], 1, GH), ALU.mult).then_inc(W_done, 1)
                elif kind == "yd":
                    n = 5 * g + c
                    y_ = y1[c % 2][:, :]
                    if c >= 2:
                        dve.wait_ge(ssd_mm, SSD_USE[("yT", g, c - 2)] + 1)
                    elif g:
                        dve.wait_ge(ssd_mm, SSD_USE[("yT", g - 1, 4)] + 1)
                    chain(tt(h64(y_), h64(xt), bc(d_bc[:, GH * g:GH * (g + 1)], 2, HD), ALU.mult))
                    b = ssd_wait(ev)
                    tt(y_, y_, bank(b), ALU.add).then_inc(ssd_free_dve, 1)
                    dve.wait_ge(*ssd_end(ev))
                    if c == 0:
                        nc.vector.memset(small[:, 60:61], 0.0).then_inc(y_done, 1)
                elif kind == "yo":
                    y_ = y1[c % 2][:, :]
                    for d_ in range(2):
                        b = ssd_wait(ev + (d_,))
                        tt(h64(y2[:, :]), h64(bank(b)), per_head(eacs, c, d_, g), ALU.mult).then_inc(ssd_free_dve, 1)
                        dve.wait_ge(*ssd_end(ev + (d_,)))
                        ins = tt(y_, y_, y2[:, :], ALU.add)
                        if d_ == 0:
                            chain(ins)
                        else:
                            ins.then_inc(y_done, 1)
                            dve.wait_ge(y_done, 5 * g + c + 1)
                elif kind == "yT":
                    b = ssd_wait(ev)
                    if c == 0:
                        dve.wait_ge(acc_free_act, acc_ends[A_E + 10 * g + 9][1])
                    dst = yg[:, 4 * g:4 * g + 4, chunk_col(c):chunk_col(c) + P]
                    tt(dst, bank(b).rearrange("p (q n) -> p q n", q=4), dst, ALU.mult).then_inc(ssd_free_dve, 1)

            for k in range(12, 16):
                y_low(k)
            dve.wait_ge(y_ss, 1)
            ts(small[:, 0:5], bank(6, 5), 1.0 / DI, EPS, ALU.mult, ALU.add).then_inc(yr_ms, 1)
            dve.wait_ge(yr_root, 1)
            chain(nc.vector.reciprocal(small[:, 48:53], small[:, 8:13]))
            tt(diag[:, :, :], bc(ident, 1, CHUNKS), bc(small[:, 48:53], 2, P), ALU.mult).then_inc(yr_dg, 1)
            dve.wait_ge(yr_rb, 1)
            step(cp(rbs[:, 0:NP_], bank(4, P)))
            step(cp(rbs[:, S0:S0 + NS], bank(5)))
            step.wait()
            dve.wait_ge(x_back, 32)

            def so_residual(i):
                for half in range(2):
                    m = 2 * i + half
                    dve.wait_ge(mm_done, 4 * i + (T_O + 2 + half + 1))
                    buf = tn[half]
                    for s_, cols in RANGES:
                        gate = modc(1, 2, m, s_) if isinstance(m, int) else \
                            mod[:, bass.ds(m + (48 + 16), 1), s_:s_ + 1]
                        ins = stt(buf[:, cols], acc(half)[:, cols], gate, rbs[:, cols], ALU.mult, ALU.mult)
                        (step(ins) if s_ == 0 else ins.then_inc(acc_free_dve, 1))
                    dve.wait_ge(acc_free_dve, 2 * i + (dve_accs(A_O) + half))
                    for s_, cols in RANGES:
                        x_ = xT[:, m, cols] if isinstance(m, int) else xT[:, bass.ds(m, 1), cols]
                        ins = tt(x_, x_, buf[:, cols], ALU.add)
                        (step(ins) if s_ == 0 else ins.then_inc(so_x, 1))
                    if not isinstance(i, int):
                        add_square(3, 2 * i + (half - 1), sq[1 - half])

            so_residual(0)
            with dve.Fori(1, 4) as i:
                step.turn(i - 1, 4)
                dve.wait_ge(so_x, 2 * i)
                so_residual(i)
            step.leave(3)
            add_square(3, 7, sq[1])
            norm(3)
            ffn(1, T_F1, A_F1)

            inv_root(4)
            dve.wait_ge(fg_in, 16)
            for c in range(CHUNKS):
                dve.wait_ge(fin_ps, c + 1)
                if c >= 2:
                    dve.wait_ge(y_stored[c % 2], 16 * (c // 2))
                src = bank(4, D) if c % 2 == 0 else bank(2, D)
                stt(y_out[c % 2][:, :], src, small[:, 48 + c:49 + c], fg_bc[:, :], ALU.mult, ALU.mult
                    ).then_inc(fin_y, 1)


_INS = ["x_prompt", "x_sample", "cache_k", "cache_v", "state_ssm_fwd", "state_ssm_bwd", "c", "c_ctx", "ada_w",
        "ada_b", "norm_mix_g", "norm_ffn_g", "att_w_in", "att_lambda", "att_subln_g", "pool_w", "pool_scale",
        "att_w_out", "ssd_w_in", "ssd_conv_w", "ssd_conv_b", "ssd_dt_bias", "ssd_a_log", "ssd_d", "ssd_norm_g",
        "ssd_w_out", "ffn_w_up", "ffn_conv_w", "ffn_conv_b", "ffn_w_down", "final_norm_g"]
_OUTS = [("y_prompt", (1, NP_, D)), ("y_sample", (1, NS, D)), ("new_cache_k", (1, 1, NP_, HEADS, 2, HD)),
         ("new_cache_v", (1, 1, NP_, HEADS, 2 * HD)), ("new_state_fwd", (1, 1, 32, 64, 128)),
         ("new_state_bwd", (1, 1, 32, 64, 128))]


def tables():
    eye = np.eye(P, dtype=np.float32)
    rot = np.zeros((P, P), np.float32)
    for ch in range(P):
        base, f = ch - ch % 32, ch % 16
        if ch % 32 < 16:
            rot[base + 16 + f, ch] = -1.0
        else:
            rot[base + f, ch] = 1.0
    i = np.arange(P)
    le = (i[:, None] <= i[None, :]).astype(np.float32)
    inv = np.float32(10000.0) ** (-np.arange(16, dtype=np.float32) / np.float32(16))
    tok = np.arange(NS)
    pos = np.stack([tok // 64, tok % 64]).astype(np.float32)
    ch = np.arange(P)
    ang = (pos[(ch % 64) // 32, :] * inv[ch % 16][:, None]).astype(np.float32)
    inv_n = np.zeros((4, NP_ + NS), np.float32)
    for g, w in enumerate(POOL_WINDOWS):
        for at, n in ((0, NP_), (NP_, NS)):
            t = np.arange(n)
            inv_n[g, at:at + n] = 1.0 / (np.clip(t + w // 2, 0, n) - np.clip(t - w // 2, 0, n))
    return np.concatenate([eye, le, le.T, rot, np.cos(ang), np.sin(ang)], axis=1).astype(np.float32), inv_n


PICK = np.array([[1, 0], [0, 1], [1, 0], [0, 1]], np.float32)


def kernel(**inputs):
    import concourse.bacc as bacc
    from concourse.bass_utils import run_bass_kernel_spmd

    nc = bacc.Bacc("TRN2", target_bir_lowering=False, num_devices=1)
    arrays, A, O = {}, {}, {}
    table, inv_n = tables()
    for name, a in [(n, inputs[n]) for n in _INS] + [("tables", table), ("inv_n", inv_n), ("pick", PICK)]:
        a = np.ascontiguousarray(a)
        arrays[f"in_{name}"] = a
        A[name] = nc.dram_tensor(f"in_{name}", a.shape, mybir.dt.from_np(a.dtype), kind="ExternalInput").ap()
    for name, shape in _OUTS:
        O[name] = nc.dram_tensor(f"out_{name}", shape, F32, kind="ExternalOutput").ap()
    build(nc, A, O)
    r = run_bass_kernel_spmd(nc, [arrays], core_ids=[0])
    return tuple(r.results[0][f"out_{name}"] for name, _ in _OUTS)
```
